# Optimizing a Trainium2 kernel written in Bass

```python
import math
import jax
import jax.numpy as jnp
from jax import lax
import numpy as np

D_MODEL = 1024
BATCH = 1
SEQ = 512
DEPTH = 2

MEM_LEN = 256
GROUP_WIDTH = D_MODEL // 2
N_GROUPS = 4
MIX_WIDTH = N_GROUPS * GROUP_WIDTH

SWA_HEADS = 8
SWA_KV_HEADS = 2
SWA_HEAD_DIM = GROUP_WIDTH // SWA_HEADS
WINDOW = 128
REL_BUCKETS = 32
REL_MAX_DIST = 128
GDN_HEADS = 4
GDN_HEAD_DIM = GROUP_WIDTH // GDN_HEADS
GDN_CONV = 4
GDN_CHUNK = 64
MLA_HEADS = 4
MLA_NOPE_DIM = 128
MLA_ROPE_DIM = 64
MLA_V_DIM = GROUP_WIDTH // MLA_HEADS
MLA_Q_RANK = D_MODEL // 4
MLA_KV_RANK = D_MODEL // 8
ROPE_THETA = 10000.0
Q_BLOCK = 128
MEM_HEADS = 4
MEM_HEAD_DIM = GROUP_WIDTH // MEM_HEADS

RMS_EPS = 1e-6
NEG_INF = -1e30

IN_SPLITS = (
    SWA_HEADS * SWA_HEAD_DIM,
    SWA_KV_HEADS * SWA_HEAD_DIM,
    SWA_KV_HEADS * SWA_HEAD_DIM,
    GROUP_WIDTH,
    3 * GROUP_WIDTH,
    GDN_HEADS,
    GDN_HEADS,
    GROUP_WIDTH,
    MLA_Q_RANK,
    MLA_KV_RANK,
    MLA_ROPE_DIM,
    GROUP_WIDTH,
    MEM_HEADS * MEM_HEAD_DIM,
    GROUP_WIDTH,
)
D_IN = sum(IN_SPLITS)

kernel_name = 'hybrid_parallel_heads_block'

def rmsnorm(t, gain):
    tf = t.astype(jnp.float32)
    tf = tf * lax.rsqrt(jnp.mean(tf * tf, axis=-1, keepdims=True) + RMS_EPS)
    return (tf * gain.astype(jnp.float32)).astype(t.dtype)

def l2norm(t):
    return t * lax.rsqrt(jnp.sum(t * t, axis=-1, keepdims=True) + 1e-6)

def split_columns(t, sizes):
    offs = np.cumsum(sizes)[:-1].tolist()
    return jnp.split(t, offs, axis=-1)

def t5_bucket(rel):
    n = jnp.maximum(rel, 0)
    max_exact = REL_BUCKETS // 2
    nf = jnp.maximum(n, 1).astype(jnp.float32)
    large = max_exact + (jnp.log(nf / max_exact) / math.log(REL_MAX_DIST / max_exact)
                         * (REL_BUCKETS - max_exact)).astype(jnp.int32)
    large = jnp.minimum(large, REL_BUCKETS - 1)
    return jnp.where(n < max_exact, n, large)

def banded_rel_bias(rel_bias, positions):
    B, S = positions.shape
    nb = S // WINDOW
    pq = positions.reshape(B, nb, WINDOW)
    pprev = jnp.pad(pq, ((0, 0), (1, 0), (0, 0)))[:, :-1]
    pk = jnp.concatenate([pprev, pq], axis=2)
    bucket = t5_bucket(pq[..., :, None] - pk[..., None, :])
    bias = jnp.take(rel_bias.T.astype(jnp.float32), bucket, axis=1)
    bias = bias.reshape(SWA_KV_HEADS, SWA_HEADS // SWA_KV_HEADS, B, nb, WINDOW, 2 * WINDOW)
    return jnp.moveaxis(bias, 2, 0)

def rope_tables(positions):
    inv_freq = 1.0 / (ROPE_THETA ** (jnp.arange(0, MLA_ROPE_DIM, 2, dtype=jnp.float32) / MLA_ROPE_DIM))
    ang = positions.astype(jnp.float32)[..., None] * inv_freq
    return jnp.cos(ang), jnp.sin(ang)

def apply_rope(t, cos, sin):
    half = t.shape[-1] // 2
    t1, t2 = t[..., :half], t[..., half:]
    return jnp.concatenate([t1 * cos - t2 * sin, t1 * sin + t2 * cos], axis=-1)

def swa_sink_attention(q, k, v, sinks, bias):
    B, S, HQ, Dh = q.shape
    HKV = k.shape[2]
    G = HQ // HKV
    W = WINDOW
    nb = S // W
    qb = q.astype(jnp.float32).reshape(B, nb, W, HKV, G, Dh)

    def with_prev(t):
        tb = t.astype(jnp.float32).reshape(B, nb, W, HKV, Dh)
        prev = jnp.pad(tb, ((0, 0), (1, 0), (0, 0), (0, 0), (0, 0)))[:, :-1]
        return jnp.concatenate([prev, tb], axis=2)

    kb, vb = with_prev(k), with_prev(v)
    s = jnp.einsum('bnqhgd,bnkhd->bhgnqk', qb, kb) * (Dh ** -0.5) + bias
    qi = jnp.arange(W)[:, None]
    kj = jnp.arange(2 * W)[None, :]
    band = (kj > qi) & (kj <= qi + W)
    valid = band[None] & ((jnp.arange(nb) > 0)[:, None, None] | (kj >= W)[None])
    s = jnp.where(valid, s, NEG_INF)
    sink = sinks.astype(jnp.float32).reshape(HKV, G)[None, :, :, None, None]
    m = jnp.maximum(jnp.max(s, axis=-1), sink)
    p = jnp.exp(s - m[..., None])
    denom = jnp.sum(p, axis=-1) + jnp.exp(sink - m)
    p = p / denom[..., None]
    o = jnp.einsum('bhgnqk,bnkhd->bnqhgd', p, vb)
    return o.reshape(B, S, HQ * Dh)

def causal_depthwise_conv(t, w):
    K, C = w.shape
    return lax.conv_general_dilated(
        t.astype(jnp.float32), w.astype(jnp.float32)[:, None, :],
        window_strides=(1,), padding=[(K - 1, 0)],
        dimension_numbers=('NWC', 'WIO', 'NWC'), feature_group_count=C)

def gated_delta_rule_chunked(q, k, v, g, beta):
    B, S, H, Dk = q.shape
    Dv = v.shape[-1]
    C = GDN_CHUNK
    N = S // C

    def chunks(t):
        t = t.reshape(B, N, C, H, *t.shape[3:])
        return jnp.moveaxis(t, 3, 1)

    q = chunks(q * (Dk ** -0.5))
    k = chunks(k)
    v = chunks(v)
    beta = chunks(beta)
    g = jnp.cumsum(chunks(g), axis=-1)
    k_beta = k * beta[..., None]
    v_beta = v * beta[..., None]
    incl = jnp.tril(jnp.ones((C, C), bool))
    strict = jnp.tril(jnp.ones((C, C), bool), -1)
    gdiff = g[..., :, None] - g[..., None, :]
    decay = jnp.where(incl, jnp.exp(jnp.where(incl, gdiff, 0.0)), 0.0)
    L = jnp.where(strict, jnp.einsum('bhncd,bhnmd->bhncm', k_beta, k) * decay, 0.0)
    eye = jnp.eye(C, dtype=jnp.float32)
    T = lax.linalg.triangular_solve(eye + L, jnp.broadcast_to(eye, L.shape),
                                    left_side=True, lower=True)
    u = T @ v_beta
    w = T @ (k_beta * jnp.exp(g)[..., None])
    a_qk = jnp.einsum('bhncd,bhnmd->bhncm', q, k) * decay
    qg = q * jnp.exp(g)[..., None]
    g_last = g[..., -1]
    kd = k * jnp.exp(g_last[..., None] - g)[..., None]

    def step(state, inp):
        qg_i, a_i, u_i, w_i, kd_i, gl_i = inp
        v_new = u_i - jnp.einsum('bhcd,bhde->bhce', w_i, state)
        o_i = jnp.einsum('bhcd,bhde->bhce', qg_i, state) + jnp.einsum('bhcm,bhme->bhce', a_i, v_new)
        state = state * jnp.exp(gl_i)[..., None, None] + jnp.einsum('bhcd,bhce->bhde', kd_i, v_new)
        return state, o_i

    xs = tuple(jnp.moveaxis(t, 2, 0) for t in (qg, a_qk, u, w, kd, g_last))
    state0 = jnp.zeros((B, H, Dk, Dv), jnp.float32)
    _, o = lax.scan(step, state0, xs)
    return jnp.transpose(o, (1, 0, 3, 2, 4)).reshape(B, S, H, Dv)

def mla_causal_attention(q_nope, q_rope, k_nope, k_rope, v):
    B, S, H, _ = q_nope.shape
    nb = S // Q_BLOCK
    scale = (MLA_NOPE_DIM + MLA_ROPE_DIM) ** -0.5
    k_idx = jnp.arange(S)

    def to_blocks(t):
        return jnp.moveaxis(t.reshape(B, nb, Q_BLOCK, *t.shape[2:]), 1, 0)

    def block(args):
        qn, qr, start = args
        s = (jnp.einsum('bqhd,bkhd->bhqk', qn, k_nope)
             + jnp.einsum('bqhd,bkd->bhqk', qr, k_rope)) * scale
        q_idx = start + jnp.arange(Q_BLOCK)
        s = jnp.where(k_idx[None, :] <= q_idx[:, None], s, NEG_INF)
        p = jax.nn.softmax(s, axis=-1)
        return jnp.einsum('bhqk,bkhd->bqhd', p, v)

    o = lax.map(block, (to_blocks(q_nope), to_blocks(q_rope), jnp.arange(nb) * Q_BLOCK))
    return jnp.moveaxis(o, 0, 1).reshape(B, S, H * v.shape[-1])

def memory_cross_attention(q, mk, mv):
    B, S, H, D = q.shape
    s = jnp.einsum('bshd,bmhd->bhsm', q, mk) * (D ** -0.5)
    p = jax.nn.softmax(s, axis=-1)
    return jnp.einsum('bhsm,bmhd->bshd', p, mv).reshape(B, S, H * D)

def hybrid_layer(x, mem, cos, sin, bias_blocks, norm_pre, norm_post, w_in, attn_sinks,
                 gdn_conv_w, gdn_a_log, gdn_dt_bias, gdn_norm, mla_q_norm, mla_kv_norm,
                 mla_w_uq, mla_w_ukv, mem_norm, mem_w_kv, w_out):
    B, S, _ = x.shape
    f32 = jnp.float32
    h = rmsnorm(x, norm_pre)
    (a_q, a_k, a_v, a_z, b_qkv, b_a, b_b, b_z,
     c_cq, c_ckv, c_kr, c_z, d_q, d_z) = split_columns(h @ w_in, IN_SPLITS)

    o_a = swa_sink_attention(a_q.reshape(B, S, SWA_HEADS, SWA_HEAD_DIM),
                             a_k.reshape(B, S, SWA_KV_HEADS, SWA_HEAD_DIM),
                             a_v.reshape(B, S, SWA_KV_HEADS, SWA_HEAD_DIM),
                             attn_sinks, bias_blocks)
    o_a = o_a * jax.nn.silu(a_z.astype(f32))

    qkv = jax.nn.silu(causal_depthwise_conv(b_qkv, gdn_conv_w))
    g_q, g_k, g_v = jnp.split(qkv, 3, axis=-1)
    g_q = l2norm(g_q.reshape(B, S, GDN_HEADS, GDN_HEAD_DIM))
    g_k = l2norm(g_k.reshape(B, S, GDN_HEADS, GDN_HEAD_DIM))
    g_v = g_v.reshape(B, S, GDN_HEADS, GDN_HEAD_DIM)
    beta = jax.nn.sigmoid(b_b.astype(f32))
    log_decay = -jnp.exp(gdn_a_log.astype(f32)) * jax.nn.softplus(b_a.astype(f32) + gdn_dt_bias.astype(f32))
    o_b = gated_delta_rule_chunked(g_q, g_k, g_v, log_decay, beta)
    o_b = rmsnorm(o_b, gdn_norm) * jax.nn.silu(b_z.astype(f32).reshape(B, S, GDN_HEADS, GDN_HEAD_DIM))
    o_b = o_b.reshape(B, S, GROUP_WIDTH)

    cq = rmsnorm(c_cq, mla_q_norm)
    qh = (cq @ mla_w_uq).astype(f32).reshape(B, S, MLA_HEADS, MLA_NOPE_DIM + MLA_ROPE_DIM)
    q_nope, q_rope = qh[..., :MLA_NOPE_DIM], qh[..., MLA_NOPE_DIM:]
    q_rope = apply_rope(q_rope, cos[:, :, None, :], sin[:, :, None, :])
    ckv = rmsnorm(c_ckv, mla_kv_norm)
    kv = (ckv @ mla_w_ukv).astype(f32).reshape(B, S, MLA_HEADS, MLA_NOPE_DIM + MLA_V_DIM)
    k_nope, m_v = kv[..., :MLA_NOPE_DIM], kv[..., MLA_NOPE_DIM:]
    k_rope = apply_rope(c_kr.astype(f32), cos, sin)
    o_c = mla_causal_attention(q_nope, q_rope, k_nope, k_rope, m_v)
    o_c = o_c * jax.nn.silu(c_z.astype(f32))

    mkv = (rmsnorm(mem, mem_norm) @ mem_w_kv).astype(f32)
    mk, mv = jnp.split(mkv, 2, axis=-1)
    M = mem.shape[1]
    o_d = memory_cross_attention(d_q.astype(f32).reshape(B, S, MEM_HEADS, MEM_HEAD_DIM),
                                 mk.reshape(B, M, MEM_HEADS, MEM_HEAD_DIM),
                                 mv.reshape(B, M, MEM_HEADS, MEM_HEAD_DIM))
    o_d = o_d * jax.nn.silu(d_z.astype(f32))

    mixed = jnp.concatenate([o_a, o_b, o_c, o_d], axis=-1).astype(x.dtype)
    y = mixed @ w_out
    return x + rmsnorm(y, norm_post)

def setup_inputs(seed: int = 0) -> dict:
    key = jax.random.key(seed)
    ks = jax.random.split(key, 20)

    def nrm(k, shape, scale):
        return jax.random.normal(k, shape, jnp.float32) * scale

    def gain(k, shape):
        return 1.0 + 0.02 * jax.random.normal(k, shape, jnp.float32)

    x = nrm(ks[0], (BATCH, SEQ, D_MODEL), 1.0)
    mem = nrm(ks[1], (BATCH, MEM_LEN, D_MODEL), 1.0)
    offset = jax.random.randint(ks[2], (BATCH, 1), 0, 1024, dtype=jnp.int32)
    positions = offset + jnp.arange(SEQ, dtype=jnp.int32)[None, :]
    rel_bias = nrm(ks[3], (REL_BUCKETS, SWA_HEADS), 0.5)
    norm_pre = gain(ks[4], (DEPTH, D_MODEL))
    norm_post = gain(ks[5], (DEPTH, D_MODEL))
    w_in = nrm(ks[6], (DEPTH, D_MODEL, D_IN), D_MODEL ** -0.5)
    attn_sinks = nrm(ks[7], (DEPTH, SWA_HEADS), 0.5)
    gdn_conv_w = nrm(ks[8], (DEPTH, GDN_CONV, 3 * GROUP_WIDTH), GDN_CONV ** -0.5)
    gdn_a_log = jnp.log(jax.random.uniform(ks[9], (DEPTH, GDN_HEADS), jnp.float32, 1.0, 16.0))
    dt = jnp.exp(jax.random.uniform(ks[10], (DEPTH, GDN_HEADS), jnp.float32,
                                    math.log(1e-3), math.log(1e-1)))
    gdn_dt_bias = jnp.log(jnp.expm1(dt))
    gdn_norm = gain(ks[11], (DEPTH, GDN_HEAD_DIM))
    mla_q_norm = gain(ks[12], (DEPTH, MLA_Q_RANK))
    mla_kv_norm = gain(ks[13], (DEPTH, MLA_KV_RANK))
    mla_w_uq = nrm(ks[14], (DEPTH, MLA_Q_RANK, MLA_HEADS * (MLA_NOPE_DIM + MLA_ROPE_DIM)), MLA_Q_RANK ** -0.5)
    mla_w_ukv = nrm(ks[15], (DEPTH, MLA_KV_RANK, MLA_HEADS * (MLA_NOPE_DIM + MLA_V_DIM)), MLA_KV_RANK ** -0.5)
    mem_norm = gain(ks[16], (DEPTH, D_MODEL))
    mem_w_kv = nrm(ks[17], (DEPTH, D_MODEL, 2 * GROUP_WIDTH), D_MODEL ** -0.5)
    w_out = nrm(ks[18], (DEPTH, MIX_WIDTH, D_MODEL), MIX_WIDTH ** -0.5)
    return {'x': x, 'mem': mem, 'positions': positions, 'rel_bias': rel_bias,
            'norm_pre': norm_pre, 'norm_post': norm_post, 'w_in': w_in,
            'attn_sinks': attn_sinks, 'gdn_conv_w': gdn_conv_w, 'gdn_a_log': gdn_a_log,
            'gdn_dt_bias': gdn_dt_bias, 'gdn_norm': gdn_norm, 'mla_q_norm': mla_q_norm,
            'mla_kv_norm': mla_kv_norm, 'mla_w_uq': mla_w_uq, 'mla_w_ukv': mla_w_ukv,
            'mem_norm': mem_norm, 'mem_w_kv': mem_w_kv, 'w_out': w_out}

def reference(x, mem, positions, rel_bias, norm_pre, norm_post, w_in, attn_sinks,
              gdn_conv_w, gdn_a_log, gdn_dt_bias, gdn_norm, mla_q_norm, mla_kv_norm,
              mla_w_uq, mla_w_ukv, mem_norm, mem_w_kv, w_out):
    bias_blocks = banded_rel_bias(rel_bias, positions)
    cos, sin = rope_tables(positions)
    for l in range(DEPTH):
        x = hybrid_layer(x, mem, cos, sin, bias_blocks, norm_pre[l], norm_post[l], w_in[l],
                         attn_sinks[l], gdn_conv_w[l], gdn_a_log[l], gdn_dt_bias[l], gdn_norm[l],
                         mla_q_norm[l], mla_kv_norm[l], mla_w_uq[l], mla_w_ukv[l],
                         mem_norm[l], mem_w_kv[l], w_out[l])
    return x


_drawn_inputs = setup_inputs


def setup_inputs(seed=0):
    import zlib

    import numpy as np

    out = dict(_drawn_inputs(seed))
    spreads = {}
    factors = {'attn_sinks': 175.057,
     'mla_q_norm': 8.0,
     'mla_kv_norm': 8.0,
     'mem_norm': 8.0,
     'gdn_norm': 7.259,
     'rel_bias': 3.597}
    for name, (base, spread) in spreads.items():
        noise = np.random.default_rng([zlib.crc32(name.encode()), seed]).standard_normal(out[name].shape)
        drawn = base * np.exp(spread * noise) if base else spread * noise
        out[name] = jnp.asarray(drawn.astype(out[name].dtype))
    for name, factor in factors.items():
        out[name] = (out[name] * factor).astype(out[name].dtype)
    return out
```

```python
from contextlib import ExitStack
import math

import numpy as np
import concourse.bass as bass
from concourse import mybir

F32 = mybir.dt.float32
BF16 = mybir.dt.bfloat16
I32 = mybir.dt.int32
ALU = mybir.AluOpType
ACT = mybir.ActivationFunctionType
AX = mybir.AxisListType

P = 128
S, D, DEPTH, MEM = 512, 1024, 2, 256
T = S // P
KD = D // P
GW = D // 2
NH = 4
SWA_H, SWA_D = 8, 64
NOPE, ROPE = 128, 64
BUCKETS, MAX_DIST = 32, 128
CH = 64
LEVELS = 6
EPS = 1e-6
NEG = -1e30
BANKS = 8
FB = 512
CONV = 4

OFF = {}
_at = 0
for _n, _w in (("a_q", 512), ("a_k", 128), ("a_v", 128), ("a_z", 512), ("b_q", 512), ("b_k", 512),
               ("b_v", 512), ("b_ab", 8), ("b_z", 512), ("c_q", 256), ("c_kv", 128), ("c_kr", 64),
               ("c_z", 512), ("d_q", 512), ("d_z", 512)):
    OFF[_n] = _at
    _at += _w
D_IN = _at

CONST_AT = {}


def constants():
    i = np.arange(P)
    same = (i[:, None] // CH) == (i[None, :] // CH)
    cols = []

    def put(name, a):
        CONST_AT[name] = (sum(c.shape[1] for c in cols), a.shape[1])
        cols.append(np.asarray(a, np.float32))

    put("ident", np.eye(P))
    put("ones", np.ones((P, P)))
    upto = same & (i[:, None] <= i[None, :])
    put("upto", upto)
    put("chunk", same)
    put("decay_neg", np.where(upto, 0.0, NEG))
    for lv in range(LEVELS):
        m = 1 << lv
        pair = (i[:, None] // (2 * m)) == (i[None, :] // (2 * m))
        put(f"level{lv}", pair & (i[:, None] % (2 * m) < m) & (i[None, :] % (2 * m) >= m))
    put("causal_neg", np.where(i[None, :] <= i[:, None], 0.0, NEG))
    inv_freq = np.float32(1.0) / np.power(np.float32(10000.0), np.arange(0, ROPE, 2, dtype=np.float32) / ROPE)
    put("inv_freq", inv_freq[i % 32][:, None])
    put("rope_sign", np.where(i % 64 < 32, -1.0, 1.0)[:, None])
    half = BUCKETS // 2
    least = [-1e30] + list(range(1, half)) + [
        math.ceil(half * (MAX_DIST / half) ** (j / half) - 1e-9) for j in range(half)]
    put("bucket_least", np.array(least, np.float64)[i % BUCKETS][:, None])
    put("eps", np.full((P, 1), EPS))
    return np.ascontiguousarray(np.concatenate(cols, 1))


CONSTS = constants()

WN = 256
SLOTS = 4
CHUNKS = (["memk0", "memk1", "memv0", "memv1", "d_q0", "d_q1", "d_z0", "d_z1", "b_q0", "b_q1", "b_k0", "b_k1",
           "b_v0", "b_v1", "av_ab", "b_z0", "b_z1", "c_q", "ckv_kr", "krs_ak", "c_z0", "c_z1",
           "a_q0", "a_q1", "a_z0", "a_z1"]
          + [f"out{n}{kh}" for n in range(4) for kh in range(2)])

TILES = {}
for _n in ("b_q", "b_k", "b_v", "b_z", "c_z", "d_q", "d_z", "a_q", "a_z"):
    for _j in range(4):
        TILES[f"{_n}.{_j}"] = (f"{_n}{_j // 2}", (_j % 2) * P)
for _j in range(4):
    TILES[f"mk.{_j}"] = (f"memk{_j // 2}", (_j % 2) * P)
TILES["c_q.0"], TILES["c_q.1"] = ("c_q", 0), ("c_q", P)
TILES["ckv"], TILES["kr"] = ("ckv_kr", 0), ("ckv_kr", P)
TILES["krs"], TILES["ak"] = ("krs_ak", 0), ("krs_ak", P)
GATES = [f"{g}.{j}" for g in ("d_z", "b_z", "c_z", "a_z") for j in range(4)]
MIX_AT = {f"{g}.{j}": 4 * n + j for n, g in enumerate(("a_z", "b_z", "c_z", "d_z")) for j in range(4)}

UNITS = ([("D", h, tp, 2, MEM) for h in range(NH) for tp in range(2)]
         + [("C", h, t, 1, P * (t + 1)) for h in range(NH) for t in range(T)]
         + [("A", blk, sj, 2, 2 * P if blk else P) for blk in range(T) for sj in range(4)])
GROUPS = [("D", h) for h in range(NH)] + [("C", h) for h in range(NH)] + [("A", blk) for blk in range(T)]
GROUP_OF = [GROUPS.index(u[:2]) for u in UNITS]
SCALE = {"D": float(P) ** -0.5, "C": float(NOPE + ROPE) ** -0.5, "A": 1.0}


def attention(units):
    steps = []
    n = len(units)
    for i in range(n + 3):
        if i < n:
            steps.append(("scores", units[i]))
        if 1 <= i <= n:
            steps.append(("norm", units[i - 1]))
        if 2 <= i <= n + 1:
            steps.append(("turn", units[i - 2]))
        if i >= 3:
            u = units[i - 3]
            if u == len(UNITS) - 1 or GROUP_OF[u + 1] != GROUP_OF[u]:
                steps.append(("pv", GROUP_OF[u]))
    return steps


STEPS = [("params", 0)] + [("xt", t) for t in range(T)]
STEPS += [("proj", f"mk.{h}") for h in range(NH)] + [("mv", c) for c in range(2)]
STEPS += [("proj", f"d_q.{h}") for h in range(NH)] + [("gate", f"d_z.{j}") for j in range(4)]
STEPS += attention(range(0, 8))
STEPS += [("conv", j) for j in range(12)] + [("av_ab", 0)] + [("gate", f"b_z.{j}") for j in range(4)]
STEPS += [("log_decay", 0)]
STEPS += [("l2", j) for j in range(8)]
STEPS += [("decay", t) for t in range(T)]
STEPS += [("chunk_rows", t) for t in range(T)]
STEPS += [("chunk_products", t) for t in range(T)]
for _lv in range(LEVELS):
    STEPS += [("solve_a", (_lv, t)) for t in range(T)] + [("solve_b", (_lv, t)) for t in range(T)]
STEPS += [("w", t) for t in range(T)] + [("qg", t) for t in range(T)]
STEPS += [("state", n) for n in range(S // CH)]
STEPS += [("delta_out", h) for h in range(NH)]
STEPS += [("proj", x) for x in ("c_q.0", "c_q.1", "ckv")] + [("c_norm", 0), ("c_norm", 1)]
STEPS += [("rope", "k"), ("proj", "ak")]
STEPS += [("qn", h) for h in range(NH)] + [("kn", h) for h in range(NH)] + [("cv", t) for t in range(T)]
STEPS += [("rope", 0), ("rope", 1)] + [("gate", f"c_z.{j}") for j in range(4)]
STEPS += [("proj", f"a_q.{j}") for j in range(4)] + [("gate", f"a_z.{j}") for j in range(4)]
STEPS += attention(range(8, 24)) + attention(range(24, 40))
STEPS += [("out", n) for n in range(4)] + [("residual", 0)]


def tasks_of(step):
    kind, i = step
    return {
        "params": lambda: [("params", "A")],
        "xt": lambda: [(f"xt{i}.{kk}", "V") for kk in range(2)],
        "proj": lambda: [(f"proj {i}", "A")],
        "mv": lambda: [(f"mv{i}", "A")],
        "gate": lambda: [(f"gate {i}", "V")],
        "scores": lambda: [(f"scores{i}", "V" if i >= 24 else "A")],
        "turn": lambda: [(f"turn{i}", "A")],
        "pv": lambda: [(f"pv{i}", "V")],
        "conv": lambda: [(f"conv{i}", "A")],
        "av_ab": lambda: [("av", "A"), ("ab", "A")],
        "log_decay": lambda: [("cum", "V")],
        "l2": lambda: [(f"l2.{i}", "A")],
        "decay": lambda: [(f"gr{i}", "V")],
        "chunk_rows": lambda: [(f"krows{i}", "V"), (f"vrows{i}", "V")],
        "chunk_products": lambda: [(f"kk{i}", "V"), (f"br{i}", "V"), (f"qk{i}", "V")],
        "solve_a": lambda: [(f"p{i}", "A")],
        "solve_b": lambda: ([(f"xx{i}", "V")] if 0 < i[0] < LEVELS - 1 else []) + ([(f"yy{i}", "V")] if i[0] else []),
        "w": lambda: [(f"w{i}", "A")],
        "qg": lambda: [(f"gq{i}", "A")],
        "state": lambda: [(f"vn{i}", "A"), (f"o{i}", "A"), (f"ds{i}", "V")][:3 if i != S // CH - 1 else 2],
        "delta_out": lambda: [(f"on{i}", "A")],
        "c_norm": lambda: [(f"cn{i}", "A")],
        "rope": lambda: [(f"rope{i}", "V"), (f"ropes{i}", "V")],
        "qn": lambda: [(f"qn{i}", "A")],
        "kn": lambda: [(f"kn{i}", "A")],
        "cv": lambda: [(f"cv{i}", "A")],
        "out": lambda: [(f"y{i}.{t}", "A") for t in range(T)],
    }.get(kind, list)()


TASKS = [t for s in STEPS for t in tasks_of(s)]
TASK_AT = {name: i for i, (name, _) in enumerate(TASKS)}
assert len(TASK_AT) == len(TASKS)


def nth(kind, i):
    return [x for k, x in STEPS if k == kind].index(i) + 1


def freed(i):
    who = TASKS[i][1]
    return who, sum(w == who for _, w in TASKS[:i + 1])


def th_uses():
    uses = []
    for kind, i in STEPS:
        if kind == "gate":
            uses.append((f"gate {i}", "bank"))
        elif kind == "conv" and i:
            uses.append((f"conv{i - 1}", "th"))
        elif kind == "av_ab":
            uses.append(("conv11", "th"))
        elif kind in ("l2", "qg", "delta_out", "c_norm"):
            uses.append((f"{kind}{i}", "th"))
    return uses


TH = th_uses()
TH_AT = {name: i for i, (name, _) in enumerate(TH)}


def sq_uses():
    uses = []
    for kind, i in STEPS:
        if kind == "l2":
            uses.append((f"l2.{i}", f"l2.{i}"))
        elif kind == "delta_out":
            uses.append((f"on{i}", f"on{i}"))
        elif kind == "c_norm":
            uses += [("cq0", "cn0"), ("cq1", "cn0")] if i == 0 else [("ckv", "cn1")]
    return uses


SQ = sq_uses()
SQ_AT = {name: i for i, (name, _) in enumerate(SQ)}

CHUNK_LAST = {}
for _s in STEPS:
    _kind, _i = _s
    if _kind in ("proj", "gate"):
        CHUNK_LAST[TILES[_i][0]] = tasks_of(_s)[-1][0]
    elif _kind == "conv":
        CHUNK_LAST[TILES[f"b_{'qkv'[_i // 4]}.{_i % 4}"][0]] = f"conv{_i}"
    elif _kind == "mv":
        CHUNK_LAST[f"memv{_i}"] = f"mv{_i}"
    elif _kind == "av_ab":
        CHUNK_LAST["av_ab"] = "ab"
    elif _kind == "rope" and _i == "k":
        CHUNK_LAST["ckv_kr"], CHUNK_LAST["krs_ak"] = "ropek", "ropesk"
    elif _kind == "out":
        CHUNK_LAST[f"out{_i}0"] = CHUNK_LAST[f"out{_i}1"] = f"y{_i}.{T - 1}"
CHUNK_LAST["krs_ak"] = "proj ak"

N_PARAM_ROWS = KD + KD + 2 + 1 + 1 + 12 * CONV
PRE, MEMN, CQN, CKVN, GDNN, CONVW = 0, KD, 2 * KD, 2 * KD + 2, 2 * KD + 3, 2 * KD + 4


class Memory:

    def __init__(self, nc, ctx):
        def sb(name, shape, dt=F32):
            return ctx.enter_context(nc.sbuf_tensor(name, shape, dt))

        self.consts = sb("consts", [P, CONSTS.shape[1]])
        self.x = sb("x_rows", [P, T, D])
        self.hT = sb("hT", [P, KD, S])
        self.ring = sb("w_ring", [P, SLOTS, KD, WN])
        self.mix = sb("mix", [P, 16, S])
        self.memT = sb("memT", [P, KD, MEM])
        self.cosT = sb("cosT", [P, S])
        self.sinT = sb("sinT", [P, S])
        self.gpost = sb("gpost", [P, D])
        self.pad = sb("pad", [P, 2, S + 4])
        self.th = sb("th", [P, 2, S])
        self.sq = sb("sq", [P, 2, S])
        self.prow = sb("param_rows", [N_PARAM_ROWS, P])
        self.pcol = sb("param_cols", [P, N_PARAM_ROWS])
        self.stat = sb("stat", [P, 5, 2 * len(UNITS)])
        self.small = sb("small", [P, 352])
        self.arena = sb("arena", [P, 18944])
        self.ps = ctx.enter_context(nc.psum_tensor("ps", [P, BANKS, FB], F32))
        self._sem = lambda name: ctx.enter_context(nc.semaphore(name))

    def view(self, at, *shape):
        n = int(np.prod(shape))
        v = self.arena[:, at:at + n]
        if len(shape) == 2:
            v = v.rearrange("p (a b) -> p a b", b=shape[1])
        elif len(shape) == 3:
            v = v.rearrange("p (a b c) -> p a b c", b=shape[1], c=shape[2])
        return v

    def const(self, name):
        at, n = CONST_AT[name]
        return self.consts[:, at:at + n]


def heads(ap):
    return ap.rearrange("p (h c) -> p h c", h=NH)


def prologue(nc, m, ctx, args, bias_dram):
    x, mem, positions, rel_bias, consts = args
    sem = m._sem
    s_const, s_x, s_mem, s_pos, s_rb, s_bias_out = (sem(n) for n in (
        "const_in", "x_in", "mem_in", "pos_in", "rb_in", "bias_out"))
    s_chain, s_stat, s_mact, s_xs, s_steps, s_fill, s_free, s_trig, s_tab, s_sel, s_delta, s_zero, s_posf = (sem(n) for n in (
        "pro_chain", "mem_sums", "mem_rstd", "mem_scaled", "steps_ready", "pro_filled", "pro_freed",
        "angles_ready", "trig_ready", "masked", "delta_ready", "rb_zero", "posf_ready"))

    SLAB = 64
    PER = 16
    steps = [m.arena[:, 4096 * b:4096 * (b + 1)].bitcast(BF16).rearrange("p (k q) -> p k q", q=P) for b in range(2)]
    stage = m.view(8192, 7, 8, P)
    memr = m.view(8192 + 7168, 2, D)
    hs = m.hT[:, :, :].rearrange("p k s -> p (k s)")
    posi = hs[:, 0:512].bitcast(I32)
    posf = hs[:, 512:1024]
    wini = hs[:, 1024:1280].bitcast(I32)
    winf = hs[:, 1280:1536]
    ang, kk, red = hs[:, 1536:2048], hs[:, 2048:2560], hs[:, 2560:3072]
    ang2 = hs[:, 3072:3584]
    rb, rbp, dl, r1, r2 = (hs[:, 3584 + 8 * i:3592 + 8 * i] for i in range(5))
    parts = hs[:, 3640:3652].bitcast(BF16)
    junk = m.ring[:, 0, 0:4, :].rearrange("p k c -> p (k c)")
    ss, lg, rs = m.small[:, 0:2], m.small[:, 2:4], m.small[:, 4:6]

    tasks = [("mem", mt, kh) for mt in range(2) for kh in range(2)]
    first = len(tasks)
    tasks += [("bias", sl, g, part) for sl in range(4) for g in range(1 if sl < 2 else 0, 4) for part in range(SLAB // PER)]

    with nc.Block() as block:
        @block.sync
        def _(sp):
            sp.dma_start(m.consts[:, :], consts[:, :]).then_inc(s_const, 16)
            sp.dma_start(memr, mem[0].rearrange("(t p) d -> p t d", p=P)).then_inc(s_mem, 16)
            sp.dma_start(posi, positions[0:1, :].partition_broadcast(P).rearrange("p a s -> p (a s)")).then_inc(s_pos, 16)
            for g in range(4):
                lo = max(g - 1, 0) * P
                w = P if g == 0 else 2 * P
                sp.dma_start(wini[32 * g:32 * g + 32, 2 * P - w:2 * P],
                             positions[0:1, lo:lo + w].partition_broadcast(32).rearrange("p a s -> p (a s)")).then_inc(s_pos, 16)
            sp.wait_ge(s_zero, 2)
            for g in range(4):
                sp.dma_start(rb[32 * g:32 * g + 32, :], rel_bias[:, :]).then_inc(s_rb, 16)
                sp.dma_start(rbp[32 * g + 1:32 * g + 32, :], rel_bias[0:BUCKETS - 1, :]).then_inc(s_rb, 16)
            sp.dma_start(m.x[:, :, :], x[0].rearrange("(t p) d -> p t d", p=P)).then_inc(s_x, 16)
            sp.wait_ge(s_x, 16)

        @block.gpsimd
        def _(pool):
            pool.memset(rbp, 0.0).then_inc(s_zero, 1)
            pool.memset(m.pad[:, :, 0:CONV - 1], 0.0).then_inc(s_zero, 1)
            last = {}
            for i, (_, sl, g, part) in enumerate(tasks[first:]):
                last[(sl // 2, g)] = i
            n = 0
            for half in range(2):
                for g in range(1 - half, 4):
                    pool.wait_ge(s_free, first + last[(half, g)] + 1)
                    v = stage[:, 2 * g + half - 1, :, :]
                    if half == 0:
                        pool.affine_select(out=v, in_=v, pattern=[[0, 8], [1, P]], compare_op=ALU.is_gt, fill=NEG,
                                           base=0, channel_multiplier=-1).then_inc(s_sel, 1)
                    else:
                        pool.affine_select(out=v, in_=v, pattern=[[0, 8], [-1, P]], compare_op=ALU.is_ge, fill=NEG,
                                           base=0, channel_multiplier=1).then_inc(s_sel, 1)
                    n += 1
                    pool.wait_ge(s_sel, n)
                    pool.dma_start(bias_dram[g, :, :, half * P:(half + 1) * P], v).then_inc(s_bias_out, 16)
            pool.wait_ge(s_bias_out, 16 * n)

        @block.scalar
        def _(act):
            act.wait_ge(s_mem, 16)
            for t in range(2):
                act.activation(junk, memr[:, t, :], ACT.Square, accum_out=ss[:, t:t + 1]).then_inc(s_stat, 1)
                act.wait_ge(s_stat, t + 1)
            act.wait_ge(s_const, 16)
            act.activation(lg, ss, ACT.Ln, scale=1.0 / D, bias=m.const("eps")).then_inc(s_stat, 1)
            act.wait_ge(s_stat, 3)
            act.activation(rs, lg, ACT.Exp, scale=-0.5).then_inc(s_mact, 1)
            act.wait_ge(s_trig, 1)
            act.activation(m.cosT[:, :], ang2, ACT.Sin).then_inc(s_tab, 1)
            act.wait_ge(s_trig, 2)
            act.activation(m.sinT[:, :], ang, ACT.Sin).then_inc(s_tab, 1)

        @block.vector
        def _(dve):
            chain = [0]

            def link(ins):
                chain[0] += 1
                ins.then_inc(s_chain, 1)
                dve.wait_ge(s_chain, chain[0])

            dve.wait_ge(s_pos, 80)
            dve.wait_ge(s_const, 16)
            link(dve.tensor_copy(winf[:, P:2 * P], wini[:, P:2 * P]))
            for g in range(1, 4):
                link(dve.tensor_copy(winf[32 * g:32 * g + 32, 0:P], wini[32 * g:32 * g + 32, 0:P]))
            dve.wait_ge(s_rb, 128)
            link(dve.tensor_tensor(dl, rb, rbp, ALU.subtract))
            link(dve.tensor_copy(parts[:, 0:8], dl))
            link(dve.tensor_tensor(r1, dl, parts[:, 0:8], ALU.subtract))
            link(dve.tensor_copy(parts[:, 8:16], r1))
            link(dve.tensor_tensor(r2, r1, parts[:, 8:16], ALU.subtract))
            dve.tensor_copy(parts[:, 16:24], r2).then_inc(s_delta, 1)

            def make_steps(sl):
                if sl >= 2:
                    done = [i for i, t in enumerate(tasks) if t[:2] == ("bias", sl - 2)]
                    dve.wait_ge(s_fill, done[-1] + 1)
                lo = 32 if sl < 2 else 0
                for a in ((32, 64), (64, 128)) if lo else ((0, 128),):
                    ins = dve.scalar_tensor_tensor(
                        out=steps[sl % 2][a[0]:a[1], :, :],
                        in0=winf[a[0]:a[1], SLAB * sl:SLAB * (sl + 1)].unsqueeze(2).to_broadcast([a[1] - a[0], SLAB, P]),
                        scalar=m.const("bucket_least")[a[0]:a[1], :],
                        in1=winf[a[0]:a[1], P:2 * P].unsqueeze(1).to_broadcast([a[1] - a[0], SLAB, P]),
                        op0=ALU.add, op1=ALU.is_le)
                ins.then_inc(s_steps, 1)

            make_steps(0)
            link(dve.tensor_copy(posf, posi))
            link(dve.tensor_scalar(red, posf, m.const("inv_freq"), None, ALU.mult))
            magic = float(1.5 * 2 ** 23)
            c1 = 6.28125
            c2 = float((np.array(np.float32(2 * math.pi - c1)).view(np.int32) & np.int32(-4096)).view(np.float32))
            c3 = float(np.float32(2 * math.pi - c1 - c2))
            for i, (dst, turn) in enumerate(((ang2, 0.25), (ang, 0.0))):
                link(dve.tensor_scalar(kk, red, float(1 / (2 * math.pi)), turn, ALU.mult, ALU.add))
                link(dve.tensor_scalar(kk, kk, magic, None, ALU.add))
                link(dve.tensor_scalar(kk, kk, magic, None, ALU.subtract))
                link(dve.scalar_tensor_tensor(out=dst, in0=kk, scalar=-c1, in1=red, op0=ALU.mult, op1=ALU.add))
                link(dve.scalar_tensor_tensor(out=dst, in0=kk, scalar=-c2, in1=dst, op0=ALU.mult, op1=ALU.add))
                link(dve.scalar_tensor_tensor(out=dst, in0=kk, scalar=-c3, in1=dst, op0=ALU.mult, op1=ALU.add))
                link(dve.tensor_scalar(dst, dst, turn * 2 * math.pi, 3.1415925, ALU.add, ALU.min))
                dve.tensor_scalar(dst, dst, -3.1415925, None, ALU.max).then_inc(s_trig, 1)
            dve.wait_ge(s_tab, 2)
            link(dve.tensor_scalar(m.sinT[:, :], m.sinT[:, :], m.const("rope_sign"), None, ALU.mult))
            dve.wait_ge(s_mact, 1)
            for t in range(2):
                dve.tensor_scalar(memr[:, t, :], memr[:, t, :], rs[:, t:t + 1], None, ALU.mult).then_inc(s_xs, 1)
            made = 1
            for i, task in enumerate(tasks):
                bank = m.ps[:, i % BANKS, :]
                if task[0] == "mem":
                    _, mt, kh = task
                    dve.wait_ge(s_fill, i + 1)
                    dve.tensor_copy(m.memT[:, 4 * kh:4 * kh + 4, mt * P:(mt + 1) * P],
                                    bank.rearrange("p (k c) -> p k c", k=4)).then_inc(s_free, 1)
                    continue
                _, sl, g, part = task
                if made == sl + 1 and made < 4:
                    make_steps(made)
                    made += 1
                dve.wait_ge(s_fill, i + 1)
                k0 = (sl % 2) * SLAB + part * PER
                dve.tensor_reduce(stage[:, 2 * g + sl // 2 - 1, :, k0:k0 + PER].rearrange("p h k -> p k h"),
                                  bank[:, 0:PER * 24].rearrange("p (k s h) -> p k h s", s=3, h=8),
                                  AX.X, ALU.add).then_inc(s_free, 1)

        @block.tensor
        def _(pe):
            pe.wait_ge(s_const, 16)
            for i, task in enumerate(tasks):
                bank = m.ps[:, i % BANKS, :]
                if i >= BANKS:
                    pe.wait_ge(s_free, i - BANKS + 1)
                if task[0] == "mem":
                    _, mt, kh = task
                    pe.wait_ge(s_xs, mt + 1)
                    for k in range(4):
                        last = pe.transpose(bank[:, k * P:(k + 1) * P], memr[:, mt, (4 * kh + k) * P:(4 * kh + k + 1) * P],
                                            m.const("ident"))
                    last.then_inc(s_fill, 1)
                    continue
                _, sl, g, part = task
                if i == first:
                    pe.wait_ge(s_delta, 1)
                pe.wait_ge(s_steps, sl + 1)
                for k in range(PER):
                    last = pe.matmul(bank[:, 24 * k:24 * (k + 1)], steps[sl % 2][32 * g:32 * g + 32, part * PER + k, :],
                                     parts[32 * g:32 * g + 32, 0:24], start=True, stop=True)
                last.then_inc(s_fill, 1)


def layer(nc, m, l, w, bias_dram, layer_sems):
    (s_fill, s_act, s_dve, s_slot, s_par, s_uq, s_bias, s_gpost, s_rstd, s_xs, s_memg, s_actc, s_dvec, s_neg, s_expA,
     s_norm, s_taps, s_th, s_thused, s_sq, s_ab, s_nabs, s_ln1p, s_g, s_dec, s_diff, s_exps,
     s_bt, s_sol0, s_mixB, s_cq0, s_rope, s_xfin, s_y) = layer_sems

    xs = m.view(0, T, D)
    junk = m.arena[:, 4096:5120]
    memg = m.view(4096 + 1024, KD, MEM)
    mkT = m.view(7168, NH, MEM)
    mvr = m.view(8192, 2, GW)
    dqT = m.view(9216, NH, S)
    ptD = m.view(11264, 2, 2, S)
    qkvT = m.view(0, 12, S)
    kbg, kd, vb = (m.view(6144 + 2048 * i, T, NH, P) for i in range(3))
    LT = m.view(12288, T, NH * P)
    BT = m.view(14336, T, NH * P)
    state = m.view(16384, 2, NH * P)
    avr = m.view(17408, T, P)
    vnew = m.view(17920, 2, NH * P)
    Xm, Ym = qkvT[:, 8:12, :], qkvT[:, 4:8, :]
    nwT = LT
    oT = kbg.rearrange("p t h c -> p t (h c)")
    Aqk = m.mix[:, 0:4, :]
    dec = m.mix[:, 8:12, :]
    cqT, ckvT = m.view(0, 2, S), m.arena[:, 1024:1536]
    qnT, qrT, knT = m.view(1536, NH, S), m.view(3584, 2, S), m.view(4608, NH, S)
    krT = m.arena[:, 6656:7168]
    cvr = m.view(7168, T, GW)
    pt = m.view(9216, 2, 4, S)
    craw = m.view(9216, 3, S)
    uqs = m.view(13312, 2, 2, P)
    uqr = m.mix[:, 3, :].rearrange("p (k b c) -> p k b c", k=2, b=2)
    ukv = m.arena[:, 13824:14848].rearrange("p (h c) -> p h c", h=NH)
    aqT, akT = m.view(14848, NH, S), m.arena[:, 16896:17408]
    uq = m.mix[:, 0:3, :].rearrange("p k s -> p (k s)").rearrange("p (k c) -> p k c", k=2)
    bias = m.hT[:, :, :].rearrange("p k s -> p (k s)").rearrange("p (b h c) -> p b h c", b=2, h=8)
    y = m.view(0, T, D)
    prob = m.pad[:, :, CONV - 1:CONV - 1 + S]

    sm = m.small
    ss, lg, rstd = sm[:, 0:4], sm[:, 4:8], sm[:, 8:12]
    alog, dtb, sink = sm[:, 12:16], sm[:, 16:20], sm[:, 20:28]
    abr = sm[:, 32:64].rearrange("p (t c) -> p t c", t=T)
    tb, beta, xdt, mx, nabs, lnp, g16, ea = (sm[:, 64 + 16 * i:80 + 16 * i] for i in range(8))
    gc = sm[:, 192:224]
    gdiff, eg, ed, nbeg, vbs = (sm[:, 224 + 16 * i:240 + 16 * i] for i in range(5))
    gle = sm[:, 304:336].rearrange("p (t h c) -> p t h c", t=T, h=NH)
    ss2, lg2, rs2 = sm[:, 336:340], sm[:, 340:344], sm[:, 344:348]

    def th4(ap):
        return ap.rearrange("p (t h) -> p t h", t=T)

    def weights(name):
        return w[name][bass.ds(l, 1)]

    def done(name):
        who, n = freed(TASK_AT[name])
        return (s_act if who == "A" else s_dve), n

    def filled(name):
        return s_fill, TASK_AT[name] + 1

    def th_free(i):
        name, by = TH[i - 2]
        return done(name) if by == "bank" else used(name)

    def used(name):
        return s_thused, sum(by == "th" for _, by in TH[:TH_AT[name] + 1])

    def bank(name):
        return m.ps[:, TASK_AT[name] % BANKS, :]

    def segments(u):
        _, _, _, n, width = UNITS[u]
        return n, width

    def stats(row, u):
        return m.stat[:, row, 2 * u:2 * u + UNITS[u][3]]

    def pieces(name):
        def cols(c0, n, at, src="w_in"):
            return (slice(at, at + n), slice(0, P), slice(0, KD),
                    weights(src)[:, :, c0:c0 + n].rearrange("a (k p) c -> p (a k) c", p=P))

        if name.startswith("mem"):
            return [cols(("kv".index(name[3]) * 2 + int(name[4])) * WN, WN, 0, "mem_w_kv")]
        if name == "av_ab":
            return [cols(OFF["a_v"], P, 0), cols(OFF["b_ab"], 8, P)]
        if name == "c_q":
            return [cols(OFF["c_q"], WN, 0)]
        if name == "ckv_kr":
            return [cols(OFF["c_kv"], P + ROPE, 0), cols(OFF["c_kr"], ROPE, P + ROPE)]
        if name == "krs_ak":
            return [cols(OFF["c_kr"] + 32 * (1 - i % 2), 32, 32 * i) for i in range(4)] + [cols(OFF["a_k"], P, P)]
        if name.startswith("a_"):
            i = int(name[3])
            return [cols(OFF[name[:3]] + 256 * half + 64 * (2 * i + j), 64, P * j + 64 * half)
                    for j in range(2) for half in range(2)]
        if name.startswith("out"):
            n, kh = int(name[3]), int(name[4])
            src = weights("w_out")[:, :, WN * n:WN * (n + 1)]
            if kh:
                return [(slice(0, WN), slice(0, P), slice(0, KD), src[:, D:2 * D, :].rearrange("a (k p) c -> p (a k) c", p=P))]
            return [(slice(0, WN), slice(64 * half, 64 * half + 64), slice(0, 4),
                     src[:, 256 * half:256 * half + 256, :].rearrange("a (k p) c -> p (a k) c", p=64)) for half in range(2)] + [
                (slice(0, WN), slice(0, P), slice(4, 8), src[:, GW:D, :].rearrange("a (k p) c -> p (a k) c", p=P))]
        return [cols(OFF[name[:3]] + WN * int(name[3]), WN, 0)]

    n_pieces = [len(pieces(c)) for c in CHUNKS]

    def arrived(chunk):
        i = CHUNKS.index(chunk)
        return s_slot[i % SLOTS], 16 * sum(n_pieces[i % SLOTS:i + 1:SLOTS])

    def slot(chunk):
        return m.ring[:, CHUNKS.index(chunk) % SLOTS, :, :]

    with nc.Block() as block:
        @block.sync
        def _(sp):
            r = m.prow
            rows = [("norm_pre", PRE, KD), ("mem_norm", MEMN, KD), ("mla_q_norm", CQN, 2), ("mla_kv_norm", CKVN, 1),
                    ("gdn_norm", GDNN, 1)]
            for name, at, n in rows:
                sp.dma_start(r[at:at + n, :], weights(name).rearrange("a (k p) -> (a k) p", p=P)).then_inc(s_par, 16)
            sp.dma_start(r[CONVW:CONVW + 12 * CONV, :],
                         weights("gdn_conv_w").rearrange("a t (j p) -> (a t j) p", p=P)).then_inc(s_par, 16)
            for dst, name in ((alog, "gdn_a_log"), (dtb, "gdn_dt_bias"), (sink, "attn_sinks")):
                sp.dma_start(dst, weights(name).partition_broadcast(P).rearrange("p a c -> p (a c)")).then_inc(s_par, 16)
            sp.dma_start(m.gpost[:, :], weights("norm_post").partition_broadcast(P).rearrange("p a c -> p (a c)")).then_inc(s_gpost, 16)
            for i, chunk in enumerate(CHUNKS):
                if i >= SLOTS:
                    sp.wait_ge(*filled(CHUNK_LAST[CHUNKS[i - SLOTS]]))
                for cs, ps, ks, src in pieces(chunk):
                    sp.dma_start(m.ring[ps, i % SLOTS, ks, cs], src).then_inc(s_slot[i % SLOTS], 16)
                if chunk == "c_q":
                    sp.wait_ge(*filled(f"o{S // CH - 1}"))
                    sp.wait_ge(*done(f"on{NH - 1}"))
                    sp.dma_start(uq, weights("mla_w_uq").rearrange("a (k p) c -> p (a k) c", p=P)).then_inc(s_uq, 16)
                    for k in range(2):
                        for half in range(2):
                            src = weights("mla_w_uq")[:, k * P:(k + 1) * P, :].rearrange("a p (h c) -> p (a h) c", h=NH)
                            sp.dma_start(uqs[:, k, :, :].rearrange("p b c -> p (b c)").rearrange("p (h c) -> p h c", h=NH)[:, :, 32 * half:32 * half + 32],
                                         src[:, :, NOPE + 32 * (1 - half):NOPE + 32 * (1 - half) + 32]).then_inc(s_uq, 16)
                        sp.dma_start(uqr[:, k, :, :].rearrange("p b c -> p (b c)").rearrange("p (h c) -> p h c", h=NH),
                                     src[:, :, NOPE:NOPE + ROPE]).then_inc(s_uq, 16)
                    sp.dma_start(ukv.rearrange("p h c -> p (h c)"), weights("mla_w_ukv").rearrange("a p c -> p (a c)")).then_inc(s_uq, 16)
                if chunk == "out01":
                    sp.wait_ge(*filled("gate a_z.3"))
                    for blk in range(T):
                        if blk >= 2:
                            sp.wait_ge(*done(f"scores{24 + 4 * (blk - 2) + 3}"))
                        lo = P if blk == 0 else 0
                        sp.dma_start(bias[:, blk % 2, :, lo:2 * P], bias_dram[blk, :, :, lo:2 * P]).then_inc(s_bias[blk % 2], 16)

        @block.gpsimd
        def _(pool):
            for kind, i in STEPS:
                if kind == "solve_a":
                    lv, t = i
                    pool.wait_ge(*done(f"br{t}"))
                    if lv:
                        pool.wait_ge(*filled(f"p{(lv - 1, t)}"))
                    if lv == 1:
                        pool.wait_ge(s_sol0, t + 1)
                    pool.tensor_tensor(heads(BT[:, t, :]), heads(LT[:, t, :]),
                                       m.const(f"level{lv}").unsqueeze(1).to_broadcast([P, NH, P]), ALU.mult).then_inc(s_bt, 1)

        @block.tensor
        def _(pe):
            ident, ones = m.const("ident"), m.const("ones")

            def open_bank(name):
                i = TASK_AT[name]
                if i >= BANKS:
                    who, n = freed(i - BANKS)
                    pe.wait_ge(s_act if who == "A" else s_dve, n)
                return bank(name)

            def project(out, chunk, c0, rhs):
                pe.wait_ge(*arrived(chunk))
                for k in range(KD):
                    last = pe.matmul(out, slot(chunk)[:, k, c0:c0 + P], rhs[:, k, :], start=(k == 0), stop=(k == KD - 1))
                return last

            for kind, i in STEPS:
                if kind == "params":
                    b = open_bank("params")
                    pe.wait_ge(s_par, 9 * 16)
                    pe.transpose(b[:, 0:N_PARAM_ROWS], m.prow[:, :], ident[0:N_PARAM_ROWS, 0:N_PARAM_ROWS]).then_inc(s_fill, 1)

                elif kind == "xt":
                    pe.wait_ge(s_xs, i + 1)
                    for kk in range(2):
                        b = open_bank(f"xt{i}.{kk}")
                        for k in range(4):
                            last = pe.transpose(b[:, k * P:(k + 1) * P], xs[:, i, (4 * kk + k) * P:(4 * kk + k + 1) * P], ident)
                        last.then_inc(s_fill, 1)

                elif kind in ("proj", "gate", "conv"):
                    tile_name = f"b_{'qkv'[i // 4]}.{i % 4}" if kind == "conv" else i
                    chunk, c0 = TILES[tile_name]
                    task = f"conv{i}" if kind == "conv" else f"{kind} {i}"
                    b = open_bank(task)
                    if tile_name.startswith("mk"):
                        pe.wait_ge(s_memg, 1)
                        project(b[:, 0:MEM], chunk, c0, memg).then_inc(s_fill, 1)
                    else:
                        pe.wait_ge(*done("xt3.1"))
                        project(b, chunk, c0, m.hT).then_inc(s_fill, 1)

                elif kind == "mv":
                    b = open_bank(f"mv{i}")
                    pe.wait_ge(*arrived(f"memv{i}"))
                    for mt in range(2):
                        for k in range(KD):
                            last = pe.matmul(b[:, mt * WN:(mt + 1) * WN], memg[:, k, mt * P:(mt + 1) * P],
                                             slot(f"memv{i}")[:, k, :], start=(k == 0), stop=(k == KD - 1))
                    last.then_inc(s_fill, 1)

                elif kind == "av_ab":
                    pe.wait_ge(*arrived("av_ab"))
                    for task, c0, n in (("av", 0, P), ("ab", P, 8)):
                        b = open_bank(task)
                        for t in range(T):
                            for k in range(KD):
                                last = pe.matmul(b[:, t * n:(t + 1) * n], m.hT[:, k, t * P:(t + 1) * P],
                                                 slot("av_ab")[:, k, c0:c0 + n], start=(k == 0), stop=(k == KD - 1))
                        last.then_inc(s_fill, 1)

                elif kind == "scores":
                    group, a, c, n, width = UNITS[i]
                    b = open_bank(f"scores{i}")
                    if group == "D":
                        pe.wait_ge(*done(f"proj d_q.{a}"))
                        for tl in range(2):
                            t = 2 * c + tl
                            last = pe.matmul(b[:, tl * MEM:(tl + 1) * MEM], dqT[:, a, t * P:(t + 1) * P], mkT[:, a, :],
                                             start=True, stop=True)
                    elif group == "C":
                        pe.wait_ge(*done(f"kn{a}"))
                        pe.wait_ge(s_rope, 3)
                        r = slice(64 * (a % 2), 64 * (a % 2) + 64)
                        pe.matmul(b[:, 0:width], qnT[:, a, c * P:(c + 1) * P], knT[:, a, 0:width], start=True, stop=False)
                        pe.matmul(b[:, width - P:width], ident, m.const("causal_neg"), start=False, stop=False)
                        last = pe.matmul(b[:, 0:width], qrT[r, a // 2, c * P:(c + 1) * P], krT[r, 0:width], start=False,
                                         stop=True)
                    else:
                        s, jp = divmod(c, 2)
                        pe.wait_ge(*done("proj a_q.3"))
                        pe.wait_ge(*done("proj ak"))
                        r = slice(64 * s, 64 * s + 64)
                        k1 = (a + 1) * P
                        for jj in range(2):
                            last = pe.matmul(b[:, jj * width:(jj + 1) * width], aqT[r, 2 * jp + jj, a * P:(a + 1) * P],
                                             akT[r, k1 - width:k1], start=True, stop=True)
                    last.then_inc(s_fill, 1)

                elif kind == "turn":
                    group, a, c, n, width = UNITS[i]
                    b = open_bank(f"turn{i}")
                    pe.wait_ge(s_norm, i + 1)
                    p = prob[:, i % 2, :]
                    nb = width // P
                    for seg in range(n):
                        for j in range(nb):
                            at = seg * P + j * n * P
                            last = pe.transpose(b[:, at:at + P], p[:, seg * width + j * P:seg * width + (j + 1) * P], ident)
                    last.then_inc(s_fill, 1)

                elif kind == "pv":
                    group, a = GROUPS[i]
                    b = open_bank(f"pv{i}")
                    pe.wait_ge(*done(f"turn{max(u for u in range(len(UNITS)) if GROUP_OF[u] == i)}"))
                    if group == "D":
                        for mt in range(2):
                            last = pe.matmul(b, mvr[:, mt, a * P:(a + 1) * P], ptD[:, i % 2, mt, :], start=(mt == 0), stop=(mt == 1))
                    elif group == "C":
                        for j in range(T):
                            last = pe.matmul(b[:, j * P:S], cvr[:, j, a * P:(a + 1) * P], pt[:, i % 2, j, j * P:S],
                                             start=(j == 0), stop=True, skip_group_check=(j > 0))
                    else:
                        ptv = pt[:, i % 2, :, :].rearrange("p (s f) c -> p s f c", s=2)
                        pe.wait_ge(*done("av"))
                        for s in range(2):
                            r = slice(64 * s, 64 * s + 64)
                            for half in range(0 if a else 1, 2):
                                last = pe.matmul(b[r, :], avr[:, a - 1 + half, r], ptv[:, s, half, :],
                                                 start=(half == 0 or a == 0), stop=(half == 1))
                    last.then_inc(s_fill, 1)

                elif kind == "log_decay":
                    b = open_bank("cum")
                    pe.wait_ge(s_g, 1)
                    pe.matmul(b[:, 0:16], m.const("upto"), g16, start=True, stop=True)
                    pe.matmul(b[:, 16:32], m.const("chunk"), g16, start=True, stop=True).then_inc(s_fill, 1)

                elif kind == "l2":
                    b = open_bank(f"l2.{i}")
                    at = SQ_AT[f"l2.{i}"]
                    pe.wait_ge(s_sq, at + 1)
                    pe.matmul(b, ones, m.sq[:, at % 2, :], start=True, stop=True).then_inc(s_fill, 1)

                elif kind == "decay":
                    b = open_bank(f"gr{i}")
                    for h in range(NH):
                        g = g16[:, 4 * i + h:4 * i + h + 1]
                        last = pe.matmul(b[:, h * P:(h + 1) * P], g.to_broadcast([P, P]), m.const("upto"), start=True, stop=True)
                    last.then_inc(s_fill, 1)

                elif kind == "chunk_rows":
                    for name, first, ready in ((f"krows{i}", 4, "l27"), (f"vrows{i}", 8, "conv11")):
                        b = open_bank(name)
                        pe.wait_ge(*used(ready))
                        for h in range(NH):
                            last = pe.transpose(b[:, h * P:(h + 1) * P], qkvT[:, first + h, i * P:(i + 1) * P], ident)
                        last.then_inc(s_fill, 1)

                elif kind == "chunk_products":
                    tc = slice(i * P, (i + 1) * P)
                    b = open_bank(f"kk{i}")
                    for h in range(NH):
                        last = pe.matmul(b[:, h * P:(h + 1) * P], qkvT[:, 4 + h, tc], qkvT[:, 4 + h, tc], start=True, stop=True)
                    last.then_inc(s_fill, 1)
                    b = open_bank(f"br{i}")
                    for h in range(NH):
                        bc = beta[:, 4 * i + h:4 * i + h + 1]
                        last = pe.matmul(b[:, h * P:(h + 1) * P], bc.to_broadcast([P, P]), ident, start=True, stop=True)
                    last.then_inc(s_fill, 1)
                    b = open_bank(f"qk{i}")
                    for h in range(NH):
                        last = pe.matmul(b[:, h * P:(h + 1) * P], qkvT[:, 4 + h, tc], qkvT[:, h, tc], start=True, stop=True)
                    last.then_inc(s_fill, 1)

                elif kind == "solve_a":
                    lv, t = i
                    b = open_bank(f"p{i}")
                    pe.wait_ge(s_bt, nth("solve_a", i))
                    if lv == 1:
                        pe.wait_ge(s_sol0, t + 1)
                    if lv > 1:
                        pe.wait_ge(*done(f"xx{(lv - 1, t)}"))
                    for h in range(NH):
                        hc = slice(h * P, (h + 1) * P)
                        last = pe.matmul(b[:, hc], BT[:, t, hc], Xm[:, t, hc] if lv else ident, start=True, stop=True)
                    last.then_inc(s_fill, 1)

                elif kind == "solve_b":
                    lv, t = i
                    if lv == 0:
                        continue
                    pe.wait_ge(*done(f"p{i}"))
                    if lv > 1:
                        pe.wait_ge(*done(f"yy{(lv - 1, t)}"))
                    if lv < LEVELS - 1:
                        b = open_bank(f"xx{i}")
                        for h in range(NH):
                            hc = slice(h * P, (h + 1) * P)
                            last = pe.matmul(b[:, hc], Ym[:, t, hc], dec[:, t, hc], start=True, stop=True)
                        last.then_inc(s_fill, 1)
                    b = open_bank(f"yy{i}")
                    for h in range(NH):
                        hc = slice(h * P, (h + 1) * P)
                        last = pe.matmul(b[:, hc], dec[:, t, hc], Ym[:, t, hc], start=True, stop=True)
                    last.then_inc(s_fill, 1)

                elif kind == "w":
                    b = open_bank(f"w{i}")
                    pe.wait_ge(*done(f"krows{i}"))
                    pe.wait_ge(*done(f"yy{(LEVELS - 1, i)}"))
                    for h in range(NH):
                        last = pe.matmul(b[:, h * P:(h + 1) * P], kbg[:, i, h, :], Ym[:, i, h * P:(h + 1) * P], start=True, stop=True)
                    last.then_inc(s_fill, 1)

                elif kind == "qg":
                    b = open_bank(f"gq{i}")
                    for h in range(NH):
                        g = g16[:, 4 * i + h:4 * i + h + 1]
                        last = pe.matmul(b[:, h * P:(h + 1) * P], g.to_broadcast([P, P]), m.const("upto"), start=True, stop=True)
                    last.then_inc(s_fill, 1)

                elif kind == "state":
                    t, r = i // 2, slice(CH * (i % 2), CH * (i % 2) + CH)
                    c0 = CH * (i % 2)
                    st = state[:, i % 2, :]
                    b = open_bank(f"vn{i}")
                    pe.wait_ge(*done(f"vrows{t}"))
                    pe.wait_ge(*done(f"w{t}"))
                    if i:
                        pe.wait_ge(*done(f"ds{i - 1}"))
                    for h in range(NH):
                        hc = slice(h * P, (h + 1) * P)
                        last = pe.matmul(b[r, hc], Ym[r, t, h * P + c0:h * P + c0 + CH], vb[r, t, h, :], start=True, stop=(i == 0))
                        if i:
                            last = pe.matmul(b[r, hc], nwT[:, t, h * P + c0:h * P + c0 + CH], st[:, hc], start=False, stop=True)
                    last.then_inc(s_fill, 1)
                    b = open_bank(f"o{i}")
                    pe.wait_ge(*used(f"qg{t}"))
                    pe.wait_ge(*done(f"vn{i}"))
                    for h in range(NH):
                        hc, oc = slice(h * P, (h + 1) * P), slice(h * CH, (h + 1) * CH)
                        if i:
                            pe.matmul(b[:, oc], st[:, hc], qkvT[:, h, i * CH:(i + 1) * CH], start=True, stop=False)
                        last = pe.matmul(b[:, oc], vnew[r, i % 2, hc], Aqk[r, t, h * P + c0:h * P + c0 + CH],
                                         start=(i == 0), stop=True)
                    last.then_inc(s_fill, 1)
                    if i < S // CH - 1:
                        b = open_bank(f"ds{i}")
                        for h in range(NH):
                            hc = slice(h * P, (h + 1) * P)
                            last = pe.matmul(b[:, hc], kd[r, t, h, :], vnew[r, i % 2, hc], start=True, stop=True)
                        last.then_inc(s_fill, 1)

                elif kind == "delta_out":
                    b = open_bank(f"on{i}")
                    at = SQ_AT[f"on{i}"]
                    pe.wait_ge(s_sq, at + 1)
                    pe.matmul(b, ones, m.sq[:, at % 2, :], start=True, stop=True).then_inc(s_fill, 1)

                elif kind == "c_norm":
                    b = open_bank(f"cn{i}")
                    names = ("cq0", "cq1") if i == 0 else ("ckv",)
                    for n, name in enumerate(names):
                        at = SQ_AT[name]
                        pe.wait_ge(s_sq, at + 1)
                        last = pe.matmul(b, ones, m.sq[:, at % 2, :], start=(n == 0), stop=(n == len(names) - 1))
                    last.then_inc(s_fill, 1)

                elif kind == "rope":
                    if i == "k":
                        for task, tile_name in (("ropek", "kr"), ("ropesk", "krs")):
                            b = open_bank(task)
                            project(b, *TILES[tile_name], m.hT).then_inc(s_fill, 1)
                    else:
                        pe.wait_ge(s_uq, 8 * 16)
                        pe.wait_ge(*used("c_norm0"))
                        for task in (f"rope{i}", f"ropes{i}"):
                            b = open_bank(task)
                            for k in range(2):
                                lhs = (uqr if task == f"rope{i}" else uqs)[:, k, i, :]
                                last = pe.matmul(b, lhs, cqT[:, k, :], start=(k == 0), stop=(k == 1))
                            last.then_inc(s_fill, 1)

                elif kind == "qn":
                    b = open_bank(f"qn{i}")
                    pe.wait_ge(s_uq, 8 * 16)
                    pe.wait_ge(*used("c_norm0"))
                    for k in range(2):
                        last = pe.matmul(b, uq[:, k, i * (NOPE + ROPE):i * (NOPE + ROPE) + NOPE], cqT[:, k, :],
                                         start=(k == 0), stop=(k == 1))
                    last.then_inc(s_fill, 1)

                elif kind == "kn":
                    b = open_bank(f"kn{i}")
                    pe.wait_ge(*used("c_norm1"))
                    pe.matmul(b, ukv[:, i, 0:NOPE], ckvT, start=True, stop=True).then_inc(s_fill, 1)

                elif kind == "cv":
                    b = open_bank(f"cv{i}")
                    pe.matmul(heads(b), ckvT[:, i * P:(i + 1) * P], ukv[:, :, NOPE:2 * NOPE], start=True, stop=True).then_inc(s_fill, 1)

                elif kind == "out":
                    for t in range(T):
                        b = open_bank(f"y{i}.{t}")
                        if i == 0 and t == 0:
                            for g in range(len(GROUPS)):
                                pe.wait_ge(*done(f"pv{g}"))
                            pe.wait_ge(s_mixB, NH)
                        for k in range(16):
                            chunk = f"out{i}{k // 8}"
                            if t == 0 and k % 8 == 0:
                                pe.wait_ge(*arrived(chunk))
                            last = pe.matmul(b[:, 0:WN], m.mix[:, k, t * P:(t + 1) * P], slot(chunk)[:, k % 8, :],
                                             start=(k == 0), stop=(k == 15))
                        last.then_inc(s_fill, 1)

        @block.scalar
        def _(act):
            chain = [0]

            def link(ins):
                chain[0] += 1
                ins.then_inc(s_actc, 1)
                act.wait_ge(s_actc, chain[0])

            eps = m.const("eps")

            def tanh_half(src, name, first_wait):
                at = TH_AT[name]
                act.wait_ge(*first_wait)
                if at >= 2:
                    act.wait_ge(*th_free(at))
                act.activation(m.th[:, at % 2, :], src, ACT.Tanh, scale=0.5).then_inc(s_th, 1)

            def square(src, name):
                at = SQ_AT[name]
                if at >= 2:
                    act.wait_ge(*filled(SQ[at - 2][1]))
                act.activation(m.sq[:, at % 2, :], src, ACT.Square).then_inc(s_sq, 1)

            def inv_root(task, name, scale):
                at = TH_AT[name]
                act.wait_ge(*filled(task))
                act.wait_ge(*th_free(at))
                act.activation(m.th[:, at % 2, :], bank(task), ACT.Ln, scale=scale, bias=eps).then_inc(s_act, 1)
                act.wait_ge(*done(task))
                act.activation(m.th[:, at % 2, :], m.th[:, at % 2, :], ACT.Exp, scale=-0.5).then_inc(s_th, 1)

            def copy(task, dst, src, scale=1.0):
                act.wait_ge(*filled(task))
                act.activation(dst, src, ACT.Copy, scale=scale).then_inc(s_act, 1)

            for kind, i in STEPS:
                if kind == "params":
                    for t in range(T):
                        link(act.activation(junk, m.x[:, t, :], ACT.Square, accum_out=ss[:, t:t + 1]))
                    link(act.activation(lg, ss, ACT.Ln, scale=1.0 / D, bias=eps))
                    act.activation(rstd, lg, ACT.Exp, scale=-0.5).then_inc(s_rstd, 1)
                    copy("params", m.pcol[:, :], bank("params")[:, 0:N_PARAM_ROWS])

                elif kind == "proj":
                    group, j = (i.split(".") + ["0"])[:2]
                    j = int(j)
                    if i == "c_q.0":
                        act.wait_ge(*done(f"on{NH - 1}"))
                        act.wait_ge(s_mixB, NH)
                    b = bank(f"proj {i}")
                    if group == "mk":
                        copy(f"proj {i}", mkT[:, j, :], b[:, 0:MEM])
                    else:
                        dst = {"d_q": dqT[:, j, :], "c_q": craw[:, min(j, 1), :], "ckv": craw[:, 2, :], "ak": akT,
                               "a_q": aqT[:, j, :]}[group]
                        copy(f"proj {i}", dst, b, SWA_D ** -0.5 if group == "a_q" else 1.0)
                        if group in ("c_q", "ckv"):
                            act.wait_ge(*done(f"proj {i}"))
                            square(dst, f"cq{j}" if group == "c_q" else "ckv")

                elif kind == "mv":
                    copy(f"mv{i}", mvr[:, :, i * WN:(i + 1) * WN], bank(f"mv{i}").rearrange("p (m c) -> p m c", m=2))

                elif kind == "gate":
                    tanh_half(bank(f"gate {i}"), f"gate {i}", filled(f"gate {i}"))

                elif kind == "scores":
                    n, width = segments(i)
                    group = UNITS[i][0]
                    act.wait_ge(s_neg, i + 1)
                    if group != "A" and i >= 2:
                        act.wait_ge(*filled(f"turn{i - 2}"))
                    for seg in range(n):
                        cs = slice(seg * width, (seg + 1) * width)
                        src = prob[:, i % 2, cs] if group == "A" else bank(f"scores{i}")[:, cs]
                        ins = act.activation(prob[:, i % 2, cs], src, ACT.Exp, scale=SCALE[group],
                                             bias=stats(1, i)[:, seg:seg + 1], accum_out=stats(2, i)[:, seg:seg + 1])
                    if group == "A":
                        act.activation(stats(3, i), stats(3, i), ACT.Exp).then_inc(s_expA, 1)
                    else:
                        ins.then_inc(s_act, 1)

                elif kind == "turn":
                    group, a, c, n, width = UNITS[i]
                    g = GROUP_OF[i]
                    act.wait_ge(*filled(f"turn{i}"))
                    first = [u for u in range(len(UNITS)) if GROUP_OF[u] == g][0]
                    if i == first and g >= 2:
                        act.wait_ge(*filled(f"pv{g - 2}"))
                    nb = width // P
                    src = bank(f"turn{i}")[:, 0:nb * n * P].rearrange("p (j c) -> p j c", j=nb)
                    if group == "D":
                        dst = ptD[:, g % 2, :, 2 * c * P:(2 * c + 2) * P]
                    elif group == "C":
                        dst = pt[:, g % 2, 0:nb, c * P:(c + 1) * P]
                    else:
                        s, jp = divmod(c, 2)
                        dst = pt[:, g % 2, 2 * s + 2 - nb:2 * s + 2, 2 * jp * P:(2 * jp + 2) * P]
                    act.activation(dst, src, ACT.Copy).then_inc(s_act, 1)

                elif kind == "conv":
                    if i >= 2:
                        act.wait_ge(s_taps, i - 1)
                    copy(f"conv{i}", m.pad[:, i % 2, CONV - 1:CONV - 1 + S], bank(f"conv{i}"))
                    if i:
                        tanh_half(qkvT[:, i - 1, :], f"conv{i - 1}", (s_taps, i))

                elif kind == "av_ab":
                    tanh_half(qkvT[:, 11, :], "conv11", (s_taps, 12))
                    copy("av", avr.rearrange("p t c -> p (t c)"), bank("av"))
                    copy("ab", sm[:, 32:64], bank("ab")[:, 0:32])

                elif kind == "log_decay":
                    act.wait_ge(*done("ab"))
                    act.activation(th4(tb), abr[:, :, 4:8], ACT.Tanh, scale=0.5).then_inc(s_ab, 1)
                    act.activation(ea[:, 0:4], alog, ACT.Exp).then_inc(s_ab, 1)
                    act.wait_ge(s_nabs, 1)
                    link(act.activation(lnp, nabs, ACT.Exp))
                    act.activation(lnp, lnp, ACT.Ln, bias=1.0).then_inc(s_ln1p, 1)
                    act.wait_ge(s_diff, 1)
                    act.activation(eg, gc[:, 0:16], ACT.Exp)
                    act.activation(ed, gdiff, ACT.Exp).then_inc(s_exps, 1)

                elif kind == "l2":
                    act.wait_ge(*used(f"conv{i}"))
                    square(qkvT[:, i, :], f"l2.{i}")
                    if i:
                        inv_root(f"l2.{i - 1}", f"l2{i - 1}", 0.25)
                    if i == 7:
                        inv_root("l2.7", "l27", 0.25)

                elif kind == "decay":
                    act.wait_ge(*done(f"gr{i}"))
                    act.activation(dec[:, i, :], dec[:, i, :], ACT.Exp).then_inc(s_dec, 1)

                elif kind == "solve_a":
                    lv, t = i
                    if lv == 0:
                        act.wait_ge(*done(f"qk{t}"))
                    elif lv == 1:
                        act.wait_ge(s_sol0, t + 1)
                    elif lv > 1:
                        act.wait_ge(*filled(f"yy{(lv - 1, t)}"))
                    copy(f"p{i}", dec[:, t, :], bank(f"p{i}"))

                elif kind == "w":
                    copy(f"w{i}", nwT[:, i, :], bank(f"w{i}"))

                elif kind == "qg":
                    at = TH_AT[f"qg{i}"]
                    act.wait_ge(*th_free(at))
                    act.wait_ge(*filled(f"gq{i}"))
                    act.activation(m.th[:, at % 2, :], bank(f"gq{i}"), ACT.Exp).then_inc(s_act, 1)

                elif kind == "state":
                    r = slice(CH * (i % 2), CH * (i % 2) + CH)
                    if i >= 2:
                        act.wait_ge(*filled(f"ds{i - 2}"))
                    copy(f"vn{i}", vnew[r, i % 2, :], bank(f"vn{i}")[r, :])
                    if i == 0:
                        act.wait_ge(*filled(f"w{T - 1}"))
                    copy(f"o{i}", oT[:, :, i * CH:(i + 1) * CH], bank(f"o{i}")[:, 0:NH * CH].rearrange("p (h c) -> p h c", h=NH))

                elif kind == "delta_out":
                    if i == 0:
                        act.wait_ge(*done(f"o{S // CH - 1}"))
                    square(oT[:, i, :], f"on{i}")
                    if i:
                        inv_root(f"on{i - 1}", f"delta_out{i - 1}", 1.0 / P)
                    if i == NH - 1:
                        inv_root(f"on{i}", f"delta_out{i}", 1.0 / P)

                elif kind == "c_norm":
                    inv_root(f"cn{i}", f"c_norm{i}", 1.0 / (2 * P if i == 0 else P))

                elif kind in ("qn", "kn", "cv"):
                    dst = {"qn": qnT, "kn": knT, "cv": cvr}[kind][:, i, :]
                    copy(f"{kind}{i}", dst, bank(f"{kind}{i}"))

                elif kind == "out":
                    for t in range(T):
                        copy(f"y{i}.{t}", y[:, t, i * WN:(i + 1) * WN], bank(f"y{i}.{t}")[:, 0:WN])

                elif kind == "residual":
                    act.wait_ge(*done(f"y3.{T - 1}"))
                    for t in range(T):
                        link(act.activation(junk, y[:, t, :], ACT.Square, accum_out=ss2[:, t:t + 1]))
                    link(act.activation(lg2, ss2, ACT.Ln, scale=1.0 / D, bias=eps))
                    act.activation(rs2, lg2, ACT.Exp, scale=-0.5).then_inc(s_y, 1)

        @block.vector
        def _(dve):
            chain = [0]

            def link(ins):
                chain[0] += 1
                ins.then_inc(s_dvec, 1)
                dve.wait_ge(s_dvec, chain[0])

            def th(name):
                at = TH_AT[name]
                if name.startswith("qg"):
                    dve.wait_ge(*done(f"gq{name[2:]}"))
                else:
                    dve.wait_ge(s_th, sum(not x.startswith("qg") for x, _ in TH[:at + 1]))
                return m.th[:, at % 2, :]

            def col(i):
                return m.pcol[:, i:i + 1]

            def over_free(cols, n=P):
                return cols.unsqueeze(2).to_broadcast([P, cols.shape[1], n])

            def silu2(j):
                dve.wait_ge(s_taps, j + 1)
                t = th(f"conv{j}")
                dve.scalar_tensor_tensor(out=qkvT[:, j, :], in0=t, scalar=1.0, in1=qkvT[:, j, :],
                                         op0=ALU.add, op1=ALU.mult).then_inc(s_thused, 1)

            def l2_scale(j):
                t = th(f"l2{j}")
                dve.scalar_tensor_tensor(out=qkvT[:, j, :], in0=qkvT[:, j, :], scalar=0.5 * (float(P) ** -0.5 if j < 4 else 1.0),
                                         in1=t, op0=ALU.mult, op1=ALU.mult).then_inc(s_thused, 1)

            def delta_gate(h):
                t = th(f"delta_out{h}")
                dve.scalar_tensor_tensor(out=oT[:, h, :], in0=oT[:, h, :], scalar=col(GDNN), in1=t,
                                         op0=ALU.mult, op1=ALU.mult).then_inc(s_thused, 1)
                dve.wait_ge(*used(f"delta_out{h}"))
                dve.wait_ge(*done(f"gate b_z.{h}"))
                dve.scalar_tensor_tensor(out=m.mix[:, 4 + h, :], in0=oT[:, h, :], scalar=0.5, in1=m.mix[:, 4 + h, :],
                                         op0=ALU.mult, op1=ALU.mult).then_inc(s_mixB, 1)

            for kind, i in STEPS:
                if kind == "params":
                    dve.wait_ge(s_rstd, 1)
                    for t in range(T):
                        dve.tensor_scalar(xs[:, t, :], m.x[:, t, :], rstd[:, t:t + 1], None, ALU.mult).then_inc(s_xs, 1)
                    dve.wait_ge(*done("params"))
                    dve.tensor_tensor(memg, m.memT[:, :, :], over_free(m.pcol[:, MEMN:MEMN + KD], MEM), ALU.mult).then_inc(s_memg, 1)

                elif kind == "xt":
                    for kk in range(2):
                        dve.wait_ge(*filled(f"xt{i}.{kk}"))
                        dve.tensor_tensor(m.hT[:, 4 * kk:4 * kk + 4, i * P:(i + 1) * P], heads(bank(f"xt{i}.{kk}")),
                                          over_free(m.pcol[:, PRE + 4 * kk:PRE + 4 * kk + 4]), ALU.mult).then_inc(s_dve, 1)

                elif kind == "gate":
                    t = th(f"gate {i}")
                    dve.scalar_tensor_tensor(out=m.mix[:, MIX_AT[i], :], in0=t, scalar=1.0, in1=bank(f"gate {i}"),
                                             op0=ALU.add, op1=ALU.mult).then_inc(s_dve, 1)

                elif kind == "scores":
                    group, a, c, _, _ = UNITS[i]
                    n, width = segments(i)
                    b = bank(f"scores{i}")[:, 0:n * width].rearrange("p (s k) -> p s k", s=n)
                    dve.wait_ge(*filled(f"scores{i}"))
                    if group != "A":
                        link(dve.tensor_reduce(stats(0, i), b, AX.X, ALU.max))
                        dve.tensor_scalar(stats(1, i), stats(0, i), -SCALE[group], None, ALU.mult).then_inc(s_neg, 1)
                    else:
                        s, jp = divmod(c, 2)
                        h0 = 4 * s + 2 * jp
                        p = prob[:, i % 2, 0:n * width].rearrange("p (s k) -> p s k", s=n)
                        dve.wait_ge(*filled(f"turn{i - 2}"))
                        dve.wait_ge(s_bias[a % 2], 16 * (a // 2 + 1))
                        dve.tensor_tensor(p, b, bias[:, a % 2, h0:h0 + 2, 2 * P - width:2 * P], ALU.add).then_inc(s_dve, 1)
                        dve.wait_ge(*done(f"scores{i}"))
                        link(dve.tensor_reduce(stats(0, i), p, AX.X, ALU.max))
                        link(dve.tensor_tensor(stats(0, i), stats(0, i), sink[:, h0:h0 + 2], ALU.max))
                        link(dve.tensor_scalar(stats(1, i), stats(0, i), -1.0, None, ALU.mult))
                        dve.tensor_tensor(stats(3, i), sink[:, h0:h0 + 2], stats(1, i), ALU.add).then_inc(s_neg, 1)

                elif kind == "norm":
                    n, width = segments(i)
                    if UNITS[i][0] == "A":
                        dve.wait_ge(s_expA, i - 24 + 1)
                        link(dve.tensor_tensor(stats(2, i), stats(2, i), stats(3, i), ALU.add))
                    else:
                        dve.wait_ge(*done(f"scores{i}"))
                    link(dve.reciprocal(stats(4, i), stats(2, i)))
                    for seg in range(n):
                        p = prob[:, i % 2, seg * width:(seg + 1) * width]
                        ins = dve.tensor_scalar(p, p, stats(4, i)[:, seg:seg + 1], None, ALU.mult)
                    ins.then_inc(s_norm, 1)

                elif kind == "pv":
                    group, a = GROUPS[i]
                    dve.wait_ge(*filled(f"pv{i}"))
                    if group == "A":
                        dve.wait_ge(*done("gate a_z.3"))
                        g = m.mix[:, 0:4, a * P:(a + 1) * P]
                        b = heads(bank(f"pv{i}"))
                    else:
                        z = "d_z" if group == "D" else "c_z"
                        dve.wait_ge(*done(f"gate {z}.{a}"))
                        g = m.mix[:, MIX_AT[f"{z}.{a}"], :]
                        b = bank(f"pv{i}")
                    dve.scalar_tensor_tensor(out=g, in0=b, scalar=0.5, in1=g, op0=ALU.mult, op1=ALU.mult).then_inc(s_dve, 1)

                elif kind == "conv":
                    dve.wait_ge(*done(f"conv{i}"))
                    p = m.pad[:, i % 2, :]
                    acc = qkvT[:, i, :]
                    if i == 0:
                        dve.wait_ge(*filled(f"pv{NH - 1}"))
                    link(dve.tensor_scalar(acc, p[:, 0:S], col(CONVW + i), None, ALU.mult))
                    for tap in range(1, CONV):
                        ins = dve.scalar_tensor_tensor(out=acc, in0=p[:, tap:tap + S], scalar=col(CONVW + 12 * tap + i),
                                                       in1=acc, op0=ALU.mult, op1=ALU.add)
                        if tap < CONV - 1:
                            link(ins)
                    ins.then_inc(s_taps, 1)
                    if i:
                        silu2(i - 1)

                elif kind == "av_ab":
                    silu2(11)

                elif kind == "log_decay":
                    dve.wait_ge(s_ab, 2)
                    dve.wait_ge(*done("ab"))
                    link(dve.tensor_scalar(beta, tb, 0.5, 0.5, ALU.mult, ALU.add))
                    link(dve.tensor_tensor(th4(xdt), abr[:, :, 0:4], dtb.unsqueeze(1).to_broadcast([P, T, NH]), ALU.add))
                    link(dve.tensor_scalar(mx, xdt, 0.0, None, ALU.max))
                    dve.scalar_tensor_tensor(out=nabs, in0=mx, scalar=-2.0, in1=xdt, op0=ALU.mult, op1=ALU.add).then_inc(s_nabs, 1)
                    dve.wait_ge(s_ln1p, 1)
                    link(dve.tensor_tensor(mx, mx, lnp, ALU.add))
                    dve.scalar_tensor_tensor(out=th4(g16), in0=th4(mx), scalar=-1.0,
                                             in1=ea[:, 0:4].unsqueeze(1).to_broadcast([P, T, NH]),
                                             op0=ALU.mult, op1=ALU.mult).then_inc(s_g, 1)
                    dve.wait_ge(*filled("cum"))
                    dve.tensor_copy(gc, bank("cum")[:, 0:32]).then_inc(s_dve, 1)
                    dve.wait_ge(*done("cum"))
                    dve.tensor_tensor(gdiff, gc[:, 16:32], gc[:, 0:16], ALU.subtract).then_inc(s_diff, 1)
                    link(dve.tensor_scalar(vbs, beta, 0.5, None, ALU.mult))
                    dve.wait_ge(s_exps, 1)
                    link(dve.scalar_tensor_tensor(out=nbeg, in0=beta, scalar=-1.0, in1=eg, op0=ALU.mult, op1=ALU.mult))

                elif kind == "l2":
                    if i:
                        l2_scale(i - 1)
                    if i == 7:
                        l2_scale(7)

                elif kind == "decay":
                    dve.wait_ge(*filled(f"gr{i}"))
                    for h in range(NH):
                        hc = slice(h * P, (h + 1) * P)
                        ins = dve.scalar_tensor_tensor(out=dec[:, i, hc], in0=bank(f"gr{i}")[:, hc],
                                                       scalar=gc[:, 4 * i + h:4 * i + h + 1], in1=m.const("decay_neg"),
                                                       op0=ALU.subtract, op1=ALU.add)
                    ins.then_inc(s_dve, 1)

                elif kind == "chunk_rows":
                    dve.wait_ge(*filled(f"krows{i}"))
                    k = heads(bank(f"krows{i}"))
                    c = slice(4 * i, 4 * i + 4)
                    dve.tensor_tensor(kbg[:, i, :, :], k, over_free(nbeg[:, c]), ALU.mult)
                    dve.tensor_tensor(kd[:, i, :, :], k, over_free(ed[:, c]), ALU.mult).then_inc(s_dve, 1)
                    dve.wait_ge(*filled(f"vrows{i}"))
                    dve.tensor_tensor(vb[:, i, :, :], heads(bank(f"vrows{i}")), over_free(vbs[:, c]), ALU.mult).then_inc(s_dve, 1)

                elif kind == "chunk_products":
                    dve.wait_ge(s_dec, i + 1)
                    dve.wait_ge(*filled(f"kk{i}"))
                    dve.tensor_tensor(LT[:, i, :], bank(f"kk{i}"), dec[:, i, :], ALU.mult).then_inc(s_dve, 1)
                    dve.wait_ge(*done(f"kk{i}"))
                    dve.wait_ge(*filled(f"br{i}"))
                    dve.tensor_tensor(LT[:, i, :], bank(f"br{i}"), LT[:, i, :], ALU.mult).then_inc(s_dve, 1)
                    dve.wait_ge(*filled(f"qk{i}"))
                    dve.tensor_tensor(Aqk[:, i, :], bank(f"qk{i}"), dec[:, i, :], ALU.mult).then_inc(s_dve, 1)

                elif kind == "solve_b":
                    lv, t = i
                    if lv == 0:
                        eye = m.const("ident").unsqueeze(1).to_broadcast([P, NH, P])
                        dve.wait_ge(s_bt, t + 1)
                        dve.wait_ge(*done(f"p{i}"))
                        dve.tensor_tensor(heads(Ym[:, t, :]), eye, heads(BT[:, t, :]), ALU.subtract)
                        dve.tensor_tensor(heads(Xm[:, t, :]), eye, heads(dec[:, t, :]), ALU.subtract).then_inc(s_sol0, 1)
                    else:
                        for name, dst in ((f"xx{i}", Xm), (f"yy{i}", Ym)):
                            if name in TASK_AT:
                                dve.wait_ge(*filled(name))
                                dve.tensor_tensor(dst[:, t, :], dst[:, t, :], bank(name), ALU.subtract).then_inc(s_dve, 1)

                elif kind == "qg":
                    t = heads(th(f"qg{i}"))
                    dve.tensor_copy(gle[:, i, :, :], t[:, :, CH - 1::CH])
                    q = qkvT[:, 0:4, i * P:(i + 1) * P]
                    dve.wait_ge(*done(f"qk{i}"))
                    dve.tensor_tensor(q, q, t, ALU.mult).then_inc(s_thused, 1)

                elif kind == "state":
                    if i < S // CH - 1:
                        new, old = state[:, (i + 1) % 2, :], state[:, i % 2, :]
                        if i:
                            if i >= 2:
                                dve.wait_ge(*filled(f"ds{i - 1}"))
                            dve.wait_ge(*done(f"ds{i - 1}"))
                            link(dve.tensor_tensor(heads(new), heads(old),
                                                   gle[:, i // 2, :, i % 2:i % 2 + 1].to_broadcast([P, NH, P]), ALU.mult))
                            dve.wait_ge(*filled(f"ds{i}"))
                            dve.tensor_tensor(new, new, bank(f"ds{i}"), ALU.add).then_inc(s_dve, 1)
                        else:
                            dve.wait_ge(*filled("ds0"))
                            dve.tensor_copy(new, bank("ds0")).then_inc(s_dve, 1)

                elif kind == "delta_out":
                    if i:
                        delta_gate(i - 1)
                    if i == NH - 1:
                        delta_gate(i)

                elif kind == "c_norm":
                    t = th(f"c_norm{i}")
                    if i == 0:
                        dve.scalar_tensor_tensor(out=cqT[:, 0, :], in0=craw[:, 0, :], scalar=col(CQN), in1=t,
                                                 op0=ALU.mult, op1=ALU.mult).then_inc(s_cq0, 1)
                        dve.scalar_tensor_tensor(out=cqT[:, 1, :], in0=craw[:, 1, :], scalar=col(CQN + 1), in1=t,
                                                 op0=ALU.mult, op1=ALU.mult).then_inc(s_thused, 1)
                    else:
                        dve.scalar_tensor_tensor(out=ckvT, in0=craw[:, 2, :], scalar=col(CKVN), in1=t,
                                                 op0=ALU.mult, op1=ALU.mult).then_inc(s_thused, 1)

                elif kind == "rope":
                    dst = krT if i == "k" else qrT[:, i, :]
                    dve.wait_ge(*filled(f"rope{i}"))
                    dve.tensor_tensor(dst, bank(f"rope{i}"), m.cosT[:, :], ALU.mult).then_inc(s_dve, 1)
                    dve.wait_ge(*filled(f"ropes{i}"))
                    dve.tensor_tensor(prob[:, 0, :], bank(f"ropes{i}"), m.sinT[:, :], ALU.mult).then_inc(s_dve, 1)
                    dve.wait_ge(*done(f"ropes{i}"))
                    dve.tensor_tensor(dst, dst, prob[:, 0, :], ALU.add).then_inc(s_rope, 1)
                    dve.wait_ge(s_rope, ["k", 0, 1].index(i) + 1)

                elif kind == "residual":
                    dve.wait_ge(s_y, 1)
                    dve.wait_ge(s_gpost, 16)
                    for t in range(T):
                        link(dve.scalar_tensor_tensor(out=y[:, t, :], in0=y[:, t, :], scalar=rs2[:, t:t + 1], in1=m.gpost[:, :],
                                                      op0=ALU.mult, op1=ALU.mult))
                        dve.tensor_tensor(m.x[:, t, :], m.x[:, t, :], y[:, t, :], ALU.add).then_inc(s_xfin, 1)


LAYER_SEMS = ["bank_filled", "freed_by_act", "freed_by_dve", "slot_in0", "slot_in1", "slot_in2", "slot_in3", "params_in", "uq_in",
              "bias_in0", "bias_in1", "gpost_in", "rstd_ready", "xs_ready", "memg_ready", "act_chain", "dve_chain", "neg_max_ready",
              "exp_ready", "prob_ready", "taps_done", "th_ready", "th_used", "squares_ready", "ab_ready", "nabs_ready",
              "ln1p_ready", "log_decay_ready", "decay_ready", "diff_ready", "exps_ready",
              "level_ready", "solve0_ready", "mix_delta_ready", "cq0_ready", "rope_ready", "x_ready", "y_rstd_ready"]


def program(nc, ins, out):
    with ExitStack() as ctx:
        m = Memory(nc, ctx)
        bias_dram = nc.dram_tensor("swa_bias", (T, P, SWA_H, 2 * P), F32, kind="Internal").ap()
        sems = [m._sem(n) for n in LAYER_SEMS]
        w = {n: ins[n] for n in ("norm_pre", "norm_post", "w_in", "attn_sinks", "gdn_conv_w", "gdn_a_log", "gdn_dt_bias",
                                 "gdn_norm", "mla_q_norm", "mla_kv_norm", "mla_w_uq", "mla_w_ukv", "mem_norm", "mem_w_kv", "w_out")}
        grouped = sems[0:3] + [sems[3:7]] + sems[7:9] + [sems[9:11]] + sems[11:]
        prologue(nc, m, ctx, (ins["x"], ins["mem"], ins["positions"], ins["rel_bias"], ins["consts"]), bias_dram)
        with nc.Fori(0, DEPTH) as l:
            layer(nc, m, l, w, bias_dram, grouped)
            with nc.Block() as block:
                @block.gpsimd
                def _(pool):
                    for s in sems:
                        pool.sem_clear(s)
        s_out = m._sem("out_written")
        with nc.Block() as block:
            @block.sync
            def _(sp):
                sp.dma_start(out[0].rearrange("(t p) d -> p t d", p=P), m.x[:, :, :]).then_inc(s_out, 16)
                sp.wait_ge(s_out, 16)


_INS = ["x", "mem", "positions", "rel_bias", "norm_pre", "norm_post", "w_in", "attn_sinks", "gdn_conv_w", "gdn_a_log",
        "gdn_dt_bias", "gdn_norm", "mla_q_norm", "mla_kv_norm", "mla_w_uq", "mla_w_ukv", "mem_norm", "mem_w_kv", "w_out"]


def kernel(**inputs):
    import numpy as _np
    import concourse.bacc as _bacc
    from concourse import mybir as _mybir
    from concourse.bass_utils import run_bass_kernel_spmd as _run

    nc = _bacc.Bacc("TRN2", target_bir_lowering=False, num_devices=1)
    arrays, args = {}, {}
    for name in _INS:
        a = _np.ascontiguousarray(inputs[name])
        arrays[f"in_{name}"] = a
        args[name] = nc.dram_tensor(f"in_{name}", a.shape, _mybir.dt.from_np(a.dtype), kind="ExternalInput").ap()
    arrays["in_consts"] = CONSTS
    args["consts"] = nc.dram_tensor("in_consts", CONSTS.shape, _mybir.dt.float32, kind="ExternalInput").ap()
    out = nc.dram_tensor("out", (1, S, D), _mybir.dt.float32, kind="ExternalOutput").ap()
    program(nc, args, out)
    r = _run(nc, [arrays], core_ids=[0])
    return r.results[0]["out"]
```

```python
from contextlib import ExitStack
import itertools
import math

import numpy as np
import concourse.bass as bass
from concourse import mybir

F32 = mybir.dt.float32
F32R = mybir.dt.float32r
BF16 = mybir.dt.bfloat16
I32 = mybir.dt.int32
ALU = mybir.AluOpType
ACT = mybir.ActivationFunctionType
AX = mybir.AxisListType

P = 128
S, D, DEPTH, MEM = 512, 1024, 2, 256
T = S // P
KD = D // P
GW = D // 2
NH = 4
SWA_H, SWA_D = 8, 64
NOPE, ROPE = 128, 64
BUCKETS, MAX_DIST = 32, 128
CH = 64
LEVELS = 6
EPS = 1e-6
NEG = -1e30
BANKS = 8
FB = 512
CONV = 4

OFF = {}
_at = 0
for _n, _w in (("a_q", 512), ("a_k", 128), ("a_v", 128), ("a_z", 512), ("b_q", 512), ("b_k", 512),
               ("b_v", 512), ("b_ab", 8), ("b_z", 512), ("c_q", 256), ("c_kv", 128), ("c_kr", 64),
               ("c_z", 512), ("d_q", 512), ("d_z", 512)):
    OFF[_n] = _at
    _at += _w
D_IN = _at

CONST_AT = {}


def constants():
    i = np.arange(P)
    same = (i[:, None] // CH) == (i[None, :] // CH)
    cols = []

    def put(name, a):
        CONST_AT[name] = (sum(c.shape[1] for c in cols), a.shape[1])
        cols.append(np.asarray(a, np.float32))

    put("ident", np.eye(P))
    put("ones", np.ones((P, P)))
    upto = same & (i[:, None] <= i[None, :])
    put("upto", upto)
    put("chunk", same)
    put("decay_neg", np.where(upto, 0.0, NEG))
    for lv in range(LEVELS):
        m = 1 << lv
        pair = (i[:, None] // (2 * m)) == (i[None, :] // (2 * m))
        put(f"level{lv}", pair & (i[:, None] % (2 * m) < m) & (i[None, :] % (2 * m) >= m))
    put("causal_neg", np.where(i[None, :] <= i[:, None], 0.0, NEG))
    inv_freq = np.float32(1.0) / np.power(np.float32(10000.0), np.arange(0, ROPE, 2, dtype=np.float32) / ROPE)
    put("inv_freq", inv_freq[i % 32][:, None])
    put("rope_sign", np.where(i % 64 < 32, -1.0, 1.0)[:, None])
    half = BUCKETS // 2
    least = [-1e30] + list(range(1, half)) + [
        math.ceil(half * (MAX_DIST / half) ** (j / half) - 1e-9) for j in range(half)]
    put("bucket_least", np.array(least, np.float64)[i % BUCKETS][:, None])
    put("eps", np.full((P, 1), EPS))
    return np.ascontiguousarray(np.concatenate(cols, 1))


CONSTS = constants()

WC = KD * P
RAW_SLOTS, SPLIT_SLOTS = 4, 2
OUT_K = list(range(12, 16)) + list(range(4, 8)) + list(range(8, 12)) + list(range(0, 4))
MIX_SLOTS = 4
GATES = [f"{g}.{j}" for g in ("d_z", "b_z", "c_z", "a_z") for j in range(4)]
MIX_AT = {f"{g}.{j}": 4 * n + j for n, g in enumerate(("a_z", "b_z", "c_z", "d_z")) for j in range(4)}

UNITS = [("D", h, tp, 2, MEM) for h in range(NH) for tp in range(2)]
for _i in range(T):
    for _j in range(T):
        UNITS += [("C", _i, _j, 1, P * (_j + 1)), ("A", _i, _j, 2, 2 * P if _i else P)]
GROUPS = [("D", h) for h in range(NH)] + [("C", h) for h in range(NH)] + [("A", blk) for blk in range(T)]
GROUP_OF = [GROUPS.index(u[:2]) for u in UNITS]
FIRST_UNIT = [GROUP_OF.index(g) for g in range(len(GROUPS))]
LAST_UNIT = [max(i for i, x in enumerate(GROUP_OF) if x == g) for g in range(len(GROUPS))]
A_UNITS = [i for i, u in enumerate(UNITS) if u[0] == "A"]
LN_EXP = "natural_log_exp_and_others"
SCALE = {"D": float(P) ** -0.5, "C": float(NOPE + ROPE) ** -0.5, "A": 1.0}


def attention(units, fillers=()):
    steps, fillers = [], list(fillers)
    n = len(units)
    for i in range(n + 4):
        if i < n:
            steps.append(("scores", units[i]))
        if 1 <= i <= n:
            steps.append(("norm", units[i - 1]))
        if fillers:
            steps.append(fillers.pop(0))
        if 2 <= i <= n + 1:
            steps.append(("turn", units[i - 2]))
        if i >= 4:
            u = units[i - 4]
            if u == LAST_UNIT[GROUP_OF[u]]:
                steps.append(("pv", GROUP_OF[u]))
    return steps + fillers


def mixed(*runs):
    return [x for row in itertools.zip_longest(*runs) for x in row if x is not None]


STEPS = [("params", 0)]
STEPS += mixed([("proj", f"mk.{h}") for h in range(NH)], [("xt", t) for t in range(T)])
STEPS += [("mv", c) for c in range(NH)] + [("h_split", 0)]
STEPS += [("proj", f"d_q.{h}") for h in range(NH)] + [("gate", f"d_z.{j}") for j in range(4)]
STEPS += attention(range(0, 8), [("conv", j) for j in range(12)])
STEPS += mixed([("l2", j) for j in range(8)], [("av", 0), ("av_turn", 0), ("ab", 0), ("ab_turn", 0)])
STEPS += [("log_decay", 0)]
STEPS += [("decay", t) for t in range(T)]
STEPS += [("chunk_rows", t) for t in range(T)]
STEPS += [("chunk_products", t) for t in range(T)]
for _lv in range(LEVELS):
    STEPS += [("solve_a", (_lv, t)) for t in range(T)] + [("solve_b", (_lv, t)) for t in range(T)]
STEPS += [("w", t) for t in range(T)] + [("qg", t) for t in range(T)]
for _n in range(S // CH):
    STEPS += [("state_v", _n), ("gate", f"{'bc'[_n // 4]}_z.{_n % 4}"), ("state_o", _n)]
STEPS += mixed([("proj", x) for x in ("c_q.0", "c_q.1", "ckv", "ak")], [("delta_out", h) for h in range(NH)])
STEPS += [("c_norm", 0), ("c_norm", 1), ("rope", "k")]
STEPS += [("qn", h) for h in range(NH)] + [("kn", h) for h in range(NH)] + [("cv", t) for t in range(T)]
STEPS += [("rope", 0), ("rope", 1)]
STEPS += [("proj", f"a_q.{j}") for j in range(4)] + [("gate", f"a_z.{j}") for j in range(4)]
STEPS += attention(range(8, 40))
STEPS += [("mix_split", n) for n in range(MIX_SLOTS)]
for _n in range(16):
    STEPS += [("out", _n)] + ([("mix_split", _n + MIX_SLOTS)] if _n + MIX_SLOTS < 16 else [])
STEPS += [("residual", 0)]

CHUNKS, CHUNK_USER = [], {}
for _s in STEPS:
    _kind, _i = _s
    for _c in {"proj": [_i], "gate": [_i], "mv": [f"mv.{_i}"], "av": ["av"], "ab": ["ab"], "out": [f"out.{_i}"],
               "rope": ["kr", "krs"] if _i == "k" else [],
               "conv": [f"b_{'qkv'[_i // 4 % 3]}.{_i % 4}"] if _kind == "conv" else []}.get(_kind, []):
        CHUNKS.append(_c)
        CHUNK_USER[_c] = _s


def tasks_of(step):
    kind, i = step
    return {
        "params": lambda: [("params", "A")],
        "xt": lambda: [(f"xt{i}.{kk}", "V") for kk in range(2)],
        "proj": lambda: [(f"proj {i}", "A")],
        "mv": lambda: [(f"mv{mt}", "A") for mt in range(2)] if i == 3 else [],
        "gate": lambda: [(f"gate {i}", "V")],
        "scores": lambda: [(f"scores{i}", "V" if UNITS[i][0] == "A" else "A")],
        "turn": lambda: [(f"turn{i}", "A")],
        "pv": lambda: [(f"pv{i}", "V")],
        "conv": lambda: [(f"conv{i}", "A")],
        "av": lambda: [("avT", "A")],
        "av_turn": lambda: [("av", "A")],
        "ab": lambda: [("abT", "A")],
        "ab_turn": lambda: [("ab", "A")],
        "log_decay": lambda: [("cum", "V")],
        "l2": lambda: [(f"l2.{i}", "A")],
        "decay": lambda: [(f"gr{i}", "V")],
        "chunk_rows": lambda: [(f"krows{i}", "V"), (f"vrows{i}", "V")],
        "chunk_products": lambda: [(f"kk{i}", "V"), (f"br{i}", "V"), (f"qk{i}", "V")],
        "solve_a": lambda: [(f"p{i}", "A")],
        "solve_b": lambda: ([(f"xx{i}", "V")] if 0 < i[0] < LEVELS - 1 else []) + ([(f"yy{i}", "V")] if i[0] else []),
        "w": lambda: [(f"w{i}", "A")],
        "qg": lambda: [(f"gq{i}", "A")],
        "state_v": lambda: [(f"vn{i}", "A")],
        "state_o": lambda: ([(f"ds{i}", "V")] if i != S // CH - 1 else []) + [(f"o{i}", "A")],
        "delta_out": lambda: [(f"on{i}", "A")],
        "c_norm": lambda: [(f"cn{i}", "A")],
        "rope": lambda: [(f"rope{i}", "V"), (f"ropes{i}", "V")],
        "qn": lambda: [(f"qn{i}", "A")],
        "kn": lambda: [(f"kn{i}", "A")],
        "cv": lambda: [(f"cv{i}", "A")],
        "out": lambda: [(f"y{t}.{n}", "V") for t in range(T) for n in range(2)] if i == 15 else [],
    }.get(kind, list)()


TASKS = [t for s in STEPS for t in tasks_of(s)]
TASK_AT = {name: i for i, (name, _) in enumerate(TASKS)}
assert len(TASK_AT) == len(TASKS)


PARTIAL = [s for s in STEPS if s in [("mv", c) for c in range(3)] + [("out", n) for n in range(15)]]


def nth(kind, i):
    return [x for k, x in STEPS if k == kind].index(i) + 1


def frees_of(step):
    kind, i = step
    lag = {"l2": ("l2.", 8), "delta_out": ("on", NH)}.get(kind)
    if lag is None:
        return tasks_of(step)
    return [(f"{lag[0]}{j}", "A") for j in ([i - 1] if i else []) + ([i] if i == lag[1] - 1 else [])]


FREES = [t for s in STEPS for t in frees_of(s)]
FREED_AT = {name: i for i, (name, _) in enumerate(FREES)}
assert len(FREED_AT) == len(TASKS)


def freed(i):
    name, who = TASKS[i]
    return who, sum(w == who for _, w in FREES[:FREED_AT[name] + 1])


def th_uses():
    uses = []
    for kind, i in STEPS:
        if kind == "gate":
            uses.append((f"gate {i}", "bank"))
        elif kind == "conv":
            if i:
                uses.append((f"conv{i - 1}", "th"))
            if i == 11:
                uses.append(("conv11", "th"))
        elif kind in ("l2", "qg", "delta_out", "c_norm"):
            uses.append((f"{kind}{i}", "th"))
    return uses


TH = th_uses()
TH_AT = {name: i for i, (name, _) in enumerate(TH)}


def sq_uses():
    uses = []
    for kind, i in STEPS:
        if kind == "l2":
            uses.append((f"l2.{i}", f"l2.{i}"))
        elif kind == "delta_out":
            uses.append((f"on{i}", f"on{i}"))
        elif kind == "c_norm":
            uses += [("cq0", "cn0"), ("cq1", "cn0")] if i == 0 else [("ckv", "cn1")]
    return uses


SQ = sq_uses()
SQ_AT = {name: i for i, (name, _) in enumerate(SQ)}

N_PARAM_ROWS = KD + KD + 2 + 1 + 1 + 12 * CONV
PRE, MEMN, CQN, CKVN, GDNN, CONVW = 0, KD, 2 * KD, 2 * KD + 2, 2 * KD + 3, 2 * KD + 4


class Memory:

    def __init__(self, nc, ctx):
        def sb(name, shape, dt=F32):
            return ctx.enter_context(nc.sbuf_tensor(name, shape, dt))

        self.consts = sb("consts", [P, CONSTS.shape[1]])
        self.x = sb("x_rows", [P, T, D])
        self.h_hi = sb("h_hi", [P, KD, S], F32R)
        self.h_lo = sb("h_lo", [P, KD, S], F32R)
        self.w_raw = sb("w_raw", [P, RAW_SLOTS, WC])
        self.w_hi = sb("w_hi", [P, SPLIT_SLOTS, WC], F32R)
        self.w_lo = sb("w_lo", [P, SPLIT_SLOTS, WC], F32R)
        self.mix = sb("mix", [P, 16, S])
        self.cosT = sb("cosT", [P, S])
        self.sinT = sb("sinT", [P, S])
        self.pad = sb("pad", [P, 2, S + 4])
        self.th = sb("th", [P, 2, S])
        self.sq = sb("sq", [P, 2, S])
        self.prow = sb("param_rows", [N_PARAM_ROWS, P])
        self.pcol = sb("param_cols", [P, N_PARAM_ROWS])
        self.stat = sb("stat", [P, 5, 2 * len(UNITS)])
        self.small = sb("small", [P, 352])
        self.arena = sb("arena", [P, 17920])
        self.ps = ctx.enter_context(nc.psum_tensor("ps", [P, BANKS, FB], F32))
        self._sem = lambda name: ctx.enter_context(nc.semaphore(name))

    def view(self, at, *shape):
        n = int(np.prod(shape))
        v = self.arena[:, at:at + n]
        if len(shape) == 2:
            v = v.rearrange("p (a b) -> p a b", b=shape[1])
        elif len(shape) == 3:
            v = v.rearrange("p (a b c) -> p a b c", b=shape[1], c=shape[2])
        return v

    def const(self, name):
        at, n = CONST_AT[name]
        return self.consts[:, at:at + n]


def heads(ap):
    return ap.rearrange("p (h c) -> p h c", h=NH)


def prologue(nc, m, ctx, args, bias_dram, mem_dram):
    x, mem, positions, rel_bias, consts = args
    sem = m._sem
    s_const, s_x, s_mem, s_pos, s_rb, s_bias_out = (sem(n) for n in (
        "const_in", "x_in", "mem_in", "pos_in", "rb_in", "bias_out"))
    s_chain, s_stat, s_mact, s_xs, s_steps, s_fill, s_free, s_trig, s_tab, s_sel, s_delta, s_zero, s_posf = (sem(n) for n in (
        "pro_chain", "mem_sums", "mem_rstd", "mem_scaled", "steps_ready", "pro_filled", "pro_freed",
        "angles_ready", "trig_ready", "masked", "delta_ready", "rb_zero", "posf_ready"))

    SLAB = 64
    PER = 16
    steps = [m.arena[:, 4096 * b:4096 * (b + 1)].bitcast(BF16).rearrange("p (k q) -> p k q", q=P) for b in range(2)]
    stage = m.view(8192, 7, 8, P)
    memr = m.view(8192 + 7168, 2, D)
    hs = m.mix[:, 0:8, :].rearrange("p k s -> p (k s)")
    memT = m.mix[:, 8:12, :].rearrange("p k s -> p (k s)").rearrange("p (k c) -> p k c", k=KD)
    posi = hs[:, 0:512].bitcast(I32)
    posf = hs[:, 512:1024]
    wini = hs[:, 1024:1280].bitcast(I32)
    winf = hs[:, 1280:1536]
    ang, kk, red = hs[:, 1536:2048], hs[:, 2048:2560], hs[:, 2560:3072]
    ang2 = hs[:, 3072:3584]
    rb, rbp, dl, r1, r2 = (hs[:, 3584 + 8 * i:3592 + 8 * i] for i in range(5))
    parts = hs[:, 3640:3652].bitcast(BF16)
    junk = m.w_raw[:, 0, :]
    ss, lg, rs = m.small[:, 0:2], m.small[:, 2:4], m.small[:, 4:6]

    tasks = [("mem", mt, kh) for mt in range(2) for kh in range(2)]
    first = len(tasks)
    tasks += [("bias", sl, g, part) for sl in range(4) for g in range(1 if sl < 2 else 0, 4) for part in range(SLAB // PER)]

    with nc.Block() as block:
        @block.sync
        def _(sp):
            sp.dma_start(m.consts[:, :], consts[:, :]).then_inc(s_const, 16)
            sp.dma_start(memr, mem[0].rearrange("(t p) d -> p t d", p=P)).then_inc(s_mem, 16)
            sp.dma_start(posi, positions[0:1, :].partition_broadcast(P).rearrange("p a s -> p (a s)")).then_inc(s_pos, 16)
            for g in range(4):
                lo = max(g - 1, 0) * P
                w = P if g == 0 else 2 * P
                sp.dma_start(wini[32 * g:32 * g + 32, 2 * P - w:2 * P],
                             positions[0:1, lo:lo + w].partition_broadcast(32).rearrange("p a s -> p (a s)")).then_inc(s_pos, 16)
            sp.wait_ge(s_zero, 2)
            for g in range(4):
                sp.dma_start(rb[32 * g:32 * g + 32, :], rel_bias[:, :]).then_inc(s_rb, 16)
                sp.dma_start(rbp[32 * g + 1:32 * g + 32, :], rel_bias[0:BUCKETS - 1, :]).then_inc(s_rb, 16)
            sp.dma_start(m.x[:, :, :], x[0].rearrange("(t p) d -> p t d", p=P)).then_inc(s_x, 16)
            sp.wait_ge(s_x, 16)
            sp.wait_ge(s_free, first)
            sp.dma_start(mem_dram[:, :, :], memT).then_inc(s_x, 16)
            sp.wait_ge(s_x, 32)

        @block.gpsimd
        def _(pool):
            pool.memset(rbp, 0.0).then_inc(s_zero, 1)
            pool.memset(m.pad[:, :, 0:CONV - 1], 0.0).then_inc(s_zero, 1)
            last = {}
            for i, (_, sl, g, part) in enumerate(tasks[first:]):
                last[(sl // 2, g)] = i
            n = 0
            for half in range(2):
                for g in range(1 - half, 4):
                    pool.wait_ge(s_free, first + last[(half, g)] + 1)
                    v = stage[:, 2 * g + half - 1, :, :]
                    if half == 0:
                        pool.affine_select(out=v, in_=v, pattern=[[0, 8], [1, P]], compare_op=ALU.is_gt, fill=NEG,
                                           base=0, channel_multiplier=-1).then_inc(s_sel, 1)
                    else:
                        pool.affine_select(out=v, in_=v, pattern=[[0, 8], [-1, P]], compare_op=ALU.is_ge, fill=NEG,
                                           base=0, channel_multiplier=1).then_inc(s_sel, 1)
                    n += 1
                    pool.wait_ge(s_sel, n)
                    pool.dma_start(bias_dram[g, :, :, half * P:(half + 1) * P], v).then_inc(s_bias_out, 16)
            pool.wait_ge(s_bias_out, 16 * n)

        @block.scalar
        def _(act):
            act.wait_ge(s_mem, 16)
            for t in range(2):
                act.activation(junk, memr[:, t, :], ACT.Square, accum_out=ss[:, t:t + 1]).then_inc(s_stat, 1)
                act.wait_ge(s_stat, t + 1)
            act.wait_ge(s_const, 16)
            act.activation(lg, ss, ACT.Ln, scale=1.0 / D, bias=m.const("eps")).then_inc(s_stat, 1)
            act.wait_ge(s_stat, 3)
            act.activation(rs, lg, ACT.Exp, scale=-0.5).then_inc(s_mact, 1)
            act.wait_ge(s_trig, 1)
            act.activation(m.cosT[:, :], ang2, ACT.Sin).then_inc(s_tab, 1)
            act.wait_ge(s_trig, 2)
            act.activation(m.sinT[:, :], ang, ACT.Sin).then_inc(s_tab, 1)

        @block.vector
        def _(dve):
            chain = [0]

            def link(ins):
                chain[0] += 1
                ins.then_inc(s_chain, 1)
                dve.wait_ge(s_chain, chain[0])

            dve.wait_ge(s_pos, 80)
            dve.wait_ge(s_const, 16)
            link(dve.tensor_copy(winf[:, P:2 * P], wini[:, P:2 * P]))
            for g in range(1, 4):
                link(dve.tensor_copy(winf[32 * g:32 * g + 32, 0:P], wini[32 * g:32 * g + 32, 0:P]))
            dve.wait_ge(s_rb, 128)
            link(dve.tensor_tensor(dl, rb, rbp, ALU.subtract))
            link(dve.tensor_copy(parts[:, 0:8], dl))
            link(dve.tensor_tensor(r1, dl, parts[:, 0:8], ALU.subtract))
            link(dve.tensor_copy(parts[:, 8:16], r1))
            link(dve.tensor_tensor(r2, r1, parts[:, 8:16], ALU.subtract))
            dve.tensor_copy(parts[:, 16:24], r2).then_inc(s_delta, 1)

            def make_steps(sl):
                if sl >= 2:
                    done = [i for i, t in enumerate(tasks) if t[:2] == ("bias", sl - 2)]
                    dve.wait_ge(s_fill, done[-1] + 1)
                lo = 32 if sl < 2 else 0
                for a in ((32, 64), (64, 128)) if lo else ((0, 128),):
                    ins = dve.scalar_tensor_tensor(
                        out=steps[sl % 2][a[0]:a[1], :, :],
                        in0=winf[a[0]:a[1], SLAB * sl:SLAB * (sl + 1)].unsqueeze(2).to_broadcast([a[1] - a[0], SLAB, P]),
                        scalar=m.const("bucket_least")[a[0]:a[1], :],
                        in1=winf[a[0]:a[1], P:2 * P].unsqueeze(1).to_broadcast([a[1] - a[0], SLAB, P]),
                        op0=ALU.add, op1=ALU.is_le)
                ins.then_inc(s_steps, 1)

            make_steps(0)
            link(dve.tensor_copy(posf, posi))
            link(dve.tensor_scalar(red, posf, m.const("inv_freq"), None, ALU.mult))
            magic = float(1.5 * 2 ** 23)
            c1 = 6.28125
            c2 = float((np.array(np.float32(2 * math.pi - c1)).view(np.int32) & np.int32(-4096)).view(np.float32))
            c3 = float(np.float32(2 * math.pi - c1 - c2))
            for i, (dst, turn) in enumerate(((ang2, 0.25), (ang, 0.0))):
                link(dve.tensor_scalar(kk, red, float(1 / (2 * math.pi)), turn, ALU.mult, ALU.add))
                link(dve.tensor_scalar(kk, kk, magic, None, ALU.add))
                link(dve.tensor_scalar(kk, kk, magic, None, ALU.subtract))
                link(dve.scalar_tensor_tensor(out=dst, in0=kk, scalar=-c1, in1=red, op0=ALU.mult, op1=ALU.add))
                link(dve.scalar_tensor_tensor(out=dst, in0=kk, scalar=-c2, in1=dst, op0=ALU.mult, op1=ALU.add))
                link(dve.scalar_tensor_tensor(out=dst, in0=kk, scalar=-c3, in1=dst, op0=ALU.mult, op1=ALU.add))
                link(dve.tensor_scalar(dst, dst, turn * 2 * math.pi, 3.1415925, ALU.add, ALU.min))
                dve.tensor_scalar(dst, dst, -3.1415925, None, ALU.max).then_inc(s_trig, 1)
            dve.wait_ge(s_tab, 2)
            link(dve.tensor_scalar(m.sinT[:, :], m.sinT[:, :], m.const("rope_sign"), None, ALU.mult))
            dve.wait_ge(s_mact, 1)
            for t in range(2):
                dve.tensor_scalar(memr[:, t, :], memr[:, t, :], rs[:, t:t + 1], None, ALU.mult).then_inc(s_xs, 1)
            made = 1
            for i, task in enumerate(tasks):
                bank = m.ps[:, i % BANKS, :]
                if task[0] == "mem":
                    _, mt, kh = task
                    dve.wait_ge(s_fill, i + 1)
                    dve.tensor_copy(memT[:, 4 * kh:4 * kh + 4, mt * P:(mt + 1) * P],
                                    bank.rearrange("p (k c) -> p k c", k=4)).then_inc(s_free, 1)
                    continue
                _, sl, g, part = task
                if made == sl + 1 and made < 4:
                    make_steps(made)
                    made += 1
                dve.wait_ge(s_fill, i + 1)
                k0 = (sl % 2) * SLAB + part * PER
                dve.tensor_reduce(stage[:, 2 * g + sl // 2 - 1, :, k0:k0 + PER].rearrange("p h k -> p k h"),
                                  bank[:, 0:PER * 24].rearrange("p (k s h) -> p k h s", s=3, h=8),
                                  AX.X, ALU.add).then_inc(s_free, 1)

        @block.tensor
        def _(pe):
            pe.wait_ge(s_const, 16)
            for i, task in enumerate(tasks):
                bank = m.ps[:, i % BANKS, :]
                if i >= BANKS:
                    pe.wait_ge(s_free, i - BANKS + 1)
                if task[0] == "mem":
                    _, mt, kh = task
                    pe.wait_ge(s_xs, mt + 1)
                    for k in range(4):
                        last = pe.transpose(bank[:, k * P:(k + 1) * P], memr[:, mt, (4 * kh + k) * P:(4 * kh + k + 1) * P],
                                            m.const("ident"))
                    last.then_inc(s_fill, 1)
                    continue
                _, sl, g, part = task
                if i == first:
                    pe.wait_ge(s_delta, 1)
                pe.wait_ge(s_steps, sl + 1)
                for k in range(PER):
                    last = pe.matmul(bank[:, 24 * k:24 * (k + 1)], steps[sl % 2][32 * g:32 * g + 32, part * PER + k, :],
                                     parts[32 * g:32 * g + 32, 0:24], start=True, stop=True)
                last.then_inc(s_fill, 1)


def layer(nc, m, l, w, bias_dram, mem_dram, layer_sems):
    (s_fill, s_act, s_dve, s_slot, s_hi, s_split, s_part, s_par, s_mem, s_uq, s_bias, s_gpost, s_rstd, s_xs,
     s_mhi, s_mlo, s_mfull, s_hhi, s_hlo, s_xhi, s_xlo, s_actc, s_dvec, s_neg, s_expA,
     s_norm, s_taps, s_th, s_thused, s_sq, s_ab, s_nabs, s_ln1p, s_g, s_dec, s_diff, s_exps,
     s_bt, s_sol0, s_mixB, s_cq0, s_rope, s_xfin, s_ysum, s_yadd, s_y) = layer_sems

    xs = m.view(0, T, D)
    junk = m.arena[:, 4096:5120]
    memT = m.view(5120, KD, MEM)
    mem_hi, mem_lo = (m.h_lo[:, 4 * i:4 * i + 4, :].rearrange("p k s -> p (k s)").rearrange("p (k c) -> p k c", k=KD)
                      for i in range(2))
    hf = m.view(13824, KD, S)
    mkT = m.view(7168, NH, MEM)
    mvr = m.view(8192, 2, GW)
    dqT = m.view(9216, NH, S)
    ptD = m.view(11264, 2, 2, S)
    qkvT = m.view(0, 12, S)
    kbg, kd, vb = (m.view(6144 + 2048 * i, T, NH, P) for i in range(3))
    LT = m.view(12288, T, NH * P)
    BT = m.view(14336, T, NH * P)
    state = m.view(16384, 2, NH * P)
    avr = m.view(17408, T, P)
    turning = {"av": m.arena[:, 16384:16896], "ab": m.arena[:, 16896:17408]}
    vnew = m.sq
    Xm, Ym = qkvT[:, 8:12, :], qkvT[:, 4:8, :]
    nwT = LT
    oT = kbg.rearrange("p t h c -> p t (h c)")
    Aqk = m.mix[:, 0:4, :]
    dec = m.mix[:, 8:12, :]
    cqT, ckvT = m.view(0, 2, S), m.arena[:, 1024:1536]
    qnT, qrT, knT = m.view(1536, NH, S), m.view(3584, 2, S), m.view(4608, NH, S)
    krT = m.arena[:, 6656:7168]
    cvr = m.view(7168, T, GW)
    pt = m.view(9216, 2, 4, S)
    craw = m.view(9216, 3, S)
    uqs = m.view(13312, 2, 2, P)
    uqr = m.mix[:, 3, :].rearrange("p (k b c) -> p k b c", k=2, b=2)
    ukv = m.arena[:, 13824:14848].rearrange("p (h c) -> p h c", h=NH)
    aqT, akT = m.view(14848, NH, S), m.arena[:, 16896:17408]
    uq = m.mix[:, 0:3, :].rearrange("p k s -> p (k s)").rearrange("p (k c) -> p k c", k=2)
    bias = m.h_lo[:, :, :].rearrange("p k s -> p (k s)").bitcast(F32).rearrange("p (b h c) -> p b h c", b=2, h=8)
    gpost = m.arena[:, 5120:6144]
    ytmp = m.view(0, 2, S)
    prob_d, prob_ca = m.view(13312, 2, S), m.pad[:, :, CONV - 1:CONV - 1 + S]

    sm = m.small
    ss, lg, rstd = sm[:, 0:4], sm[:, 4:8], sm[:, 8:12]
    alog, dtb, sink = sm[:, 12:16], sm[:, 16:20], sm[:, 20:28]
    abr = sm[:, 32:64].rearrange("p (t c) -> p t c", t=T)
    tb, beta, xdt, mx, nabs, lnp, g16, ea = (sm[:, 64 + 16 * i:80 + 16 * i] for i in range(8))
    gc = sm[:, 192:224]
    gdiff, eg, ed, nbeg, vbs = (sm[:, 224 + 16 * i:240 + 16 * i] for i in range(5))
    gle = sm[:, 304:336].rearrange("p (t h c) -> p t h c", t=T, h=NH)
    ss2, lg2, rs2 = sm[:, 336:344], sm[:, 344:348], sm[:, 348:352]

    def th4(ap):
        return ap.rearrange("p (t h) -> p t h", t=T)

    def weights(name):
        return w[name][bass.ds(l, 1)]

    def done(name):
        who, n = freed(TASK_AT[name])
        return (s_act if who == "A" else s_dve), n

    def filled(name):
        return s_fill, TASK_AT[name] + 1

    def th_free(i):
        name, by = TH[i - 2]
        return done(name) if by == "bank" else used(name)

    def used(name):
        return s_thused, sum(by == "th" for _, by in TH[:TH_AT[name] + 1])

    def bank(name):
        return m.ps[:, TASK_AT[name] % BANKS, :]

    def segments(u):
        _, _, _, n, width = UNITS[u]
        return n, width

    def stats(row, u):
        return m.stat[:, row, 2 * u:2 * u + UNITS[u][3]]

    def mix_ready(n):
        k = OUT_K[n]
        if 4 <= k < 8:
            return s_mixB, k - 3
        return done({0: f"pv{len(GROUPS) - 1}", 2: f"pv{k - 4}", 3: f"pv{k - 12}"}[k // 4])

    def prob_of(u):
        return (prob_d if UNITS[u][0] == "D" else prob_ca)[:, u % 2, :]

    def user_done(chunk):
        step = CHUNK_USER[chunk]
        if step in PARTIAL:
            return s_part, PARTIAL.index(step) + 1
        name = {"kr": "ropek", "krs": "ropesk"}.get(chunk) or tasks_of(step)[-1][0]
        return filled(name)

    def pieces(name, slot):
        group, j = (name.split(".") + ["0"])[:2]
        j = int(j)
        n = 8 if name == "ab" else P
        grid = slot[:, 0:KD * n].rearrange("p (k c) -> p k c", k=KD)

        def cols(c0, n, at, src="w_in"):
            return grid[:, :, at:at + n], weights(src)[:, :, c0:c0 + n].rearrange("a (k p) c -> p (a k) c", p=P)

        if group == "mk":
            return [cols(j * P, P, 0, "mem_w_kv")]
        if group == "mv":
            return [(slot.rearrange("p (k c) -> p k c", k=2),
                     weights("mem_w_kv")[:, 2 * j * P:2 * (j + 1) * P, GW:2 * GW].rearrange("a (k p) c -> p (a k) c", p=P))]
        if group == "ckv":
            return [cols(OFF["c_kv"], P, 0)]
        if group == "kr":
            return [cols(OFF["c_kr"], ROPE, ROPE * i) for i in range(2)]
        if group == "krs":
            return [cols(OFF["c_kr"] + 32 * (1 - i % 2), 32, 32 * i) for i in range(4)]
        if group in ("ak", "av", "ab"):
            return [cols(OFF[{"ak": "a_k", "av": "a_v", "ab": "b_ab"}[group]], n, 0)]
        if group in ("a_q", "a_z"):
            return [cols(OFF[group] + 256 * half + 64 * j, 64, 64 * half) for half in range(2)]
        if group == "out":
            k = OUT_K[j]
            if k < 4:
                return [(slot[64 * half:64 * half + 64, :],
                         weights("w_out")[:, 256 * half + 64 * k:256 * half + 64 * k + 64, :].rearrange("a p c -> (a p) c"))
                        for half in range(2)]
            return [(slot, weights("w_out")[:, k * P:(k + 1) * P, :].rearrange("a p c -> (a p) c"))]
        return [cols(OFF[group] + j * P, P, 0)]

    n_pieces = [len(pieces(c, m.w_raw[:, 0, :])) for c in CHUNKS]

    def arrived(i):
        return s_slot[i % RAW_SLOTS], 16 * sum(n_pieces[i % RAW_SLOTS:i + 1:RAW_SLOTS])

    def slots(i):
        n = KD * 8 if CHUNKS[i] == "ab" else WC
        return m.w_raw[:, i % RAW_SLOTS, 0:n], m.w_hi[:, i % SPLIT_SLOTS, 0:n], m.w_lo[:, i % SPLIT_SLOTS, 0:n]

    def chunks_behind(step):
        return [i + SPLIT_SLOTS for i, c in enumerate(CHUNKS) if CHUNK_USER[c] == step and i + SPLIT_SLOTS < len(CHUNKS)]

    def w_parts(chunk):
        i, n = CHUNKS.index(chunk), 8 if chunk == "ab" else P
        return [x[:, i % SPLIT_SLOTS, 0:KD * n].rearrange("p (k c) -> p k c", k=KD) for x in (m.w_hi, m.w_lo)]

    with nc.Block() as block:
        @block.sync
        def _(sp):
            r = m.prow
            sp.dma_start(memT, mem_dram[:, :, :]).then_inc(s_mem, 16)
            rows = [("norm_pre", PRE, KD), ("mem_norm", MEMN, KD), ("mla_q_norm", CQN, 2), ("mla_kv_norm", CKVN, 1),
                    ("gdn_norm", GDNN, 1)]
            for name, at, n in rows:
                sp.dma_start(r[at:at + n, :], weights(name).rearrange("a (k p) -> (a k) p", p=P)).then_inc(s_par, 16)
            sp.dma_start(r[CONVW:CONVW + 12 * CONV, :],
                         weights("gdn_conv_w").rearrange("a t (j p) -> (a t j) p", p=P)).then_inc(s_par, 16)
            for dst, name in ((alog, "gdn_a_log"), (dtb, "gdn_dt_bias"), (sink, "attn_sinks")):
                sp.dma_start(dst, weights(name).partition_broadcast(P).rearrange("p a c -> p (a c)")).then_inc(s_par, 16)
            for i, chunk in enumerate(CHUNKS):
                if i >= RAW_SLOTS:
                    sp.wait_ge(s_split, i - RAW_SLOTS + 1)
                for dst, src in pieces(chunk, m.w_raw[:, i % RAW_SLOTS, :]):
                    sp.dma_start(dst, src).then_inc(s_slot[i % RAW_SLOTS], 16)

        @block.gpsimd
        def _(pool):
            def rest(i):
                raw, hi, lo = slots(i)
                pool.wait_ge(s_hi, i + 1)
                pool.tensor_tensor(lo, raw, hi, ALU.subtract).then_inc(s_split, 1)

            for i in range(SPLIT_SLOTS):
                rest(i)
            for kind, i in STEPS:
                for c in chunks_behind((kind, i)):
                    rest(c)
                if kind == "solve_a":
                    lv, t = i
                    pool.wait_ge(*done(f"br{t}"))
                    if lv:
                        pool.wait_ge(*filled(f"p{(lv - 1, t)}"))
                    if lv == 1:
                        pool.wait_ge(s_sol0, t + 1)
                    pool.tensor_tensor(heads(BT[:, t, :]), heads(LT[:, t, :]),
                                       m.const(f"level{lv}").unsqueeze(1).to_broadcast([P, NH, P]), ALU.mult).then_inc(s_bt, 1)

        @block.tensor
        def _(pe):
            ident, ones = m.const("ident"), m.const("ones")

            def open_bank(name):
                i = TASK_AT[name]
                if i >= BANKS:
                    who, n = freed(i - BANKS)
                    pe.wait_ge(s_act if who == "A" else s_dve, n)
                return bank(name)

            def passes(chunk, other_hi, other_lo, before_lo=None):
                hi, lo = w_parts(chunk)
                pe.wait_ge(s_split, CHUNKS.index(chunk) + 1)
                yield hi, other_hi
                yield lo, other_hi
                if before_lo:
                    pe.wait_ge(*before_lo)
                yield hi, other_lo

            def project(out, chunk, rhs_hi, rhs_lo, before_lo=None):
                n = 0
                for wt, rhs in passes(chunk, rhs_hi, rhs_lo, before_lo):
                    for k in range(KD):
                        last = pe.matmul(out, wt[:, k, :], rhs[:, k, :], start=(n == 0), stop=(n == 3 * KD - 1))
                        n += 1
                return last

            for kind, i in STEPS:
                if kind == "params":
                    b = open_bank("params")
                    pe.wait_ge(s_par, 9 * 16)
                    pe.transpose(b[:, 0:N_PARAM_ROWS], m.prow[:, :], ident[0:N_PARAM_ROWS, 0:N_PARAM_ROWS]).then_inc(s_fill, 1)

                elif kind == "xt":
                    pe.wait_ge(s_xs, i + 1)
                    for kk in range(2):
                        b = open_bank(f"xt{i}.{kk}")
                        for k in range(4):
                            last = pe.transpose(b[:, k * P:(k + 1) * P], xs[:, i, (4 * kk + k) * P:(4 * kk + k + 1) * P], ident)
                        last.then_inc(s_fill, 1)

                elif kind in ("proj", "gate", "conv"):
                    chunk = f"b_{'qkv'[i // 4]}.{i % 4}" if kind == "conv" else i
                    b = open_bank(f"conv{i}" if kind == "conv" else f"{kind} {i}")
                    if chunk.startswith("mk"):
                        pe.wait_ge(s_mhi, 1)
                        project(b[:, 0:MEM], chunk, mem_hi, mem_lo, (s_mlo, 1)).then_inc(s_fill, 1)
                    else:
                        pe.wait_ge(s_hhi, T)
                        project(b, chunk, m.h_hi, m.h_lo, (s_hlo, T)).then_inc(s_fill, 1)

                elif kind == "mv":
                    if i == 0:
                        for mt in range(2):
                            open_bank(f"mv{mt}")
                    at = CHUNKS.index(f"mv.{i}")
                    hi, lo = (x.rearrange("p (k c) -> p k c", k=2) for x in slots(at)[1:])
                    pe.wait_ge(s_split, at + 1)
                    for mt in range(2):
                        ms = slice(mt * P, (mt + 1) * P)
                        for k in range(2):
                            b = bank(f"mv{mt}")
                            pe.matmul(b, mem_hi[:, 2 * i + k, ms], hi[:, k, :], start=(i == 0 and k == 0), stop=False)
                            pe.matmul(b, mem_hi[:, 2 * i + k, ms], lo[:, k, :], start=False, stop=False)
                            last = pe.matmul(b, mem_lo[:, 2 * i + k, ms], hi[:, k, :], start=False, stop=(i == 3 and k == 1))
                        if i == 3:
                            last.then_inc(s_fill, 1)
                    if i < 3:
                        last.then_inc(s_part, 1)

                elif kind == "av":
                    b = open_bank("avT")
                    project(b, "av", m.h_hi, m.h_lo).then_inc(s_fill, 1)

                elif kind == "ab":
                    b = open_bank("abT")
                    project(b[0:8, :], "ab", m.h_hi, m.h_lo).then_inc(s_fill, 1)

                elif kind in ("av_turn", "ab_turn"):
                    name, n = kind[:2], P if kind == "av_turn" else 8
                    b = open_bank(name)
                    pe.wait_ge(*done(f"{name}T"))
                    for t in range(T):
                        last = pe.transpose(b[:, t * n:(t + 1) * n], turning[name][0:n, t * P:(t + 1) * P], ident[0:n, 0:n])
                    last.then_inc(s_fill, 1)

                elif kind == "scores":
                    group, a, c, n, width = UNITS[i]
                    b = open_bank(f"scores{i}")
                    if group == "D":
                        pe.wait_ge(*done(f"proj d_q.{a}"))
                        for tl in range(2):
                            t = 2 * c + tl
                            last = pe.matmul(b[:, tl * MEM:(tl + 1) * MEM], dqT[:, a, t * P:(t + 1) * P], mkT[:, a, :],
                                             start=True, stop=True)
                    elif group == "C":
                        pe.wait_ge(*done(f"kn{a}"))
                        pe.wait_ge(s_rope, 3)
                        r = slice(64 * (a % 2), 64 * (a % 2) + 64)
                        pe.matmul(b[:, 0:width], qnT[:, a, c * P:(c + 1) * P], knT[:, a, 0:width], start=True, stop=False)
                        pe.matmul(b[:, width - P:width], ident, m.const("causal_neg"), start=False, stop=False)
                        last = pe.matmul(b[:, 0:width], qrT[r, a // 2, c * P:(c + 1) * P], krT[r, 0:width], start=False,
                                         stop=True)
                    else:
                        s, jp = divmod(c, 2)
                        pe.wait_ge(*done("proj a_q.3"))
                        pe.wait_ge(*done("proj ak"))
                        r = slice(64 * s, 64 * s + 64)
                        k1 = (a + 1) * P
                        for jj in range(2):
                            last = pe.matmul(b[:, jj * width:(jj + 1) * width], aqT[r, 2 * jp + jj, a * P:(a + 1) * P],
                                             akT[r, k1 - width:k1], start=True, stop=True)
                    last.then_inc(s_fill, 1)

                elif kind == "turn":
                    group, a, c, n, width = UNITS[i]
                    b = open_bank(f"turn{i}")
                    pe.wait_ge(s_norm, i + 1)
                    p = prob_of(i)
                    nb = width // P
                    for seg in range(n):
                        for j in range(nb):
                            at = seg * P + j * n * P
                            last = pe.transpose(b[:, at:at + P], p[:, seg * width + j * P:seg * width + (j + 1) * P], ident)
                    last.then_inc(s_fill, 1)

                elif kind == "pv":
                    group, a = GROUPS[i]
                    b = open_bank(f"pv{i}")
                    pe.wait_ge(*done(f"turn{LAST_UNIT[i]}"))
                    if group == "D":
                        for mt in range(2):
                            last = pe.matmul(b, mvr[:, mt, a * P:(a + 1) * P], ptD[:, i % 2, mt, :], start=(mt == 0), stop=(mt == 1))
                    elif group == "C":
                        for j in range(T):
                            last = pe.matmul(b[:, j * P:S], cvr[:, j, a * P:(a + 1) * P], pt[:, 0, j, j * P:S],
                                             start=(j == 0), stop=True, skip_group_check=(j > 0))
                    else:
                        ptv = pt[:, 1, :, :].rearrange("p (s f) c -> p s f c", s=2)
                        pe.wait_ge(*done("av"))
                        for s in range(2):
                            r = slice(64 * s, 64 * s + 64)
                            for half in range(0 if a else 1, 2):
                                last = pe.matmul(b[r, :], avr[:, a - 1 + half, r], ptv[:, s, half, :],
                                                 start=(half == 0 or a == 0), stop=(half == 1))
                    last.then_inc(s_fill, 1)

                elif kind == "log_decay":
                    b = open_bank("cum")
                    pe.wait_ge(s_g, 1)
                    pe.matmul(b[:, 0:16], m.const("upto"), g16, start=True, stop=True)
                    pe.matmul(b[:, 16:32], m.const("chunk"), g16, start=True, stop=True).then_inc(s_fill, 1)

                elif kind == "l2":
                    b = open_bank(f"l2.{i}")
                    at = SQ_AT[f"l2.{i}"]
                    pe.wait_ge(s_sq, at + 1)
                    pe.matmul(b, ones, m.sq[:, at % 2, :], start=True, stop=True).then_inc(s_fill, 1)

                elif kind == "decay":
                    b = open_bank(f"gr{i}")
                    for h in range(NH):
                        g = g16[:, 4 * i + h:4 * i + h + 1]
                        last = pe.matmul(b[:, h * P:(h + 1) * P], g.to_broadcast([P, P]), m.const("upto"), start=True, stop=True)
                    last.then_inc(s_fill, 1)

                elif kind == "chunk_rows":
                    for name, first, ready in ((f"krows{i}", 4, "l27"), (f"vrows{i}", 8, "conv11")):
                        b = open_bank(name)
                        pe.wait_ge(*used(ready))
                        for h in range(NH):
                            last = pe.transpose(b[:, h * P:(h + 1) * P], qkvT[:, first + h, i * P:(i + 1) * P], ident)
                        last.then_inc(s_fill, 1)

                elif kind == "chunk_products":
                    tc = slice(i * P, (i + 1) * P)
                    b = open_bank(f"kk{i}")
                    for h in range(NH):
                        last = pe.matmul(b[:, h * P:(h + 1) * P], qkvT[:, 4 + h, tc], qkvT[:, 4 + h, tc], start=True, stop=True)
                    last.then_inc(s_fill, 1)
                    b = open_bank(f"br{i}")
                    for h in range(NH):
                        bc = beta[:, 4 * i + h:4 * i + h + 1]
                        last = pe.matmul(b[:, h * P:(h + 1) * P], bc.to_broadcast([P, P]), ident, start=True, stop=True)
                    last.then_inc(s_fill, 1)
                    b = open_bank(f"qk{i}")
                    for h in range(NH):
                        last = pe.matmul(b[:, h * P:(h + 1) * P], qkvT[:, 4 + h, tc], qkvT[:, h, tc], start=True, stop=True)
                    last.then_inc(s_fill, 1)

                elif kind == "solve_a":
                    lv, t = i
                    b = open_bank(f"p{i}")
                    pe.wait_ge(s_bt, nth("solve_a", i))
                    if lv == 1:
                        pe.wait_ge(s_sol0, t + 1)
                    if lv > 1:
                        pe.wait_ge(*done(f"xx{(lv - 1, t)}"))
                    for h in range(NH):
                        hc = slice(h * P, (h + 1) * P)
                        last = pe.matmul(b[:, hc], BT[:, t, hc], Xm[:, t, hc] if lv else ident, start=True, stop=True)
                    last.then_inc(s_fill, 1)

                elif kind == "solve_b":
                    lv, t = i
                    if lv == 0:
                        continue
                    pe.wait_ge(*done(f"p{i}"))
                    if lv > 1:
                        pe.wait_ge(*done(f"yy{(lv - 1, t)}"))
                    if lv < LEVELS - 1:
                        b = open_bank(f"xx{i}")
                        for h in range(NH):
                            hc = slice(h * P, (h + 1) * P)
                            last = pe.matmul(b[:, hc], Ym[:, t, hc], dec[:, t, hc], start=True, stop=True)
                        last.then_inc(s_fill, 1)
                    b = open_bank(f"yy{i}")
                    for h in range(NH):
                        hc = slice(h * P, (h + 1) * P)
                        last = pe.matmul(b[:, hc], dec[:, t, hc], Ym[:, t, hc], start=True, stop=True)
                    last.then_inc(s_fill, 1)

                elif kind == "w":
                    b = open_bank(f"w{i}")
                    pe.wait_ge(*done(f"krows{i}"))
                    pe.wait_ge(*done(f"yy{(LEVELS - 1, i)}"))
                    for h in range(NH):
                        last = pe.matmul(b[:, h * P:(h + 1) * P], kbg[:, i, h, :], Ym[:, i, h * P:(h + 1) * P], start=True, stop=True)
                    last.then_inc(s_fill, 1)

                elif kind == "qg":
                    b = open_bank(f"gq{i}")
                    for h in range(NH):
                        g = g16[:, 4 * i + h:4 * i + h + 1]
                        last = pe.matmul(b[:, h * P:(h + 1) * P], g.to_broadcast([P, P]), m.const("upto"), start=True, stop=True)
                    last.then_inc(s_fill, 1)

                elif kind == "state_v":
                    t, r, c0 = i // 2, slice(CH * (i % 2), CH * (i % 2) + CH), CH * (i % 2)
                    b = open_bank(f"vn{i}")
                    pe.wait_ge(*done(f"vrows{t}"))
                    pe.wait_ge(*done(f"w{t}"))
                    if i:
                        pe.wait_ge(*done(f"ds{i - 1}"))
                    for h in range(NH):
                        hc = slice(h * P, (h + 1) * P)
                        last = pe.matmul(b[r, hc], Ym[r, t, h * P + c0:h * P + c0 + CH], vb[r, t, h, :], start=True, stop=(i == 0))
                        if i:
                            last = pe.matmul(b[r, hc], nwT[:, t, h * P + c0:h * P + c0 + CH], state[:, i % 2, hc], start=False, stop=True)
                    last.then_inc(s_fill, 1)

                elif kind == "state_o":
                    t, r, c0 = i // 2, slice(CH * (i % 2), CH * (i % 2) + CH), CH * (i % 2)
                    pe.wait_ge(*done(f"vn{i}"))
                    if i < S // CH - 1:
                        b = open_bank(f"ds{i}")
                        for h in range(NH):
                            hc = slice(h * P, (h + 1) * P)
                            last = pe.matmul(b[:, hc], kd[r, t, h, :], vnew[r, i % 2, hc], start=True, stop=True)
                        last.then_inc(s_fill, 1)
                    b = open_bank(f"o{i}")
                    pe.wait_ge(*used(f"qg{t}"))
                    for h in range(NH):
                        hc, oc = slice(h * P, (h + 1) * P), slice(h * CH, (h + 1) * CH)
                        if i:
                            pe.matmul(b[:, oc], state[:, i % 2, hc], qkvT[:, h, i * CH:(i + 1) * CH], start=True, stop=False)
                        last = pe.matmul(b[:, oc], vnew[r, i % 2, hc], Aqk[r, t, h * P + c0:h * P + c0 + CH],
                                         start=(i == 0), stop=True)
                    last.then_inc(s_fill, 1)

                elif kind == "delta_out":
                    b = open_bank(f"on{i}")
                    at = SQ_AT[f"on{i}"]
                    pe.wait_ge(s_sq, at + 1)
                    pe.matmul(b, ones, m.sq[:, at % 2, :], start=True, stop=True).then_inc(s_fill, 1)

                elif kind == "c_norm":
                    b = open_bank(f"cn{i}")
                    names = ("cq0", "cq1") if i == 0 else ("ckv",)
                    for n, name in enumerate(names):
                        at = SQ_AT[name]
                        pe.wait_ge(s_sq, at + 1)
                        last = pe.matmul(b, ones, m.sq[:, at % 2, :], start=(n == 0), stop=(n == len(names) - 1))
                    last.then_inc(s_fill, 1)

                elif kind == "rope":
                    if i == "k":
                        for task, chunk in (("ropek", "kr"), ("ropesk", "krs")):
                            b = open_bank(task)
                            project(b, chunk, m.h_hi, m.h_lo).then_inc(s_fill, 1)
                    else:
                        pe.wait_ge(s_uq, 8 * 16)
                        pe.wait_ge(*used("c_norm0"))
                        for task in (f"rope{i}", f"ropes{i}"):
                            b = open_bank(task)
                            for k in range(2):
                                lhs = (uqr if task == f"rope{i}" else uqs)[:, k, i, :]
                                last = pe.matmul(b, lhs, cqT[:, k, :], start=(k == 0), stop=(k == 1))
                            last.then_inc(s_fill, 1)

                elif kind == "qn":
                    b = open_bank(f"qn{i}")
                    pe.wait_ge(s_uq, 8 * 16)
                    pe.wait_ge(*used("c_norm0"))
                    for k in range(2):
                        last = pe.matmul(b, uq[:, k, i * (NOPE + ROPE):i * (NOPE + ROPE) + NOPE], cqT[:, k, :],
                                         start=(k == 0), stop=(k == 1))
                    last.then_inc(s_fill, 1)

                elif kind == "kn":
                    b = open_bank(f"kn{i}")
                    pe.wait_ge(*used("c_norm1"))
                    pe.matmul(b, ukv[:, i, 0:NOPE], ckvT, start=True, stop=True).then_inc(s_fill, 1)

                elif kind == "cv":
                    b = open_bank(f"cv{i}")
                    pe.matmul(heads(b), ckvT[:, i * P:(i + 1) * P], ukv[:, :, NOPE:2 * NOPE], start=True, stop=True).then_inc(s_fill, 1)

                elif kind == "out":
                    if i == 0:
                        for t in range(T):
                            for n in range(2):
                                open_bank(f"y{t}.{n}")
                    x_hi, x_lo = (m.h_hi[:, 2 * (i % MIX_SLOTS) + j, :] for j in range(2))
                    w_hi, w_lo = m.w_hi[:, CHUNKS.index(f"out.{i}") % SPLIT_SLOTS, :], m.w_lo[:, CHUNKS.index(f"out.{i}") % SPLIT_SLOTS, :]
                    pe.wait_ge(s_split, CHUNKS.index(f"out.{i}") + 1)
                    pe.wait_ge(s_xlo, i + 1)
                    for t in range(T):
                        rows = slice(t * P, (t + 1) * P)
                        for n in range(2):
                            b, c = bank(f"y{t}.{n}"), slice(n * FB, (n + 1) * FB)
                            pe.matmul(b, x_hi[:, rows], w_hi[:, c], start=(i == 0), stop=False)
                            pe.matmul(b, x_hi[:, rows], w_lo[:, c], start=False, stop=False)
                            last = pe.matmul(b, x_lo[:, rows], w_hi[:, c], start=False, stop=(i == 15))
                            if i == 15:
                                last.then_inc(s_fill, 1)
                    if i < 15:
                        last.then_inc(s_part, 1)

        @block.scalar
        def _(act):
            chain = [0]

            def link(ins):
                chain[0] += 1
                ins.then_inc(s_actc, 1)
                act.wait_ge(s_actc, chain[0])

            eps = m.const("eps")

            def tanh_half(src, name, first_wait):
                at = TH_AT[name]
                act.wait_ge(*first_wait)
                if at >= 2:
                    act.wait_ge(*th_free(at))
                act.activation(m.th[:, at % 2, :], src, ACT.Tanh, scale=0.5).then_inc(s_th, 1)

            def square(src, name):
                at = SQ_AT[name]
                if at >= 2:
                    act.wait_ge(*filled(SQ[at - 2][1]))
                act.activation(m.sq[:, at % 2, :], src, ACT.Square).then_inc(s_sq, 1)

            def inv_root(task, name, scale):
                at = TH_AT[name]
                act.wait_ge(*filled(task))
                act.wait_ge(*th_free(at))
                act.activation(m.th[:, at % 2, :], bank(task), ACT.Ln, scale=scale, bias=eps).then_inc(s_act, 1)
                act.wait_ge(*done(task))
                act.activation(m.th[:, at % 2, :], m.th[:, at % 2, :], ACT.Exp, scale=-0.5).then_inc(s_th, 1)

            def load_uq():
                act.dma_start(uq, weights("mla_w_uq").rearrange("a (k p) c -> p (a k) c", p=P)).then_inc(s_uq, 16)
                for k in range(2):
                    src = weights("mla_w_uq")[:, k * P:(k + 1) * P, :].rearrange("a p (h c) -> p (a h) c", h=NH)
                    swapped, plain = (x[:, k, :, :].rearrange("p b c -> p (b c)").rearrange("p (h c) -> p h c", h=NH) for x in (uqs, uqr))
                    for half in range(2):
                        c0 = NOPE + 32 * (1 - half)
                        act.dma_start(swapped[:, :, 32 * half:32 * half + 32], src[:, :, c0:c0 + 32]).then_inc(s_uq, 16)
                    act.dma_start(plain, src[:, :, NOPE:NOPE + ROPE]).then_inc(s_uq, 16)
                act.dma_start(ukv.rearrange("p h c -> p (h c)"), weights("mla_w_ukv").rearrange("a p c -> p (a c)")).then_inc(s_uq, 16)

            def load_bias(blk):
                lo = P if blk == 0 else 0
                act.dma_start(bias[:, blk % 2, :, lo:2 * P], bias_dram[blk, :, :, lo:2 * P]).then_inc(s_bias[blk % 2], 16)

            def copy(task, dst, src, scale=1.0):
                act.wait_ge(*filled(task))
                act.activation(dst, src, ACT.Copy, scale=scale).then_inc(s_act, 1)

            def round_chunk(i):
                raw, hi, _ = slots(i)
                act.wait_ge(*arrived(i))
                if i >= SPLIT_SLOTS:
                    act.wait_ge(*user_done(CHUNKS[i - SPLIT_SLOTS]))
                act.activation(hi, raw, ACT.Copy).then_inc(s_hi, 1)

            for kind, i in STEPS:
                if kind == "params":
                    act.preload_act_table_set(LN_EXP)
                    copy("params", m.pcol[:, :], bank("params")[:, 0:N_PARAM_ROWS])
                    for t in range(T):
                        link(act.activation(junk, m.x[:, t, :], ACT.Square, accum_out=ss[:, t:t + 1]))
                        if t == 1:
                            act.wait_ge(s_mfull, 1)
                            act.activation(mem_hi, memT, ACT.Copy).then_inc(s_mhi, 1)
                    link(act.activation(lg, ss, ACT.Ln, scale=1.0 / D, bias=eps))
                    act.activation(rstd, lg, ACT.Exp, scale=-0.5).then_inc(s_rstd, 1)
                    for c in range(SPLIT_SLOTS):
                        round_chunk(c)

                elif kind == "proj":
                    group, j = (i.split(".") + ["0"])[:2]
                    j = int(j)
                    b = bank(f"proj {i}")
                    if group == "mk":
                        copy(f"proj {i}", mkT[:, j, :], b[:, 0:MEM])
                    else:
                        dst = {"d_q": dqT[:, j, :], "c_q": craw[:, min(j, 1), :], "ckv": craw[:, 2, :], "ak": akT,
                               "a_q": aqT[:, j, :]}[group]
                        copy(f"proj {i}", dst, b, SWA_D ** -0.5 if group == "a_q" else 1.0)

                elif kind == "mv":
                    act.wait_ge(*done(f"xt{i}.1"))
                    act.activation(m.h_hi[:, :, i * P:(i + 1) * P], hf[:, :, i * P:(i + 1) * P], ACT.Copy).then_inc(s_hhi, 1)
                    if i == 3:
                        for mt in range(2):
                            copy(f"mv{mt}", mvr[:, mt, :], bank(f"mv{mt}"))

                elif kind == "gate":
                    tanh_half(bank(f"gate {i}"), f"gate {i}", filled(f"gate {i}"))
                    if i == "a_z.3":
                        load_bias(0)
                        load_bias(1)

                elif kind == "scores":
                    n, width = segments(i)
                    group = UNITS[i][0]
                    act.wait_ge(s_neg, i + 1)
                    if group != "A" and i >= 2:
                        act.wait_ge(*filled(f"turn{i - 2}"))
                    for seg in range(n):
                        cs = slice(seg * width, (seg + 1) * width)
                        src = prob_of(i)[:, cs] if group == "A" else bank(f"scores{i}")[:, cs]
                        ins = act.activation(prob_of(i)[:, cs], src, ACT.Exp, scale=SCALE[group],
                                             bias=stats(1, i)[:, seg:seg + 1], accum_out=stats(2, i)[:, seg:seg + 1])
                    if group == "A":
                        act.activation(stats(3, i), stats(3, i), ACT.Exp).then_inc(s_expA, 1)
                    else:
                        ins.then_inc(s_act, 1)

                elif kind == "turn":
                    group, a, c, n, width = UNITS[i]
                    g = GROUP_OF[i]
                    act.wait_ge(*filled(f"turn{i}"))
                    before = g - (2 if group == "D" else 1)
                    if i == FIRST_UNIT[g] and before >= 0 and GROUPS[before][0] == group:
                        act.wait_ge(*filled(f"pv{before}"))
                    nb = width // P
                    src = bank(f"turn{i}")[:, 0:nb * n * P].rearrange("p (j c) -> p j c", j=nb)
                    if group == "D":
                        dst = ptD[:, g % 2, :, 2 * c * P:(2 * c + 2) * P]
                    elif group == "C":
                        dst = pt[:, 0, 0:nb, c * P:(c + 1) * P]
                    else:
                        s, jp = divmod(c, 2)
                        dst = pt[:, 1, 2 * s + 2 - nb:2 * s + 2, 2 * jp * P:(2 * jp + 2) * P]
                    act.activation(dst, src, ACT.Copy).then_inc(s_act, 1)

                elif kind == "pv":
                    group, a = GROUPS[i]
                    if group == "A" and a + 2 < T:
                        act.wait_ge(*done(f"scores{LAST_UNIT[i]}"))
                        load_bias(a + 2)

                elif kind == "conv":
                    if i >= 2:
                        act.wait_ge(s_taps, i - 1)
                    copy(f"conv{i}", m.pad[:, i % 2, CONV - 1:CONV - 1 + S], bank(f"conv{i}"))
                    if i:
                        tanh_half(qkvT[:, i - 1, :], f"conv{i - 1}", (s_taps, i))
                    if i == 11:
                        tanh_half(qkvT[:, 11, :], "conv11", (s_taps, 12))

                elif kind == "av":
                    copy("avT", turning["av"], bank("avT"))

                elif kind == "ab":
                    copy("abT", turning["ab"][0:8, :], bank("abT")[0:8, :])

                elif kind == "av_turn":
                    copy("av", avr.rearrange("p t c -> p (t c)"), bank("av"))

                elif kind == "ab_turn":
                    copy("ab", sm[:, 32:64], bank("ab")[:, 0:32])

                elif kind == "log_decay":
                    act.wait_ge(*done("ab"))
                    act.activation(th4(tb), abr[:, :, 4:8], ACT.Exp, scale=-1.0).then_inc(s_ab, 1)
                    act.activation(ea[:, 0:4], alog, ACT.Exp).then_inc(s_ab, 1)
                    act.wait_ge(s_nabs, 1)
                    link(act.activation(lnp, nabs, ACT.Exp))
                    act.activation(lnp, lnp, ACT.Ln, bias=1.0).then_inc(s_ln1p, 1)
                    act.wait_ge(s_diff, 1)
                    act.activation(eg, gc[:, 0:16], ACT.Exp)
                    act.activation(ed, gdiff, ACT.Exp).then_inc(s_exps, 1)

                elif kind == "l2":
                    if i == 0:
                        act.preload_act_table_set(LN_EXP)
                    act.wait_ge(*used(f"conv{i}"))
                    square(qkvT[:, i, :], f"l2.{i}")
                    if i:
                        inv_root(f"l2.{i - 1}", f"l2{i - 1}", 0.25)
                    if i == 7:
                        inv_root("l2.7", "l27", 0.25)

                elif kind == "decay":
                    act.wait_ge(*done(f"gr{i}"))
                    act.activation(dec[:, i, :], dec[:, i, :], ACT.Exp).then_inc(s_dec, 1)

                elif kind == "solve_a":
                    lv, t = i
                    if lv == 0:
                        act.wait_ge(*done(f"qk{t}"))
                    elif lv == 1:
                        act.wait_ge(s_sol0, t + 1)
                    elif lv > 1:
                        act.wait_ge(*filled(f"yy{(lv - 1, t)}"))
                    copy(f"p{i}", dec[:, t, :], bank(f"p{i}"))

                elif kind == "w":
                    copy(f"w{i}", nwT[:, i, :], bank(f"w{i}"))

                elif kind == "qg":
                    at = TH_AT[f"qg{i}"]
                    act.wait_ge(*th_free(at))
                    act.wait_ge(*filled(f"gq{i}"))
                    act.activation(m.th[:, at % 2, :], bank(f"gq{i}"), ACT.Exp).then_inc(s_act, 1)

                elif kind == "state_v":
                    r = slice(CH * (i % 2), CH * (i % 2) + CH)
                    if i >= 2:
                        act.wait_ge(*filled(f"o{i - 2}"))
                    copy(f"vn{i}", vnew[r, i % 2, :], bank(f"vn{i}")[r, :])

                elif kind == "state_o":
                    copy(f"o{i}", oT[:, :, i * CH:(i + 1) * CH], bank(f"o{i}")[:, 0:NH * CH].rearrange("p (h c) -> p h c", h=NH))

                elif kind == "delta_out":
                    if i == 0:
                        act.preload_act_table_set(LN_EXP)
                        act.wait_ge(*done(f"o{S // CH - 1}"))
                        load_uq()
                    square(oT[:, i, :], f"on{i}")
                    if i:
                        inv_root(f"on{i - 1}", f"delta_out{i - 1}", 1.0 / P)
                    if i == NH - 1:
                        inv_root(f"on{i}", f"delta_out{i}", 1.0 / P)

                elif kind == "c_norm":
                    for j in ((0, 1) if i == 0 else (2,)):
                        name = ("c_q.0", "c_q.1", "ckv")[j]
                        act.wait_ge(*done(f"proj {name}"))
                        square(craw[:, j, :], ("cq0", "cq1", "ckv")[j])
                    inv_root(f"cn{i}", f"c_norm{i}", 1.0 / (2 * P if i == 0 else P))

                elif kind in ("qn", "kn", "cv"):
                    if (kind, i) == ("kn", 0):
                        act.wait_ge(s_mixB, NH)
                    dst = {"qn": qnT, "kn": knT, "cv": cvr}[kind][:, i, :]
                    copy(f"{kind}{i}", dst, bank(f"{kind}{i}"))

                elif kind == "mix_split":
                    if i == 0:
                        act.dma_start(gpost, weights("norm_post").partition_broadcast(P).rearrange("p a c -> p (a c)")).then_inc(s_gpost, 16)
                    act.wait_ge(*mix_ready(i))
                    if i >= MIX_SLOTS:
                        act.wait_ge(s_part, PARTIAL.index(("out", i - MIX_SLOTS)) + 1)
                    act.activation(m.h_hi[:, 2 * (i % MIX_SLOTS), :], m.mix[:, OUT_K[i], :], ACT.Copy).then_inc(s_xhi, 1)

                elif kind == "residual":
                    act.preload_act_table_set(LN_EXP)

                    def root(t):
                        act.wait_ge(s_yadd, t + 1)
                        link(act.activation(rs2[:, t:t + 1], lg2[:, t:t + 1], ACT.Ln, scale=1.0 / D, bias=eps))
                        act.activation(rs2[:, t:t + 1], rs2[:, t:t + 1], ACT.Exp, scale=-0.5).then_inc(s_y, 1)

                    for t in range(T):
                        for n in range(2):
                            act.wait_ge(*filled(f"y{t}.{n}"))
                            act.activation(junk[:, 0:FB], bank(f"y{t}.{n}"), ACT.Square,
                                           accum_out=ss2[:, 2 * t + n:2 * t + n + 1]).then_inc(s_ysum, 1)
                            act.wait_ge(s_ysum, 2 * t + n + 1)
                        if t:
                            root(t - 1)
                    root(T - 1)

                for c in chunks_behind((kind, i)):
                    round_chunk(c)

        @block.vector
        def _(dve):
            chain = [0]

            def link(ins):
                chain[0] += 1
                ins.then_inc(s_dvec, 1)
                dve.wait_ge(s_dvec, chain[0])

            def th(name):
                at = TH_AT[name]
                if name.startswith("qg"):
                    dve.wait_ge(*done(f"gq{name[2:]}"))
                else:
                    dve.wait_ge(s_th, sum(not x.startswith("qg") for x, _ in TH[:at + 1]))
                return m.th[:, at % 2, :]

            def col(i):
                return m.pcol[:, i:i + 1]

            def over_free(cols, n=P):
                return cols.unsqueeze(2).to_broadcast([P, cols.shape[1], n])

            def silu2(j):
                dve.wait_ge(s_taps, j + 1)
                t = th(f"conv{j}")
                dve.scalar_tensor_tensor(out=qkvT[:, j, :], in0=t, scalar=1.0, in1=qkvT[:, j, :],
                                         op0=ALU.add, op1=ALU.mult).then_inc(s_thused, 1)

            def l2_scale(j):
                t = th(f"l2{j}")
                dve.scalar_tensor_tensor(out=qkvT[:, j, :], in0=qkvT[:, j, :], scalar=0.5 * (float(P) ** -0.5 if j < 4 else 1.0),
                                         in1=t, op0=ALU.mult, op1=ALU.mult).then_inc(s_thused, 1)

            def delta_gate(h):
                t = th(f"delta_out{h}")
                dve.scalar_tensor_tensor(out=oT[:, h, :], in0=oT[:, h, :], scalar=col(GDNN), in1=t,
                                         op0=ALU.mult, op1=ALU.mult).then_inc(s_thused, 1)
                dve.wait_ge(*used(f"delta_out{h}"))
                dve.wait_ge(*done(f"gate b_z.{h}"))
                dve.scalar_tensor_tensor(out=m.mix[:, 4 + h, :], in0=oT[:, h, :], scalar=0.5, in1=m.mix[:, 4 + h, :],
                                         op0=ALU.mult, op1=ALU.mult).then_inc(s_mixB, 1)

            for kind, i in STEPS:
                if kind == "params":
                    dve.wait_ge(*done("params"))
                    dve.wait_ge(s_mem, 16)
                    dve.tensor_tensor(memT, memT, over_free(m.pcol[:, MEMN:MEMN + KD], MEM), ALU.mult).then_inc(s_mfull, 1)
                    dve.wait_ge(s_mfull, 1)
                    dve.wait_ge(s_mhi, 1)
                    dve.tensor_tensor(mem_lo, memT, mem_hi, ALU.subtract).then_inc(s_mlo, 1)
                    dve.wait_ge(s_rstd, 1)
                    for t in range(T):
                        dve.tensor_scalar(xs[:, t, :], m.x[:, t, :], rstd[:, t:t + 1], None, ALU.mult).then_inc(s_xs, 1)

                elif kind == "xt":
                    for kk in range(2):
                        dve.wait_ge(*filled(f"xt{i}.{kk}"))
                        dve.tensor_tensor(hf[:, 4 * kk:4 * kk + 4, i * P:(i + 1) * P], heads(bank(f"xt{i}.{kk}")),
                                          over_free(m.pcol[:, PRE + 4 * kk:PRE + 4 * kk + 4]), ALU.mult).then_inc(s_dve, 1)

                elif kind == "h_split":
                    dve.wait_ge(*filled("mv1"))
                    for t in range(T):
                        tc = slice(t * P, (t + 1) * P)
                        dve.wait_ge(s_hhi, t + 1)
                        dve.tensor_tensor(m.h_lo[:, :, tc], hf[:, :, tc], m.h_hi[:, :, tc], ALU.subtract).then_inc(s_hlo, 1)

                elif kind == "gate":
                    t = th(f"gate {i}")
                    dve.scalar_tensor_tensor(out=m.mix[:, MIX_AT[i], :], in0=t, scalar=1.0, in1=bank(f"gate {i}"),
                                             op0=ALU.add, op1=ALU.mult).then_inc(s_dve, 1)

                elif kind == "scores":
                    group, a, c, _, _ = UNITS[i]
                    n, width = segments(i)
                    b = bank(f"scores{i}")[:, 0:n * width].rearrange("p (s k) -> p s k", s=n)
                    dve.wait_ge(*filled(f"scores{i}"))
                    if group != "A":
                        link(dve.tensor_reduce(stats(0, i), b, AX.X, ALU.max))
                        dve.tensor_scalar(stats(1, i), stats(0, i), -SCALE[group], None, ALU.mult).then_inc(s_neg, 1)
                    else:
                        s, jp = divmod(c, 2)
                        h0 = 4 * s + 2 * jp
                        p = prob_of(i)[:, 0:n * width].rearrange("p (s k) -> p s k", s=n)
                        dve.wait_ge(*filled(f"turn{i - 2}"))
                        dve.wait_ge(s_bias[a % 2], 16 * (a // 2 + 1))
                        dve.tensor_tensor(p, b, bias[:, a % 2, h0:h0 + 2, 2 * P - width:2 * P], ALU.add).then_inc(s_dve, 1)
                        dve.wait_ge(*done(f"scores{i}"))
                        link(dve.tensor_reduce(stats(0, i), p, AX.X, ALU.max))
                        link(dve.tensor_tensor(stats(0, i), stats(0, i), sink[:, h0:h0 + 2], ALU.max))
                        link(dve.tensor_scalar(stats(1, i), stats(0, i), -1.0, None, ALU.mult))
                        dve.tensor_tensor(stats(3, i), sink[:, h0:h0 + 2], stats(1, i), ALU.add).then_inc(s_neg, 1)

                elif kind == "norm":
                    n, width = segments(i)
                    if UNITS[i][0] == "A":
                        dve.wait_ge(s_expA, A_UNITS.index(i) + 1)
                        link(dve.tensor_tensor(stats(2, i), stats(2, i), stats(3, i), ALU.add))
                    else:
                        dve.wait_ge(*done(f"scores{i}"))
                    link(dve.reciprocal(stats(4, i), stats(2, i)))
                    for seg in range(n):
                        p = prob_of(i)[:, seg * width:(seg + 1) * width]
                        ins = dve.tensor_scalar(p, p, stats(4, i)[:, seg:seg + 1], None, ALU.mult)
                    ins.then_inc(s_norm, 1)

                elif kind == "pv":
                    group, a = GROUPS[i]
                    dve.wait_ge(*filled(f"pv{i}"))
                    if group == "A":
                        dve.wait_ge(*done("gate a_z.3"))
                        g = m.mix[:, 0:4, a * P:(a + 1) * P]
                        b = heads(bank(f"pv{i}"))
                    else:
                        z = "d_z" if group == "D" else "c_z"
                        dve.wait_ge(*done(f"gate {z}.{a}"))
                        g = m.mix[:, MIX_AT[f"{z}.{a}"], :]
                        b = bank(f"pv{i}")
                    dve.scalar_tensor_tensor(out=g, in0=b, scalar=0.5, in1=g, op0=ALU.mult, op1=ALU.mult).then_inc(s_dve, 1)

                elif kind == "conv":
                    dve.wait_ge(*done(f"conv{i}"))
                    p = m.pad[:, i % 2, :]
                    acc = qkvT[:, i, :]
                    link(dve.tensor_scalar(acc, p[:, 0:S], col(CONVW + i), None, ALU.mult))
                    for tap in range(1, CONV):
                        ins = dve.scalar_tensor_tensor(out=acc, in0=p[:, tap:tap + S], scalar=col(CONVW + 12 * tap + i),
                                                       in1=acc, op0=ALU.mult, op1=ALU.add)
                        if tap < CONV - 1:
                            link(ins)
                    ins.then_inc(s_taps, 1)
                    if i:
                        silu2(i - 1)
                    if i == 11:
                        silu2(11)

                elif kind == "log_decay":
                    dve.wait_ge(s_ab, 2)
                    dve.wait_ge(*done("ab"))
                    link(dve.tensor_scalar(tb, tb, 1.0, None, ALU.add))
                    link(dve.reciprocal(beta, tb))
                    link(dve.tensor_tensor(th4(xdt), abr[:, :, 0:4], dtb.unsqueeze(1).to_broadcast([P, T, NH]), ALU.add))
                    link(dve.tensor_scalar(mx, xdt, 0.0, None, ALU.max))
                    dve.scalar_tensor_tensor(out=nabs, in0=mx, scalar=-2.0, in1=xdt, op0=ALU.mult, op1=ALU.add).then_inc(s_nabs, 1)
                    dve.wait_ge(s_ln1p, 1)
                    link(dve.tensor_tensor(mx, mx, lnp, ALU.add))
                    dve.scalar_tensor_tensor(out=th4(g16), in0=th4(mx), scalar=-1.0,
                                             in1=ea[:, 0:4].unsqueeze(1).to_broadcast([P, T, NH]),
                                             op0=ALU.mult, op1=ALU.mult).then_inc(s_g, 1)
                    dve.wait_ge(*filled("cum"))
                    dve.tensor_copy(gc, bank("cum")[:, 0:32]).then_inc(s_dve, 1)
                    dve.wait_ge(*done("cum"))
                    dve.tensor_tensor(gdiff, gc[:, 16:32], gc[:, 0:16], ALU.subtract).then_inc(s_diff, 1)
                    link(dve.tensor_scalar(vbs, beta, 0.5, None, ALU.mult))
                    dve.wait_ge(s_exps, 1)
                    link(dve.scalar_tensor_tensor(out=nbeg, in0=beta, scalar=-1.0, in1=eg, op0=ALU.mult, op1=ALU.mult))

                elif kind == "l2":
                    if i:
                        l2_scale(i - 1)
                    if i == 7:
                        l2_scale(7)

                elif kind == "decay":
                    dve.wait_ge(*filled(f"gr{i}"))
                    for h in range(NH):
                        hc = slice(h * P, (h + 1) * P)
                        ins = dve.scalar_tensor_tensor(out=dec[:, i, hc], in0=bank(f"gr{i}")[:, hc],
                                                       scalar=gc[:, 4 * i + h:4 * i + h + 1], in1=m.const("decay_neg"),
                                                       op0=ALU.subtract, op1=ALU.add)
                    ins.then_inc(s_dve, 1)

                elif kind == "chunk_rows":
                    dve.wait_ge(*filled(f"krows{i}"))
                    k = heads(bank(f"krows{i}"))
                    c = slice(4 * i, 4 * i + 4)
                    dve.tensor_tensor(kbg[:, i, :, :], k, over_free(nbeg[:, c]), ALU.mult)
                    dve.tensor_tensor(kd[:, i, :, :], k, over_free(ed[:, c]), ALU.mult).then_inc(s_dve, 1)
                    dve.wait_ge(*filled(f"vrows{i}"))
                    dve.tensor_tensor(vb[:, i, :, :], heads(bank(f"vrows{i}")), over_free(vbs[:, c]), ALU.mult).then_inc(s_dve, 1)

                elif kind == "chunk_products":
                    dve.wait_ge(s_dec, i + 1)
                    dve.wait_ge(*filled(f"kk{i}"))
                    dve.tensor_tensor(LT[:, i, :], bank(f"kk{i}"), dec[:, i, :], ALU.mult).then_inc(s_dve, 1)
                    dve.wait_ge(*done(f"kk{i}"))
                    dve.wait_ge(*filled(f"br{i}"))
                    dve.tensor_tensor(LT[:, i, :], bank(f"br{i}"), LT[:, i, :], ALU.mult).then_inc(s_dve, 1)
                    dve.wait_ge(*filled(f"qk{i}"))
                    dve.tensor_tensor(Aqk[:, i, :], bank(f"qk{i}"), dec[:, i, :], ALU.mult).then_inc(s_dve, 1)

                elif kind == "solve_b":
                    lv, t = i
                    if lv == 0:
                        eye = m.const("ident").unsqueeze(1).to_broadcast([P, NH, P])
                        dve.wait_ge(s_bt, t + 1)
                        dve.wait_ge(*done(f"p{i}"))
                        dve.tensor_tensor(heads(Ym[:, t, :]), eye, heads(BT[:, t, :]), ALU.subtract)
                        dve.tensor_tensor(heads(Xm[:, t, :]), eye, heads(dec[:, t, :]), ALU.subtract).then_inc(s_sol0, 1)
                    else:
                        for name, dst in ((f"xx{i}", Xm), (f"yy{i}", Ym)):
                            if name in TASK_AT:
                                dve.wait_ge(*filled(name))
                                dve.tensor_tensor(dst[:, t, :], dst[:, t, :], bank(name), ALU.subtract).then_inc(s_dve, 1)

                elif kind == "qg":
                    t = heads(th(f"qg{i}"))
                    dve.tensor_copy(gle[:, i, :, :], t[:, :, CH - 1::CH])
                    q = qkvT[:, 0:4, i * P:(i + 1) * P]
                    dve.wait_ge(*done(f"qk{i}"))
                    dve.tensor_tensor(q, q, t, ALU.mult).then_inc(s_thused, 1)

                elif kind == "state_o":
                    if i < S // CH - 1:
                        new, old = state[:, (i + 1) % 2, :], state[:, i % 2, :]
                        if i:
                            if i >= 1:
                                dve.wait_ge(*filled(f"o{i - 1}"))
                            dve.wait_ge(*done(f"ds{i - 1}"))
                            link(dve.tensor_tensor(heads(new), heads(old),
                                                   gle[:, i // 2, :, i % 2:i % 2 + 1].to_broadcast([P, NH, P]), ALU.mult))
                            dve.wait_ge(*filled(f"ds{i}"))
                            dve.tensor_tensor(new, new, bank(f"ds{i}"), ALU.add).then_inc(s_dve, 1)
                        else:
                            dve.wait_ge(*filled("ds0"))
                            dve.tensor_copy(new, bank("ds0")).then_inc(s_dve, 1)

                elif kind == "delta_out":
                    if i:
                        delta_gate(i - 1)
                    if i == NH - 1:
                        delta_gate(i)

                elif kind == "c_norm":
                    t = th(f"c_norm{i}")
                    if i == 0:
                        dve.scalar_tensor_tensor(out=cqT[:, 0, :], in0=craw[:, 0, :], scalar=col(CQN), in1=t,
                                                 op0=ALU.mult, op1=ALU.mult).then_inc(s_cq0, 1)
                        dve.scalar_tensor_tensor(out=cqT[:, 1, :], in0=craw[:, 1, :], scalar=col(CQN + 1), in1=t,
                                                 op0=ALU.mult, op1=ALU.mult).then_inc(s_thused, 1)
                    else:
                        dve.scalar_tensor_tensor(out=ckvT, in0=craw[:, 2, :], scalar=col(CKVN), in1=t,
                                                 op0=ALU.mult, op1=ALU.mult).then_inc(s_thused, 1)

                elif kind == "rope":
                    dst = krT if i == "k" else qrT[:, i, :]
                    dve.wait_ge(*filled(f"rope{i}"))
                    dve.tensor_tensor(dst, bank(f"rope{i}"), m.cosT[:, :], ALU.mult).then_inc(s_dve, 1)
                    dve.wait_ge(*filled(f"ropes{i}"))
                    dve.tensor_tensor(prob_ca[:, 0, :], bank(f"ropes{i}"), m.sinT[:, :], ALU.mult).then_inc(s_dve, 1)
                    dve.wait_ge(*done(f"ropes{i}"))
                    dve.tensor_tensor(dst, dst, prob_ca[:, 0, :], ALU.add).then_inc(s_rope, 1)
                    dve.wait_ge(s_rope, ["k", 0, 1].index(i) + 1)

                elif kind == "mix_split":
                    dve.wait_ge(s_xhi, i + 1)
                    slot = 2 * (i % MIX_SLOTS)
                    dve.tensor_tensor(m.h_hi[:, slot + 1, :], m.mix[:, OUT_K[i], :], m.h_hi[:, slot, :], ALU.subtract).then_inc(s_xlo, 1)

                elif kind == "residual":
                    dve.wait_ge(s_gpost, 16)

                    def add(t):
                        dve.wait_ge(s_y, t + 1)
                        if t:
                            dve.wait_ge(s_xfin, 2 * t)
                        for n in range(2):
                            c = slice(n * FB, (n + 1) * FB)
                            dve.scalar_tensor_tensor(out=ytmp[:, n, :], in0=bank(f"y{t}.{n}"), scalar=rs2[:, t:t + 1], in1=gpost[:, c],
                                                     op0=ALU.mult, op1=ALU.mult).then_inc(s_dve, 1)
                        for n in range(2):
                            c = slice(n * FB, (n + 1) * FB)
                            dve.wait_ge(*done(f"y{t}.{n}"))
                            dve.tensor_tensor(m.x[:, t, c], m.x[:, t, c], ytmp[:, n, :], ALU.add).then_inc(s_xfin, 1)

                    for t in range(T):
                        dve.wait_ge(s_ysum, 2 * t + 2)
                        dve.tensor_tensor(lg2[:, t:t + 1], ss2[:, 2 * t:2 * t + 1], ss2[:, 2 * t + 1:2 * t + 2], ALU.add).then_inc(s_yadd, 1)
                        if t:
                            add(t - 1)
                    add(T - 1)


LAYER_SEMS = ["bank_filled", "freed_by_act", "freed_by_dve", "chunk_in0", "chunk_in1", "chunk_in2", "chunk_in3", "w_rounded", "w_split",
              "part_done", "params_in", "memory_in", "uq_in", "bias_in0", "bias_in1", "gpost_in", "rstd_ready", "xs_ready",
              "mem_hi_ready", "mem_lo_ready", "mem_gained", "h_hi_ready", "h_lo_ready", "mix_hi_ready", "mix_lo_ready",
              "act_chain", "dve_chain", "neg_max_ready", "exp_ready", "prob_ready", "taps_done", "th_ready", "th_used",
              "squares_ready", "ab_ready", "nabs_ready", "ln1p_ready", "log_decay_ready", "decay_ready", "diff_ready", "exps_ready",
              "level_ready", "solve0_ready", "mix_delta_ready", "cq0_ready", "rope_ready", "x_ready", "y_sums_ready",
              "y_sum_ready", "y_rstd_ready"]


def program(nc, ins, out):
    with ExitStack() as ctx:
        m = Memory(nc, ctx)
        bias_dram = nc.dram_tensor("swa_bias", (T, P, SWA_H, 2 * P), F32, kind="Internal").ap()
        sems = [m._sem(n) for n in LAYER_SEMS]
        w = {n: ins[n] for n in ("norm_pre", "norm_post", "w_in", "attn_sinks", "gdn_conv_w", "gdn_a_log", "gdn_dt_bias",
                                 "gdn_norm", "mla_q_norm", "mla_kv_norm", "mla_w_uq", "mla_w_ukv", "mem_norm", "mem_w_kv", "w_out")}
        grouped = sems[0:3] + [sems[3:7]] + sems[7:13] + [sems[13:15]] + sems[15:]
        mem_dram = nc.dram_tensor("mem_normed", (P, KD, MEM), F32, kind="Internal").ap()
        prologue(nc, m, ctx, (ins["x"], ins["mem"], ins["positions"], ins["rel_bias"], ins["consts"]), bias_dram, mem_dram)
        with nc.Fori(0, DEPTH) as l:
            layer(nc, m, l, w, bias_dram, mem_dram, grouped)
            with nc.Block() as block:
                @block.gpsimd
                def _(pool):
                    for s in sems:
                        pool.sem_clear(s)
        s_out = m._sem("out_written")
        with nc.Block() as block:
            @block.sync
            def _(sp):
                sp.dma_start(out[0].rearrange("(t p) d -> p t d", p=P), m.x[:, :, :]).then_inc(s_out, 16)
                sp.wait_ge(s_out, 16)


_INS = ["x", "mem", "positions", "rel_bias", "norm_pre", "norm_post", "w_in", "attn_sinks", "gdn_conv_w", "gdn_a_log",
        "gdn_dt_bias", "gdn_norm", "mla_q_norm", "mla_kv_norm", "mla_w_uq", "mla_w_ukv", "mem_norm", "mem_w_kv", "w_out"]


def kernel(**inputs):
    import numpy as _np
    import concourse.bacc as _bacc
    from concourse import mybir as _mybir
    from concourse.bass_utils import run_bass_kernel_spmd as _run

    nc = _bacc.Bacc("TRN2", target_bir_lowering=False, num_devices=1)
    arrays, args = {}, {}
    for name in _INS:
        a = _np.ascontiguousarray(inputs[name])
        arrays[f"in_{name}"] = a
        args[name] = nc.dram_tensor(f"in_{name}", a.shape, _mybir.dt.from_np(a.dtype), kind="ExternalInput").ap()
    arrays["in_consts"] = CONSTS
    args["consts"] = nc.dram_tensor("in_consts", CONSTS.shape, _mybir.dt.float32, kind="ExternalInput").ap()
    out = nc.dram_tensor("out", (1, S, D), _mybir.dt.float32, kind="ExternalOutput").ap()
    program(nc, args, out)
    r = _run(nc, [arrays], core_ids=[0])
    return r.results[0]["out"]
```

```python
from contextlib import ExitStack
import itertools
import math

import numpy as np
import concourse.bass as bass
from concourse import mybir

F32 = mybir.dt.float32
F32R = mybir.dt.float32r
BF16 = mybir.dt.bfloat16
I32 = mybir.dt.int32
ALU = mybir.AluOpType
ACT = mybir.ActivationFunctionType
AX = mybir.AxisListType

P = 128
S, D, DEPTH, MEM = 512, 1024, 2, 256
T = S // P
KD = D // P
GW = D // 2
NH = 4
SWA_H, SWA_D = 8, 64
NOPE, ROPE = 128, 64
BUCKETS, MAX_DIST = 32, 128
CH = 64
LEVELS = 6
EPS = 1e-6
NEG = -1e30
BANKS = 8
FB = 512
CONV = 4

OFF = {}
_at = 0
for _n, _w in (("a_q", 512), ("a_k", 128), ("a_v", 128), ("a_z", 512), ("b_q", 512), ("b_k", 512),
               ("b_v", 512), ("b_ab", 8), ("b_z", 512), ("c_q", 256), ("c_kv", 128), ("c_kr", 64),
               ("c_z", 512), ("d_q", 512), ("d_z", 512)):
    OFF[_n] = _at
    _at += _w
D_IN = _at

CONST_AT = {}


def constants():
    i = np.arange(P)
    same = (i[:, None] // CH) == (i[None, :] // CH)
    cols = []

    def put(name, a):
        CONST_AT[name] = (sum(c.shape[1] for c in cols), a.shape[1])
        cols.append(np.asarray(a, np.float32))

    put("ident", np.eye(P))
    put("ones", np.ones((P, P)))
    upto = same & (i[:, None] <= i[None, :])
    put("upto", upto)
    put("chunk", same)
    put("decay_neg", np.where(upto, 0.0, NEG))
    for lv in range(LEVELS):
        m = 1 << lv
        pair = (i[:, None] // (2 * m)) == (i[None, :] // (2 * m))
        put(f"level{lv}", pair & (i[:, None] % (2 * m) < m) & (i[None, :] % (2 * m) >= m))
    put("causal_neg", np.where(i[None, :] <= i[:, None], 0.0, NEG))
    inv_freq = np.float32(1.0) / np.power(np.float32(10000.0), np.arange(0, ROPE, 2, dtype=np.float32) / ROPE)
    put("inv_freq", inv_freq[i % 32][:, None])
    put("rope_sign", np.where(i % 64 < 32, -1.0, 1.0)[:, None])
    half = BUCKETS // 2
    least = [-1e30] + list(range(1, half)) + [
        math.ceil(half * (MAX_DIST / half) ** (j / half) - 1e-9) for j in range(half)]
    put("bucket_least", np.array(least, np.float64)[i % BUCKETS][:, None])
    put("eps", np.full((P, 1), EPS))
    return np.ascontiguousarray(np.concatenate(cols, 1))


CONSTS = constants()

WC = KD * P
RAW_SLOTS, SPLIT_SLOTS = 4, 2
OUT_K = list(range(12, 16)) + list(range(4, 8)) + list(range(8, 12)) + list(range(0, 4))
MIX_SLOTS = 4
MIX_AT = {f"{g}.{j}": 4 * n + j for n, g in enumerate(("a_z", "b_z", "c_z", "d_z")) for j in range(4)}

UNITS = [("D", h, tp, 2, MEM) for h in range(NH) for tp in range(2)]
for _i in range(T):
    for _j in range(T):
        UNITS += [("C", _i, T - 1 - _j, 1, P * (T - _j)), ("A", _i, _j, 2, 2 * P if _i else P)]
GROUPS = [("D", h) for h in range(NH)] + [("C", h) for h in range(NH)] + [("A", blk) for blk in range(T)]
GROUP_OF = [GROUPS.index(u[:2]) for u in UNITS]
FIRST_UNIT = [GROUP_OF.index(g) for g in range(len(GROUPS))]
LAST_UNIT = [max(i for i, x in enumerate(GROUP_OF) if x == g) for g in range(len(GROUPS))]
A_UNITS = [i for i, u in enumerate(UNITS) if u[0] == "A"]
LN_EXP = "natural_log_exp_and_others"
SCALE = {"D": float(P) ** -0.5, "C": float(NOPE + ROPE) ** -0.5, "A": 1.0}


LAG = 4
PROB_SLOTS = {"D": 2, "C": 6, "A": 6}


def attention(units, lag, fillers=()):
    steps, fillers = [], list(fillers)
    n = len(units)
    for i in range(n + lag + 2):
        if i < n:
            steps.append(("scores", units[i]))
        if 1 <= i <= n:
            steps.append(("norm", units[i - 1]))
        if fillers:
            steps.append(fillers.pop(0))
        if lag <= i < n + lag:
            steps.append(("turn", units[i - lag]))
        if i >= lag + 2:
            u = units[i - lag - 2]
            if u == LAST_UNIT[GROUP_OF[u]]:
                steps.append(("pv", GROUP_OF[u]))
    return steps + fillers


def mixed(*runs):
    return [x for row in itertools.zip_longest(*runs) for x in row if x is not None]


STEPS = mixed([("proj", f"mk.{h}") for h in range(NH)], [("xt", t) for t in range(T)])
STEPS += [("mv", c) for c in range(NH)] + [("h_split", 0)]
STEPS += [("proj", f"d_q.{h}") for h in range(NH)] + [("gate", f"d_z.{j}") for j in range(4)]
STEPS += attention(range(0, 8), 2, [("conv", j) for j in range(12)])
STEPS += [("ab", 0), ("square", ("l2.", 4)), ("square", ("l2.", 5)), ("av", 0), ("ab_turn", 0), ("l2", 4),
          ("square", ("l2.", 6)), ("log_decay", 0), ("av_turn", 0), ("l2", 5), ("square", ("l2.", 7)),
          ("l2", 6), ("square", ("l2.", 0)), ("cum", 0), ("l2", 7)]
for _t in range(T):
    STEPS += ([("square", ("l2.", 1 + _t))] if _t < 3 else []) + [("decay", _t), ("l2", _t)]
STEPS += [("gate", "b_z.0")]
STEPS += [("chunk_rows", t) for t in range(T)]
STEPS += [("chunk_products", t) for t in range(T)]
STEPS += [("gate", "b_z.1")]
for _lv in range(LEVELS):
    STEPS += [("solve_a", (_lv, t)) for t in range(T)] + [("solve_b", (_lv, t)) for t in range(T)]
    STEPS += {0: [("gate", "b_z.2")], 2: [("gate", "b_z.3")]}.get(_lv, [])
STEPS += [("w", t) for t in range(T)] + [("qg", t) for t in range(T)]
_fillers = [("proj", "c_q.0"), ("proj", "c_q.1"), ("proj", "ckv")] + [("gate", f"c_z.{_j}") for _j in range(4)]
for _n in range(S // CH):
    STEPS += [("state_v", _n)] + ([_fillers[_n - 1]] if _n else []) + [("state_o", _n)]
STEPS += [("square", ("on", 0)), ("square", ("on", 1)), ("proj", "ak"), ("delta_out", 0), ("square", ("on", 2)),
          ("proj", "a_q.0"), ("delta_out", 1), ("square", ("on", 3)), ("proj", "a_q.1"), ("delta_out", 2), ("square", ("c", 0)),
          ("proj", "a_q.2"), ("delta_out", 3), ("square", ("c", 1)), ("rope", "k"), ("c_norm", 0), ("square", ("c", 2)),
          ("proj", "a_q.3"), ("c_norm", 1)]
STEPS += [("qn", h) for h in range(NH)] + [("kn", h) for h in range(NH)] + [("cv", t) for t in range(T)]
STEPS += [("rope", 0), ("rope", 1)]
STEPS += [("gate", f"a_z.{j}") for j in range(4)]
STEPS += [("params", 0)]
STEPS += attention(range(8, 40), LAG)
STEPS += [("mix_split", n) for n in range(MIX_SLOTS)]
for _n in range(16):
    STEPS += [("out", _n)] + ([("mix_split", _n + MIX_SLOTS)] if _n + MIX_SLOTS < 16 else []) + ([("memory", 0)] if _n == 12 else [])
STEPS += [("residual", t) for t in range(T + 2)]

CHUNKS, CHUNK_USER = [], {}
for _s in STEPS:
    _kind, _i = _s
    for _c in {"proj": [_i], "gate": [_i], "mv": [f"mv.{_i}"], "av": ["av"], "ab": ["ab"], "out": [f"out.{_i}"],
               "rope": ["kr", "krs"] if _i == "k" else [],
               "conv": [f"b_{'qkv'[_i // 4 % 3]}.{_i % 4}"] if _kind == "conv" else []}.get(_kind, []):
        CHUNKS.append(_c)
        CHUNK_USER[_c] = _s
CHUNK_USER["out.15"] = ("residual", 2)
assert len(CHUNKS) % RAW_SLOTS == 0


def tasks_of(step):
    kind, i = step
    return {
        "params": lambda: [("params", "A")],
        "xt": lambda: [(f"xt{i}.{kk}", "V") for kk in range(2)],
        "proj": lambda: [(f"proj {i}", "A")],
        "mv": lambda: [(f"mv{mt}", "A") for mt in range(2)] if i == 3 else [],
        "gate": lambda: [(f"gate {i}", "V")],
        "scores": lambda: [(f"scores{i}", "V" if UNITS[i][0] == "A" else "A")],
        "turn": lambda: [(f"turn{i}", "A")],
        "pv": lambda: [(f"pv{i}", "V")],
        "conv": lambda: [(f"conv{i}", "A")],
        "av": lambda: [("avT", "A")],
        "av_turn": lambda: [("av", "A")],
        "ab": lambda: [("abT", "A")],
        "ab_turn": lambda: [("ab", "A")],
        "cum": lambda: [("cum", "V")],
        "l2": lambda: [(f"l2.{i}", "A")],
        "decay": lambda: [(f"gr{i}", "V")],
        "chunk_rows": lambda: [(f"krows{i}", "V"), (f"vrows{i}", "V")],
        "chunk_products": lambda: [(f"kk{i}", "V"), (f"br{i}", "V"), (f"qk{i}", "V")],
        "solve_a": lambda: [(f"p{i}", "A")],
        "solve_b": lambda: ([(f"xx{i}", "V")] if 0 < i[0] < LEVELS - 1 else []) + ([(f"yy{i}", "V")] if i[0] else []),
        "w": lambda: [(f"w{i}", "A")],
        "qg": lambda: [(f"gq{i}", "A")],
        "state_v": lambda: [(f"vn{i}", "A")],
        "state_o": lambda: ([(f"ds{i}", "V")] if i != S // CH - 1 else []) + [(f"o{i}", "A")],
        "delta_out": lambda: [(f"on{i}", "A")],
        "c_norm": lambda: [(f"cn{i}", "A")],
        "rope": lambda: [(f"rope{i}", "V"), (f"ropes{i}", "V")],
        "qn": lambda: [(f"qn{i}", "A")],
        "kn": lambda: [(f"kn{i}", "A")],
        "cv": lambda: [(f"cv{i}", "A")],
        "out": lambda: [(f"y{t}.{n}", "V") for t in range(T) for n in range(2)] if i == 15 else [],
    }.get(kind, list)()


TASKS = [t for s in STEPS for t in tasks_of(s)]
TASK_AT = {name: i for i, (name, _) in enumerate(TASKS)}
assert len(TASK_AT) == len(TASKS)


PARTIAL = [s for s in STEPS if s in [("mv", c) for c in range(3)] + [("out", n) for n in range(15)]]


def nth(kind, i):
    return [x for k, x in STEPS if k == kind].index(i) + 1


def freed(i):
    who = TASKS[i][1]
    return who, sum(w == who for _, w in TASKS[:i + 1])


def th_uses():
    uses = []
    for kind, i in STEPS:
        if kind == "gate":
            uses.append((f"gate {i}", "bank"))
        elif kind == "conv":
            if i:
                uses.append((f"conv{i - 1}", "th"))
            if i == 11:
                uses.append(("conv11", "th"))
        elif kind in ("l2", "qg", "delta_out", "c_norm"):
            uses.append((f"{kind}{i}", "th"))
    return uses


TH = th_uses()
TH_AT = {name: i for i, (name, _) in enumerate(TH)}


def sq_uses():
    uses = []
    for kind, i in STEPS:
        if kind == "square":
            group, j = i
            uses.append((f"sq {group}{j}", f"cn{j // 2}" if group == "c" else f"{group}{j}"))
    return uses


SQ = sq_uses()
SQ_AT = {name: i for i, (name, _) in enumerate(SQ)}

N_PARAM_ROWS = KD + KD + 2 + 1 + 1 + 12 * CONV
PRE, MEMN, CQN, CKVN, GDNN, CONVW = 0, KD, 2 * KD, 2 * KD + 2, 2 * KD + 3, 2 * KD + 4


class Memory:

    def __init__(self, nc, ctx):
        def sb(name, shape, dt=F32):
            return ctx.enter_context(nc.sbuf_tensor(name, shape, dt))

        self.consts = sb("consts", [P, CONSTS.shape[1]])
        self.x = sb("x_rows", [P, T, D])
        self.h_hi = sb("h_hi", [P, KD, S], F32R)
        self.h_lo = sb("h_lo", [P, KD, S], F32R)
        self.w_raw = sb("w_raw", [P, RAW_SLOTS, WC])
        self.w_hi = sb("w_hi", [P, SPLIT_SLOTS, WC], F32R)
        self.w_lo = sb("w_lo", [P, SPLIT_SLOTS, WC], F32R)
        self.mix = sb("mix", [P, 16, S])
        self.cosT = sb("cosT", [P, S])
        self.sinT = sb("sinT", [P, S])
        self.pad = sb("pad", [P, 2, S + 4])
        self.th = sb("th", [P, 2, S])
        self.sq = sb("sq", [P, 2, S])
        self.prow = sb("param_rows", [N_PARAM_ROWS, P])
        self.pcol = sb("param_cols", [P, N_PARAM_ROWS])
        self.stat = sb("stat", [P, 5, 2 * len(UNITS)])
        self.small = sb("small", [P, 352])
        self.arena = sb("arena", [P, 17920])
        self.alog, self.dtb, self.sink = self.small[:, 12:16], self.small[:, 16:20], self.small[:, 20:28]
        self.ss, self.lg, self.rstd = (self.small[:, 4 * i:4 * i + 4] for i in range(3))
        self.mem_hi, self.mem_lo = (self.h_lo[:, 4 * i:4 * i + 4, :].rearrange("p k s -> p (k s)").rearrange(
            "p (k c) -> p k c", k=KD) for i in range(2))
        self.ps = ctx.enter_context(nc.psum_tensor("ps", [P, BANKS, FB], F32))
        self._sem = lambda name: ctx.enter_context(nc.semaphore(name))

    def view(self, at, *shape):
        n = int(np.prod(shape))
        v = self.arena[:, at:at + n]
        if len(shape) == 2:
            v = v.rearrange("p (a b) -> p a b", b=shape[1])
        elif len(shape) == 3:
            v = v.rearrange("p (a b c) -> p a b c", b=shape[1], c=shape[2])
        return v

    def const(self, name):
        at, n = CONST_AT[name]
        return self.consts[:, at:at + n]


def heads(ap):
    return ap.rearrange("p (h c) -> p h c", h=NH)


def pieces(w, l, name, slot):
    def weights(src):
        return w[src][bass.ds(l, 1)]

    group, j = (name.split(".") + ["0"])[:2]
    j = int(j)
    n = 8 if name == "ab" else P
    grid = slot[:, 0:KD * n].rearrange("p (k c) -> p k c", k=KD)

    def cols(c0, n, at, src="w_in"):
        return grid[:, :, at:at + n], weights(src)[:, :, c0:c0 + n].rearrange("a (k p) c -> p (a k) c", p=P)

    if group == "mk":
        return [cols(j * P, P, 0, "mem_w_kv")]
    if group == "mv":
        return [(slot.rearrange("p (k c) -> p k c", k=2),
                 weights("mem_w_kv")[:, 2 * j * P:2 * (j + 1) * P, GW:2 * GW].rearrange("a (k p) c -> p (a k) c", p=P))]
    if group == "ckv":
        return [cols(OFF["c_kv"], P, 0)]
    if group == "kr":
        return [cols(OFF["c_kr"], ROPE, ROPE * i) for i in range(2)]
    if group == "krs":
        return [cols(OFF["c_kr"] + 32 * (1 - i % 2), 32, 32 * i) for i in range(4)]
    if group in ("ak", "av", "ab"):
        return [cols(OFF[{"ak": "a_k", "av": "a_v", "ab": "b_ab"}[group]], n, 0)]
    if group in ("a_q", "a_z"):
        return [cols(OFF[group] + 256 * half + 64 * j, 64, 64 * half) for half in range(2)]
    if group == "out":
        k = OUT_K[j]
        if k < 4:
            return [(slot[64 * half:64 * half + 64, :],
                     weights("w_out")[:, 256 * half + 64 * k:256 * half + 64 * k + 64, :].rearrange("a p c -> (a p) c"))
                    for half in range(2)]
        return [(slot, weights("w_out")[:, k * P:(k + 1) * P, :].rearrange("a p c -> (a p) c"))]
    return [cols(OFF[group] + j * P, P, 0)]


def load_rows(eng, m, w, l, sem):
    for name, at, n in (("norm_pre", PRE, KD), ("mem_norm", MEMN, KD), ("mla_q_norm", CQN, 2), ("mla_kv_norm", CKVN, 1),
                        ("gdn_norm", GDNN, 1)):
        eng.dma_start(m.prow[at:at + n, :], w[name][bass.ds(l, 1)].rearrange("a (k p) -> (a k) p", p=P)).then_inc(sem, 16)
    eng.dma_start(m.prow[CONVW:CONVW + 12 * CONV, :],
                  w["gdn_conv_w"][bass.ds(l, 1)].rearrange("a t (j p) -> (a t j) p", p=P)).then_inc(sem, 16)


def load_scalars(eng, m, w, l, sem):
    for dst, name in ((m.alog, "gdn_a_log"), (m.dtb, "gdn_dt_bias"), (m.sink, "attn_sinks")):
        eng.dma_start(dst, w[name][bass.ds(l, 1)].partition_broadcast(P).rearrange("p a c -> p (a c)")).then_inc(sem, 16)


def prologue(nc, m, w, ctx, args, bias_dram, mem_dram):
    x, mem, positions, rel_bias, consts = args
    sem = m._sem
    s_const, s_x, s_mem, s_pos, s_rb, s_bias_out = (sem(n) for n in (
        "const_in", "x_in", "mem_in", "pos_in", "rb_in", "bias_out"))
    s_rows, s_scal, s_chunk, s_hi, s_rest, s_memhi = (sem(n) for n in (
        "pro_rows_in", "pro_scalars_in", "pro_chunks_in", "pro_w_rounded", "pro_w_split", "pro_mem_rounded"))
    s_free_act, s_gained, s_memout, s_quads, s_rope = (sem(n) for n in (
        "pro_freed_by_act", "pro_mem_gained", "mem_out", "masked_quarters", "pro_rope_chain"))
    s_least, s_posi = sem("least_in"), sem("posi_in")
    s_chain, s_stat, s_mact, s_xs, s_steps, s_fill, s_free, s_trig, s_tab, s_sel, s_delta, s_zero, s_memlo = (sem(n) for n in (
        "pro_chain", "mem_sums", "mem_rstd", "mem_scaled", "steps_ready", "pro_filled", "pro_freed",
        "angles_ready", "trig_ready", "masked", "delta_ready", "rb_zero", "pro_mem_split"))

    SLAB = 64
    PER = 16
    steps = [m.arena[:, 4096 * b:4096 * (b + 1)].bitcast(BF16).rearrange("p (k q) -> p k q", q=P) for b in range(2)]
    stage = m.view(8192, 7, 8, P)
    memr = m.view(8192 + 7168, 2, D)
    hs = m.mix[:, 0:8, :].rearrange("p k s -> p (k s)")
    memT = m.mix[:, 8:12, :].rearrange("p k s -> p (k s)").rearrange("p (k c) -> p k c", k=KD)
    posi = hs[:, 0:512].bitcast(I32)
    posf = hs[:, 512:1024]
    wini = hs[:, 1024:1280].bitcast(I32)
    winf = hs[:, 1280:1536]
    ang, kk, red = hs[:, 1536:2048], hs[:, 2048:2560], hs[:, 2560:3072]
    ang2 = hs[:, 3072:3584]
    prod = m.th[:, 0, :]
    least = m.small[:, 38:40]
    rb, rbp, dl, r1, r2 = (hs[:, 3584 + 8 * i:3592 + 8 * i] for i in range(5))
    parts = hs[:, 3640:3652].bitcast(BF16)
    mem_gained = m.mix[:, 12:16, :].rearrange("p k s -> p (k s)").rearrange("p (k c) -> p k c", k=KD)
    junk = m.sq[:, :, :].rearrange("p a s -> p (a s)")
    ss, lg, rs = m.small[:, 32:34], m.small[:, 34:36], m.small[:, 36:38]

    queries = [slice(0, 64), slice(0, P), slice(0, P), slice(64, P)]
    bias_tasks = [("bias", sl, g, part) for sl in range(4) for g in range(1 if sl < 2 else 0, 4) for part in range(SLAB // PER)]
    n0 = sum(t[1] == 0 for t in bias_tasks)
    tasks = bias_tasks[:n0] + [("mem", mt, kh) for mt in range(2) for kh in range(2)] + [("params",)] + bias_tasks[n0:]
    n_halves = 7

    def freed(i):
        bias = tasks[i][0] == "bias"
        return s_free if bias else s_free_act, sum((t[0] == "bias") == bias for t in tasks[:i + 1])

    with nc.Block() as block:
        @block.sync
        def _(sp):
            for g in range(4):
                sp.dma_start(rb[32 * g:32 * g + 32, :], rel_bias[:, :]).then_inc(s_rb, 16)
            for g in range(4):
                lo = max(g - 1, 0) * P
                n = P if g == 0 else 2 * P
                sp.dma_start(wini[32 * g:32 * g + 32, 2 * P - n:2 * P],
                             positions[0:1, lo:lo + n].partition_broadcast(32).rearrange("p a s -> p (a s)")).then_inc(s_pos, 16)
            at = CONST_AT["bucket_least"][0]
            sp.dma_start(least, consts[:, at:at + 2]).then_inc(s_least, 16)
            sp.wait_ge(s_zero, 1)
            for g in range(4):
                sp.dma_start(rbp[32 * g + 1:32 * g + 32, :], rel_bias[0:BUCKETS - 1, :]).then_inc(s_rb, 16)
            sp.dma_start(posi, positions[0:1, :].partition_broadcast(P).rearrange("p a s -> p (a s)")).then_inc(s_posi, 16)
            sp.dma_start(m.consts[:, :], consts[:, :]).then_inc(s_const, 16)
            sp.dma_start(memr, mem[0].rearrange("(t p) d -> p t d", p=P)).then_inc(s_mem, 16)
            load_rows(sp, m, w, 0, s_rows)
            for i in range(RAW_SLOTS):
                for dst, src in pieces(w, 0, CHUNKS[i], m.w_raw[:, i, :]):
                    sp.dma_start(dst, src).then_inc(s_chunk, 16)
            sp.dma_start(m.x[:, :, :], x[0].rearrange("(t p) d -> p t d", p=P)).then_inc(s_x, 16)
            load_scalars(sp, m, w, 0, s_scal)
            sp.wait_ge(s_free_act, 4)
            sp.dma_start(mem_dram[:, :, :], memT).then_inc(s_memout, 16)
            n = 0
            for half in range(2):
                for g in range(1 - half, 4):
                    n += 1
                    sp.wait_ge(s_sel, n)
                    sp.dma_start(bias_dram[g, :, :, half * P:(half + 1) * P], stage[:, 2 * g + half - 1, :, :]).then_inc(s_bias_out, 16)
            sp.wait_ge(s_scal, 3 * 16)
            sp.wait_ge(s_chunk, RAW_SLOTS * 16)
            sp.wait_ge(s_memout, 16)
            sp.wait_ge(s_bias_out, 16 * n_halves)

        @block.gpsimd
        def _(pool):
            pool.memset(rbp, 0.0).then_inc(s_zero, 1)
            pool.memset(m.pad[:, :, 0:CONV - 1], 0.0).then_inc(s_zero, 1)
            pool.memset(stage[:, 1::2, :, 0:64], 0.0).then_inc(s_quads, 1)
            pool.memset(stage[:, 0::2, :, 64:P], 0.0).then_inc(s_quads, 1)

            n_links = [0]

            def link(ins):
                n_links[0] += 1
                ins.then_inc(s_rope, 1)
                pool.wait_ge(s_rope, n_links[0])

            pool.wait_ge(s_posi, 16)
            pool.wait_ge(s_const, 16)
            link(pool.tensor_copy(posf, posi))
            link(pool.tensor_scalar(red, posf, m.const("inv_freq"), None, ALU.mult))
            magic = float(1.5 * 2 ** 23)
            c1 = 6.28125
            c2 = float((np.array(np.float32(2 * math.pi - c1)).view(np.int32) & np.int32(-4096)).view(np.float32))
            c3 = float(np.float32(2 * math.pi - c1 - c2))
            for i, (dst, turn) in enumerate(((ang2, 0.25), (ang, 0.0))):
                link(pool.tensor_scalar(kk, red, float(1 / (2 * math.pi)), turn, ALU.mult, ALU.add))
                link(pool.tensor_scalar(kk, kk, magic, None, ALU.add))
                link(pool.tensor_scalar(kk, kk, magic, None, ALU.subtract))
                for c, src in ((c1, red), (c2, dst), (c3, dst)):
                    link(pool.tensor_scalar(prod, kk, c, None, ALU.mult))
                    link(pool.tensor_tensor(dst, src, prod, ALU.subtract))
                link(pool.tensor_scalar(dst, dst, turn * 2 * math.pi, 3.1415925, ALU.add, ALU.min))
                pool.tensor_scalar(dst, dst, -3.1415925, None, ALU.max).then_inc(s_trig, 1)
            for i in range(SPLIT_SLOTS):
                pool.wait_ge(s_hi, i + 1)
                pool.tensor_tensor(m.w_lo[:, i, :], m.w_raw[:, i, :], m.w_hi[:, i, :], ALU.subtract).then_inc(s_rest, 1)
            pool.wait_ge(s_tab, 2)
            pool.tensor_scalar(m.sinT[:, :], m.sinT[:, :], m.const("rope_sign"), None, ALU.mult).then_inc(s_rest, 1)
            pool.wait_ge(s_quads, 2)
            for half in range(2):
                for g in range(1 - half, 4):
                    last = max(i for i, t in enumerate(tasks) if t[0] == "bias" and t[1] // 2 == half and t[2] == g)
                    pool.wait_ge(*freed(last))
                    v = stage[:, 2 * g + half - 1, :, :]
                    if half == 0:
                        pool.affine_select(out=v, in_=v, pattern=[[0, 8], [1, P]], compare_op=ALU.is_gt, fill=NEG,
                                           base=0, channel_multiplier=-1).then_inc(s_sel, 1)
                    else:
                        pool.affine_select(out=v, in_=v, pattern=[[0, 8], [-1, P]], compare_op=ALU.is_ge, fill=NEG,
                                           base=0, channel_multiplier=1).then_inc(s_sel, 1)

        @block.scalar
        def _(act):
            act.wait_ge(s_mem, 16)
            for t in range(2):
                act.activation(junk, memr[:, t, :], ACT.Square, accum_out=ss[:, t:t + 1]).then_inc(s_stat, 1)
                act.wait_ge(s_stat, t + 1)
            act.wait_ge(s_const, 16)
            act.activation(lg, ss, ACT.Ln, scale=1.0 / D, bias=m.const("eps")).then_inc(s_stat, 1)
            act.wait_ge(s_stat, 3)
            act.activation(rs, lg, ACT.Exp, scale=-0.5).then_inc(s_mact, 1)
            act.wait_ge(s_chunk, RAW_SLOTS * 16)
            for i in range(SPLIT_SLOTS):
                act.activation(m.w_hi[:, i, :], m.w_raw[:, i, :], ACT.Copy).then_inc(s_hi, 1)
            act.wait_ge(s_x, 16)
            for t in range(T):
                act.activation(junk, m.x[:, t, :], ACT.Square, accum_out=m.ss[:, t:t + 1]).then_inc(s_stat, 1)
                act.wait_ge(s_stat, 4 + t)
            act.activation(m.lg, m.ss, ACT.Ln, scale=1.0 / D, bias=m.const("eps")).then_inc(s_stat, 1)
            act.wait_ge(s_stat, 4 + T)
            act.activation(m.rstd, m.lg, ACT.Exp, scale=-0.5).then_inc(s_stat, 1)
            for i, task in enumerate(tasks):
                bank = m.ps[:, i % BANKS, :]
                if task[0] == "mem":
                    _, mt, kh = task
                    act.wait_ge(s_fill, i + 1)
                    act.activation(memT[:, 4 * kh:4 * kh + 4, mt * P:(mt + 1) * P],
                                   bank.rearrange("p (k c) -> p k c", k=4), ACT.Copy).then_inc(s_free_act, 1)
                elif task[0] == "params":
                    act.wait_ge(s_fill, i + 1)
                    act.activation(m.pcol[:, :], bank[:, 0:N_PARAM_ROWS], ACT.Copy).then_inc(s_free_act, 1)
            act.wait_ge(s_gained, 1)
            act.activation(m.mem_hi, mem_gained, ACT.Copy).then_inc(s_memhi, 1)
            act.wait_ge(s_trig, 1)
            act.activation(m.cosT[:, :], ang2, ACT.Sin).then_inc(s_tab, 1)
            act.wait_ge(s_trig, 2)
            act.activation(m.sinT[:, :], ang, ACT.Sin).then_inc(s_tab, 1)

        @block.vector
        def _(dve):
            chain = [0]

            def link(ins):
                chain[0] += 1
                ins.then_inc(s_chain, 1)
                dve.wait_ge(s_chain, chain[0])

            dve.wait_ge(s_pos, 4 * 16)
            link(dve.tensor_copy(winf[:, P:2 * P], wini[:, P:2 * P]))
            for g in range(1, 4):
                link(dve.tensor_copy(winf[32 * g:32 * g + 32, 0:P], wini[32 * g:32 * g + 32, 0:P]))
            link(dve.tensor_copy(winf[0:32, 0:P], wini[0:32, P:2 * P]))
            dve.wait_ge(s_rb, 128)
            link(dve.tensor_tensor(dl, rb, rbp, ALU.subtract))
            link(dve.tensor_copy(parts[:, 0:8], dl))
            link(dve.tensor_tensor(r1, dl, parts[:, 0:8], ALU.subtract))
            link(dve.tensor_copy(parts[:, 8:16], r1))
            link(dve.tensor_tensor(r2, r1, parts[:, 8:16], ALU.subtract))
            dve.tensor_copy(parts[:, 16:24], r2).then_inc(s_delta, 1)
            dve.wait_ge(s_least, 16)

            def make_steps(sl):
                if sl >= 2:
                    done = [i for i, t in enumerate(tasks) if t[:2] == ("bias", sl - 2)]
                    dve.wait_ge(s_fill, done[-1] + 1)
                q = queries[sl]
                n = q.stop - q.start
                ins = dve.scalar_tensor_tensor(
                    out=steps[sl % 2][:, :, q],
                    in0=winf[:, SLAB * sl:SLAB * (sl + 1)].unsqueeze(2).to_broadcast([P, SLAB, n]), scalar=least[:, 0:1],
                    in1=winf[:, P + q.start:P + q.stop].unsqueeze(1).to_broadcast([P, SLAB, n]),
                    op0=ALU.add, op1=ALU.is_le)
                ins.then_inc(s_steps, 1)

            make_steps(0)
            make_steps(1)
            dve.wait_ge(s_mact, 1)
            for t in range(2):
                dve.tensor_scalar(memr[:, t, :], memr[:, t, :], rs[:, t:t + 1], None, ALU.mult).then_inc(s_xs, 1)
            made = 2
            dve.wait_ge(s_quads, 2)
            for i, task in enumerate(tasks):
                bank = m.ps[:, i % BANKS, :]
                if task[0] == "bias":
                    _, sl, g, part = task
                    if made == sl + 1 and made < 4:
                        make_steps(made)
                        made += 1
                        if made == 3:
                            dve.wait_ge(*freed(tasks.index(("params",))))
                            gain = m.pcol[:, MEMN:MEMN + KD].unsqueeze(2).to_broadcast([P, KD, MEM])
                            dve.tensor_tensor(mem_gained, memT, gain, ALU.mult).then_inc(s_gained, 1)
                        else:
                            dve.wait_ge(s_memhi, 1)
                            dve.tensor_tensor(m.mem_lo, mem_gained, m.mem_hi, ALU.subtract).then_inc(s_memlo, 1)
                    dve.wait_ge(s_fill, i + 1)
                    q = queries[sl]
                    k0 = (sl % 2) * SLAB + part * PER
                    dve.tensor_reduce(stage[q, 2 * g + sl // 2 - 1, :, k0:k0 + PER].rearrange("p h k -> p k h"),
                                      bank[q, 0:PER * 24].rearrange("p (k s h) -> p k h s", s=3, h=8),
                                      AX.X, ALU.add).then_inc(s_free, 1)

        @block.tensor
        def _(pe):
            for i, task in enumerate(tasks):
                bank = m.ps[:, i % BANKS, :]
                if i >= BANKS:
                    pe.wait_ge(*freed(i - BANKS))
                if task[0] == "mem":
                    _, mt, kh = task
                    pe.wait_ge(s_const, 16)
                    pe.wait_ge(s_xs, mt + 1)
                    for k in range(4):
                        last = pe.transpose(bank[:, k * P:(k + 1) * P], memr[:, mt, (4 * kh + k) * P:(4 * kh + k + 1) * P],
                                            m.const("ident"))
                    last.then_inc(s_fill, 1)
                    continue
                if task[0] == "params":
                    pe.wait_ge(s_rows, 6 * 16)
                    pe.transpose(bank[:, 0:N_PARAM_ROWS], m.prow[:, :],
                                 m.const("ident")[0:N_PARAM_ROWS, 0:N_PARAM_ROWS]).then_inc(s_fill, 1)
                    continue
                _, sl, g, part = task
                q = queries[sl]
                if i == 0:
                    pe.wait_ge(s_delta, 1)
                pe.wait_ge(s_steps, sl + 1)
                for k in range(PER):
                    last = pe.matmul(bank[q, 24 * k:24 * (k + 1)], steps[sl % 2][32 * g:32 * g + 32, part * PER + k, q],
                                     parts[32 * g:32 * g + 32, 0:24], start=True, stop=True)
                last.then_inc(s_fill, 1)


def layer(nc, m, l, w, bias_dram, mem_dram, layer_sems):
    following = (l + 1) % DEPTH
    (s_fill, s_act, s_dve, s_slot, s_hi, s_split, s_part, s_par, s_mem, s_uq, s_bias, s_gpost, s_scalars, s_xs,
     s_mhi, s_mfull, s_hhi, s_hlo, s_xhi, s_xlo, s_actc, s_dvec, s_neg, s_expA,
     s_norm, s_taps, s_th, s_thused, s_sq, s_ab, s_nabs, s_ln1p, s_g, s_dec, s_diff, s_exps,
     s_bt, s_sol0, s_mixB, s_cq0, s_rope, s_xfin, s_ysum, s_yadd, s_y) = layer_sems

    xs = m.view(0, T, D)
    junk = m.arena[:, 4096:5120]
    memT = m.view(5120, KD, MEM)
    mem_hi, mem_lo = m.mem_hi, m.mem_lo
    hf = m.view(13824, KD, S)
    mkT = m.view(7168, NH, MEM)
    mvr = m.view(8192, 2, GW)
    dqT = m.view(9216, NH, S)
    ptD = m.view(11264, 2, 2, S)
    qkvT = m.view(0, 12, S)
    kbg, kd, vb = (m.view(6144 + 2048 * i, T, NH, P) for i in range(3))
    LT = m.view(12288, T, NH * P)
    BT = m.view(14336, T, NH * P)
    state = m.view(16384, 2, NH * P)
    avr = m.view(17408, T, P)
    turning = {"av": m.arena[:, 16384:16896], "ab": m.arena[:, 16896:17408]}
    vnew = m.sq
    Xm, Ym = qkvT[:, 8:12, :], qkvT[:, 4:8, :]
    nwT = LT
    oT = kbg.rearrange("p t h c -> p t (h c)")
    Aqk = m.mix[:, 0:4, :]
    dec = m.mix[:, 8:12, :]
    cqT, ckvT = m.view(0, 2, S), m.arena[:, 1024:1536]
    qnT, qrT, knT = m.view(1536, NH, S), m.view(3584, 2, S), m.view(4608, NH, S)
    krT = m.arena[:, 6656:7168]
    cvr = m.view(7168, T, GW)
    pt = m.view(9216, 2, 4, S)
    craw = m.view(4096, 3, S)
    uqs = m.view(13312, 2, 2, P)
    uqr = m.mix[:, 3, :].rearrange("p (k b c) -> p k b c", k=2, b=2)
    ukv = m.arena[:, 13824:14848].rearrange("p (h c) -> p h c", h=NH)
    aqT, akT = m.view(14848, NH, S), m.arena[:, 16896:17408]
    uq = m.mix[:, 0:3, :].rearrange("p k s -> p (k s)").rearrange("p (k c) -> p k c", k=2)
    bias = m.h_lo[:, :, :].rearrange("p k s -> p (k s)").bitcast(F32).rearrange("p (b h c) -> p b h c", b=2, h=8)
    gpost = m.arena[:, 7168:8192]
    ytmp = m.view(8192, 2, S)
    prob_ca = [m.pad[:, i, CONV - 1:CONV - 1 + S] for i in range(2)] + [x[:, i, :] for x in (m.th, m.sq) for i in range(2)]
    prob_slots = {"D": [m.view(13312, 2, S)[:, i, :] for i in range(2)], "C": prob_ca, "A": prob_ca}

    sm = m.small
    ss, lg, rstd, alog, dtb, sink = m.ss, m.lg, m.rstd, m.alog, m.dtb, m.sink
    abr = sm[:, 32:64].rearrange("p (t c) -> p t c", t=T)
    tb, beta, xdt, mx, nabs, lnp, g16, ea = (sm[:, 64 + 16 * i:80 + 16 * i] for i in range(8))
    gc = sm[:, 192:224]
    gdiff, eg, ed, nbeg, vbs = (sm[:, 224 + 16 * i:240 + 16 * i] for i in range(5))
    gle = sm[:, 304:336].rearrange("p (t h c) -> p t h c", t=T, h=NH)
    ss2, lg2, rs2 = sm[:, 336:344], sm[:, 344:348], sm[:, 348:352]

    def th4(ap):
        return ap.rearrange("p (t h) -> p t h", t=T)

    def weights(name):
        return w[name][bass.ds(l, 1)]

    def done(name):
        who, n = freed(TASK_AT[name])
        return (s_act if who == "A" else s_dve), n

    def filled(name):
        return s_fill, TASK_AT[name] + 1

    def th_free(i):
        name, by = TH[i - 2]
        return done(name) if by == "bank" else used(name)

    def used(name):
        return s_thused, sum(by == "th" for _, by in TH[:TH_AT[name] + 1])

    def bank(name):
        return m.ps[:, TASK_AT[name] % BANKS, :]

    def segments(u):
        _, _, _, n, width = UNITS[u]
        return n, width

    def stats(row, u):
        return m.stat[:, row, 2 * u:2 * u + UNITS[u][3]]

    def mix_ready(n):
        k = OUT_K[n]
        if 4 <= k < 8:
            return s_mixB, k - 3
        return done({0: f"pv{len(GROUPS) - 1}", 2: f"pv{k - 4}", 3: f"pv{k - 12}"}[k // 4])

    def prob_of(u):
        return prob_slots[UNITS[u][0]][u % PROB_SLOTS[UNITS[u][0]]]

    def before_in_slot(u):
        v = u - PROB_SLOTS[UNITS[u][0]]
        return v if v >= (0 if UNITS[u][0] == "D" else 8) else None

    def user_done(chunk):
        step = CHUNK_USER[chunk]
        if chunk == "out.15":
            return filled("y3.1")
        if step in PARTIAL:
            return s_part, PARTIAL.index(step) + 1
        name = {"kr": "ropek", "krs": "ropesk"}.get(chunk) or tasks_of(step)[-1][0]
        return filled(name)

    n_chunks = len(CHUNKS)
    n_pieces = [len(pieces(w, 0, c, m.w_raw[:, 0, :])) for c in CHUNKS + CHUNKS[:RAW_SLOTS]]

    def wait_arrived(eng, i):
        if i >= RAW_SLOTS:
            eng.wait_ge(s_slot[i % RAW_SLOTS], 16 * sum(n_pieces[i % RAW_SLOTS + RAW_SLOTS:i + 1:RAW_SLOTS]))

    def wait_split(eng, i):
        if i >= SPLIT_SLOTS:
            eng.wait_ge(s_split, i - SPLIT_SLOTS + 1)

    def slots(i):
        n = KD * 8 if CHUNKS[i % n_chunks] == "ab" else WC
        return m.w_raw[:, i % RAW_SLOTS, 0:n], m.w_hi[:, i % SPLIT_SLOTS, 0:n], m.w_lo[:, i % SPLIT_SLOTS, 0:n]

    def chunks_behind(step):
        return [i + SPLIT_SLOTS for i, c in enumerate(CHUNKS) if CHUNK_USER[c] == step]

    def w_parts(chunk):
        i, n = CHUNKS.index(chunk), 8 if chunk == "ab" else P
        return [x[:, i % SPLIT_SLOTS, 0:KD * n].rearrange("p (k c) -> p k c", k=KD) for x in (m.w_hi, m.w_lo)]

    with nc.Block() as block:
        @block.sync
        def _(sp):
            for i in range(RAW_SLOTS, n_chunks + RAW_SLOTS):
                wait_split(sp, i - RAW_SLOTS)
                for dst, src in pieces(w, l if i < n_chunks else following, CHUNKS[i % n_chunks], m.w_raw[:, i % RAW_SLOTS, :]):
                    sp.dma_start(dst, src).then_inc(s_slot[i % RAW_SLOTS], 16)
                if i == 2 * RAW_SLOTS:
                    load_rows(sp, m, w, following, s_par)
                if i == CHUNKS.index("out.7"):
                    sp.wait_ge(*done(f"pv{len(GROUPS) - 1}"))
                    sp.dma_start(memT, mem_dram[:, :, :]).then_inc(s_mem, 16)
                    load_scalars(sp, m, w, following, s_scalars)
            sp.wait_ge(s_scalars, 3 * 16)
            for i in range(n_chunks, n_chunks + RAW_SLOTS):
                wait_arrived(sp, i)

        @block.gpsimd
        def _(pool):
            def rest(i):
                raw, hi, lo = slots(i)
                pool.wait_ge(s_hi, i - SPLIT_SLOTS + 1)
                pool.tensor_tensor(lo, raw, hi, ALU.subtract).then_inc(s_split, 1)

            def mask_level(lv, t):
                pool.wait_ge(*done(f"br{t}"))
                if lv:
                    pool.wait_ge(*filled(f"p{(lv - 1, t)}"))
                if lv == 1:
                    pool.wait_ge(s_sol0, t + 1)
                pool.tensor_tensor(heads(BT[:, t, :]), heads(LT[:, t, :]),
                                   m.const(f"level{lv}").unsqueeze(1).to_broadcast([P, NH, P]), ALU.mult).then_inc(s_bt, 1)

            for kind, i in STEPS:
                for c in chunks_behind((kind, i)):
                    rest(c)
                if kind == "chunk_products":
                    mask_level(0, i)
                elif kind == "solve_a" and i[0] < LEVELS - 1:
                    mask_level(i[0] + 1, i[1])

        @block.tensor
        def _(pe):
            ident, ones = m.const("ident"), m.const("ones")

            def open_bank(name):
                i = TASK_AT[name]
                if i >= BANKS:
                    who, n = freed(i - BANKS)
                    pe.wait_ge(s_act if who == "A" else s_dve, n)
                return bank(name)

            def passes(chunk, other_hi, other_lo, before_lo=None):
                hi, lo = w_parts(chunk)
                wait_split(pe, CHUNKS.index(chunk))
                yield hi, other_hi
                yield lo, other_hi
                if before_lo:
                    pe.wait_ge(*before_lo)
                yield hi, other_lo

            def project(out, chunk, rhs_hi, rhs_lo, before_lo=None):
                n = 0
                for wt, rhs in passes(chunk, rhs_hi, rhs_lo, before_lo):
                    for k in range(KD):
                        last = pe.matmul(out, wt[:, k, :], rhs[:, k, :], start=(n == 0), stop=(n == 3 * KD - 1))
                        n += 1
                return last

            for kind, i in STEPS:
                if kind == "params":
                    b = open_bank("params")
                    pe.wait_ge(s_par, 6 * 16)
                    pe.transpose(b[:, 0:N_PARAM_ROWS], m.prow[:, :], ident[0:N_PARAM_ROWS, 0:N_PARAM_ROWS]).then_inc(s_fill, 1)

                elif kind == "xt":
                    pe.wait_ge(s_xs, i + 1)
                    for kk in range(2):
                        b = open_bank(f"xt{i}.{kk}")
                        for k in range(4):
                            last = pe.transpose(b[:, k * P:(k + 1) * P], xs[:, i, (4 * kk + k) * P:(4 * kk + k + 1) * P], ident)
                        last.then_inc(s_fill, 1)

                elif kind in ("proj", "gate", "conv"):
                    chunk = f"b_{'qkv'[i // 4]}.{i % 4}" if kind == "conv" else i
                    b = open_bank(f"conv{i}" if kind == "conv" else f"{kind} {i}")
                    if chunk.startswith("mk"):
                        project(b[:, 0:MEM], chunk, mem_hi, mem_lo).then_inc(s_fill, 1)
                    else:
                        pe.wait_ge(s_hhi, T)
                        project(b, chunk, m.h_hi, m.h_lo, (s_hlo, T)).then_inc(s_fill, 1)

                elif kind == "mv":
                    if i == 0:
                        for mt in range(2):
                            open_bank(f"mv{mt}")
                    at = CHUNKS.index(f"mv.{i}")
                    hi, lo = (x.rearrange("p (k c) -> p k c", k=2) for x in slots(at)[1:])
                    wait_split(pe, at)
                    for mt in range(2):
                        ms = slice(mt * P, (mt + 1) * P)
                        for k in range(2):
                            b = bank(f"mv{mt}")
                            pe.matmul(b, mem_hi[:, 2 * i + k, ms], hi[:, k, :], start=(i == 0 and k == 0), stop=False)
                            pe.matmul(b, mem_hi[:, 2 * i + k, ms], lo[:, k, :], start=False, stop=False)
                            last = pe.matmul(b, mem_lo[:, 2 * i + k, ms], hi[:, k, :], start=False, stop=(i == 3 and k == 1))
                        if i == 3:
                            last.then_inc(s_fill, 1)
                    if i < 3:
                        last.then_inc(s_part, 1)

                elif kind == "av":
                    b = open_bank("avT")
                    project(b, "av", m.h_hi, m.h_lo).then_inc(s_fill, 1)

                elif kind == "ab":
                    b = open_bank("abT")
                    project(b[0:8, :], "ab", m.h_hi, m.h_lo).then_inc(s_fill, 1)

                elif kind in ("av_turn", "ab_turn"):
                    name, n = kind[:2], P if kind == "av_turn" else 8
                    b = open_bank(name)
                    pe.wait_ge(*done(f"{name}T"))
                    for t in range(T):
                        last = pe.transpose(b[:, t * n:(t + 1) * n], turning[name][0:n, t * P:(t + 1) * P], ident[0:n, 0:n])
                    last.then_inc(s_fill, 1)

                elif kind == "scores":
                    group, a, c, n, width = UNITS[i]
                    b = open_bank(f"scores{i}")
                    if group == "D":
                        pe.wait_ge(*done(f"proj d_q.{a}"))
                        for tl in range(2):
                            t = 2 * c + tl
                            last = pe.matmul(b[:, tl * MEM:(tl + 1) * MEM], dqT[:, a, t * P:(t + 1) * P], mkT[:, a, :],
                                             start=True, stop=True)
                    elif group == "C":
                        pe.wait_ge(*done(f"kn{a}"))
                        pe.wait_ge(s_rope, 3)
                        r = slice(64 * (a % 2), 64 * (a % 2) + 64)
                        pe.matmul(b[:, 0:width], qnT[:, a, c * P:(c + 1) * P], knT[:, a, 0:width], start=True, stop=False)
                        pe.matmul(b[:, width - P:width], ident, m.const("causal_neg"), start=False, stop=False)
                        last = pe.matmul(b[:, 0:width], qrT[r, a // 2, c * P:(c + 1) * P], krT[r, 0:width], start=False,
                                         stop=True)
                    else:
                        s, jp = divmod(c, 2)
                        pe.wait_ge(*done("proj a_q.3"))
                        pe.wait_ge(*done("proj ak"))
                        r = slice(64 * s, 64 * s + 64)
                        k1 = (a + 1) * P
                        for jj in range(2):
                            last = pe.matmul(b[:, jj * width:(jj + 1) * width], aqT[r, 2 * jp + jj, a * P:(a + 1) * P],
                                             akT[r, k1 - width:k1], start=True, stop=True)
                    last.then_inc(s_fill, 1)

                elif kind == "turn":
                    group, a, c, n, width = UNITS[i]
                    b = open_bank(f"turn{i}")
                    pe.wait_ge(s_norm, i + 1)
                    p = prob_of(i)
                    nb = width // P
                    for seg in range(n):
                        for j in range(nb):
                            at = seg * P + j * n * P
                            last = pe.transpose(b[:, at:at + P], p[:, seg * width + j * P:seg * width + (j + 1) * P], ident)
                    last.then_inc(s_fill, 1)

                elif kind == "pv":
                    group, a = GROUPS[i]
                    b = open_bank(f"pv{i}")
                    pe.wait_ge(*done(f"turn{LAST_UNIT[i]}"))
                    if group == "D":
                        for mt in range(2):
                            last = pe.matmul(b, mvr[:, mt, a * P:(a + 1) * P], ptD[:, i % 2, mt, :], start=(mt == 0), stop=(mt == 1))
                    elif group == "C":
                        for j in range(T):
                            last = pe.matmul(b[:, j * P:S], cvr[:, j, a * P:(a + 1) * P], pt[:, 0, j, j * P:S],
                                             start=(j == 0), stop=True, skip_group_check=(j > 0))
                    else:
                        ptv = pt[:, 1, :, :].rearrange("p (s f) c -> p s f c", s=2)
                        pe.wait_ge(*done("av"))
                        for s in range(2):
                            r = slice(64 * s, 64 * s + 64)
                            for half in range(0 if a else 1, 2):
                                last = pe.matmul(b[r, :], avr[:, a - 1 + half, r], ptv[:, s, half, :],
                                                 start=(half == 0 or a == 0), stop=(half == 1))
                    last.then_inc(s_fill, 1)

                elif kind == "cum":
                    b = open_bank("cum")
                    pe.wait_ge(s_g, 1)
                    pe.matmul(b[:, 0:16], m.const("upto"), g16, start=True, stop=True)
                    pe.matmul(b[:, 16:32], m.const("chunk"), g16, start=True, stop=True).then_inc(s_fill, 1)

                elif kind == "l2":
                    b = open_bank(f"l2.{i}")
                    at = SQ_AT[f"sq l2.{i}"]
                    pe.wait_ge(s_sq, at + 1)
                    pe.matmul(b, ones, m.sq[:, at % 2, :], start=True, stop=True).then_inc(s_fill, 1)

                elif kind == "decay":
                    b = open_bank(f"gr{i}")
                    for h in range(NH):
                        g = g16[:, 4 * i + h:4 * i + h + 1]
                        last = pe.matmul(b[:, h * P:(h + 1) * P], g.to_broadcast([P, P]), m.const("upto"), start=True, stop=True)
                    last.then_inc(s_fill, 1)

                elif kind == "chunk_rows":
                    for name, first, ready in ((f"krows{i}", 4, "l27"), (f"vrows{i}", 8, "conv11")):
                        b = open_bank(name)
                        pe.wait_ge(*used(ready))
                        for h in range(NH):
                            last = pe.transpose(b[:, h * P:(h + 1) * P], qkvT[:, first + h, i * P:(i + 1) * P], ident)
                        last.then_inc(s_fill, 1)

                elif kind == "chunk_products":
                    tc = slice(i * P, (i + 1) * P)
                    b = open_bank(f"kk{i}")
                    for h in range(NH):
                        last = pe.matmul(b[:, h * P:(h + 1) * P], qkvT[:, 4 + h, tc], qkvT[:, 4 + h, tc], start=True, stop=True)
                    last.then_inc(s_fill, 1)
                    b = open_bank(f"br{i}")
                    for h in range(NH):
                        bc = beta[:, 4 * i + h:4 * i + h + 1]
                        last = pe.matmul(b[:, h * P:(h + 1) * P], bc.to_broadcast([P, P]), ident, start=True, stop=True)
                    last.then_inc(s_fill, 1)
                    b = open_bank(f"qk{i}")
                    pe.wait_ge(*used("l23"))
                    for h in range(NH):
                        last = pe.matmul(b[:, h * P:(h + 1) * P], qkvT[:, 4 + h, tc], qkvT[:, h, tc], start=True, stop=True)
                    last.then_inc(s_fill, 1)

                elif kind == "solve_a":
                    lv, t = i
                    b = open_bank(f"p{i}")
                    pe.wait_ge(s_bt, nth("solve_a", i))
                    if lv == 1:
                        pe.wait_ge(s_sol0, t + 1)
                    if lv > 1:
                        pe.wait_ge(*done(f"xx{(lv - 1, t)}"))
                    for h in range(NH):
                        hc = slice(h * P, (h + 1) * P)
                        last = pe.matmul(b[:, hc], BT[:, t, hc], Xm[:, t, hc] if lv else ident, start=True, stop=True)
                    last.then_inc(s_fill, 1)

                elif kind == "solve_b":
                    lv, t = i
                    if lv == 0:
                        continue
                    pe.wait_ge(*done(f"p{i}"))
                    if lv > 1:
                        pe.wait_ge(*done(f"yy{(lv - 1, t)}"))
                    if lv < LEVELS - 1:
                        b = open_bank(f"xx{i}")
                        for h in range(NH):
                            hc = slice(h * P, (h + 1) * P)
                            last = pe.matmul(b[:, hc], Ym[:, t, hc], dec[:, t, hc], start=True, stop=True)
                        last.then_inc(s_fill, 1)
                    b = open_bank(f"yy{i}")
                    for h in range(NH):
                        hc = slice(h * P, (h + 1) * P)
                        last = pe.matmul(b[:, hc], dec[:, t, hc], Ym[:, t, hc], start=True, stop=True)
                    last.then_inc(s_fill, 1)

                elif kind == "w":
                    b = open_bank(f"w{i}")
                    pe.wait_ge(*done(f"krows{i}"))
                    pe.wait_ge(*done(f"yy{(LEVELS - 1, i)}"))
                    for h in range(NH):
                        last = pe.matmul(b[:, h * P:(h + 1) * P], kbg[:, i, h, :], Ym[:, i, h * P:(h + 1) * P], start=True, stop=True)
                    last.then_inc(s_fill, 1)

                elif kind == "qg":
                    b = open_bank(f"gq{i}")
                    for h in range(NH):
                        g = g16[:, 4 * i + h:4 * i + h + 1]
                        last = pe.matmul(b[:, h * P:(h + 1) * P], g.to_broadcast([P, P]), m.const("upto"), start=True, stop=True)
                    last.then_inc(s_fill, 1)

                elif kind == "state_v":
                    t, r, c0 = i // 2, slice(CH * (i % 2), CH * (i % 2) + CH), CH * (i % 2)
                    b = open_bank(f"vn{i}")
                    pe.wait_ge(*done(f"vrows{t}"))
                    pe.wait_ge(*done(f"w{t}"))
                    if i:
                        pe.wait_ge(*done(f"ds{i - 1}"))
                    for h in range(NH):
                        hc = slice(h * P, (h + 1) * P)
                        last = pe.matmul(b[r, hc], Ym[r, t, h * P + c0:h * P + c0 + CH], vb[r, t, h, :], start=True, stop=(i == 0))
                        if i:
                            last = pe.matmul(b[r, hc], nwT[:, t, h * P + c0:h * P + c0 + CH], state[:, i % 2, hc], start=False, stop=True)
                    last.then_inc(s_fill, 1)

                elif kind == "state_o":
                    t, r, c0 = i // 2, slice(CH * (i % 2), CH * (i % 2) + CH), CH * (i % 2)
                    pe.wait_ge(*done(f"vn{i}"))
                    if i < S // CH - 1:
                        b = open_bank(f"ds{i}")
                        for h in range(NH):
                            hc = slice(h * P, (h + 1) * P)
                            last = pe.matmul(b[:, hc], kd[r, t, h, :], vnew[r, i % 2, hc], start=True, stop=True)
                        last.then_inc(s_fill, 1)
                    b = open_bank(f"o{i}")
                    pe.wait_ge(*used(f"qg{t}"))
                    for h in range(NH):
                        hc, oc = slice(h * P, (h + 1) * P), slice(h * CH, (h + 1) * CH)
                        if i:
                            pe.matmul(b[:, oc], state[:, i % 2, hc], qkvT[:, h, i * CH:(i + 1) * CH], start=True, stop=False)
                        last = pe.matmul(b[:, oc], vnew[r, i % 2, hc], Aqk[r, t, h * P + c0:h * P + c0 + CH],
                                         start=(i == 0), stop=True)
                    last.then_inc(s_fill, 1)

                elif kind == "delta_out":
                    b = open_bank(f"on{i}")
                    at = SQ_AT[f"sq on{i}"]
                    pe.wait_ge(s_sq, at + 1)
                    pe.matmul(b, ones, m.sq[:, at % 2, :], start=True, stop=True).then_inc(s_fill, 1)

                elif kind == "c_norm":
                    b = open_bank(f"cn{i}")
                    names = ("sq c0", "sq c1") if i == 0 else ("sq c2",)
                    for n, name in enumerate(names):
                        at = SQ_AT[name]
                        pe.wait_ge(s_sq, at + 1)
                        last = pe.matmul(b, ones, m.sq[:, at % 2, :], start=(n == 0), stop=(n == len(names) - 1))
                    last.then_inc(s_fill, 1)

                elif kind == "rope":
                    if i == "k":
                        for task, chunk in (("ropek", "kr"), ("ropesk", "krs")):
                            b = open_bank(task)
                            project(b, chunk, m.h_hi, m.h_lo).then_inc(s_fill, 1)
                    else:
                        pe.wait_ge(s_uq, 8 * 16)
                        pe.wait_ge(*used("c_norm0"))
                        for task in (f"rope{i}", f"ropes{i}"):
                            b = open_bank(task)
                            for k in range(2):
                                lhs = (uqr if task == f"rope{i}" else uqs)[:, k, i, :]
                                last = pe.matmul(b, lhs, cqT[:, k, :], start=(k == 0), stop=(k == 1))
                            last.then_inc(s_fill, 1)

                elif kind == "qn":
                    b = open_bank(f"qn{i}")
                    pe.wait_ge(s_uq, 8 * 16)
                    pe.wait_ge(*used("c_norm0"))
                    for k in range(2):
                        last = pe.matmul(b, uq[:, k, i * (NOPE + ROPE):i * (NOPE + ROPE) + NOPE], cqT[:, k, :],
                                         start=(k == 0), stop=(k == 1))
                    last.then_inc(s_fill, 1)

                elif kind == "kn":
                    b = open_bank(f"kn{i}")
                    pe.wait_ge(*used("c_norm1"))
                    pe.matmul(b, ukv[:, i, 0:NOPE], ckvT, start=True, stop=True).then_inc(s_fill, 1)

                elif kind == "cv":
                    b = open_bank(f"cv{i}")
                    pe.matmul(heads(b), ckvT[:, i * P:(i + 1) * P], ukv[:, :, NOPE:2 * NOPE], start=True, stop=True).then_inc(s_fill, 1)

                elif kind == "out":
                    if i == 0:
                        for t in range(T):
                            for n in range(2):
                                open_bank(f"y{t}.{n}")
                    x_hi, x_lo = (m.h_hi[:, 2 * (i % MIX_SLOTS) + j, :] for j in range(2))
                    w_hi, w_lo = m.w_hi[:, CHUNKS.index(f"out.{i}") % SPLIT_SLOTS, :], m.w_lo[:, CHUNKS.index(f"out.{i}") % SPLIT_SLOTS, :]
                    wait_split(pe, CHUNKS.index(f"out.{i}"))
                    pe.wait_ge(s_xlo, i + 1)
                    for t in range(T):
                        rows = slice(t * P, (t + 1) * P)
                        for n in range(2):
                            b, c = bank(f"y{t}.{n}"), slice(n * FB, (n + 1) * FB)
                            pe.matmul(b, x_hi[:, rows], w_hi[:, c], start=(i == 0), stop=False)
                            pe.matmul(b, x_hi[:, rows], w_lo[:, c], start=False, stop=False)
                            last = pe.matmul(b, x_lo[:, rows], w_hi[:, c], start=False, stop=(i == 15))
                            if i == 15:
                                last.then_inc(s_fill, 1)
                    if i < 15:
                        last.then_inc(s_part, 1)

        @block.scalar
        def _(act):
            chain = [0]

            def link(ins):
                chain[0] += 1
                ins.then_inc(s_actc, 1)
                act.wait_ge(s_actc, chain[0])

            eps = m.const("eps")

            def tanh_half(src, name, first_wait):
                at = TH_AT[name]
                act.wait_ge(*first_wait)
                if at >= 2:
                    act.wait_ge(*th_free(at))
                act.activation(m.th[:, at % 2, :], src, ACT.Tanh, scale=0.5).then_inc(s_th, 1)

            def square(group, j):
                name = f"sq {group}{j}"
                at = SQ_AT[name]
                if group == "l2.":
                    act.wait_ge(*used(f"conv{j}"))
                    src = qkvT[:, j, :]
                elif group == "on":
                    act.wait_ge(*done(f"o{S // CH - 1}"))
                    src = oT[:, j, :]
                else:
                    act.wait_ge(*done(f"proj {('c_q.0', 'c_q.1', 'ckv')[j]}"))
                    src = craw[:, j, :]
                if at >= 2:
                    act.wait_ge(*filled(SQ[at - 2][1]))
                act.activation(m.sq[:, at % 2, :], src, ACT.Square).then_inc(s_sq, 1)

            def inv_root(task, name, scale):
                at = TH_AT[name]
                act.wait_ge(*filled(task))
                act.wait_ge(*th_free(at))
                act.activation(m.th[:, at % 2, :], bank(task), ACT.Ln, scale=scale, bias=eps).then_inc(s_act, 1)
                act.wait_ge(*done(task))
                act.activation(m.th[:, at % 2, :], m.th[:, at % 2, :], ACT.Exp, scale=-0.5).then_inc(s_th, 1)

            def load_uq():
                act.dma_start(uq, weights("mla_w_uq").rearrange("a (k p) c -> p (a k) c", p=P)).then_inc(s_uq, 16)
                for k in range(2):
                    src = weights("mla_w_uq")[:, k * P:(k + 1) * P, :].rearrange("a p (h c) -> p (a h) c", h=NH)
                    swapped, plain = (x[:, k, :, :].rearrange("p b c -> p (b c)").rearrange("p (h c) -> p h c", h=NH) for x in (uqs, uqr))
                    for half in range(2):
                        c0 = NOPE + 32 * (1 - half)
                        act.dma_start(swapped[:, :, 32 * half:32 * half + 32], src[:, :, c0:c0 + 32]).then_inc(s_uq, 16)
                    act.dma_start(plain, src[:, :, NOPE:NOPE + ROPE]).then_inc(s_uq, 16)
                act.dma_start(ukv.rearrange("p h c -> p (h c)"), weights("mla_w_ukv").rearrange("a p c -> p (a c)")).then_inc(s_uq, 16)

            def load_bias(blk):
                lo = P if blk == 0 else 0
                act.dma_start(bias[:, blk % 2, :, lo:2 * P], bias_dram[blk, :, :, lo:2 * P]).then_inc(s_bias[blk % 2], 16)

            def copy(task, dst, src, scale=1.0):
                act.wait_ge(*filled(task))
                act.activation(dst, src, ACT.Copy, scale=scale).then_inc(s_act, 1)

            def round_chunk(i):
                raw, hi, _ = slots(i)
                wait_arrived(act, i)
                act.wait_ge(*user_done(CHUNKS[i - SPLIT_SLOTS]))
                act.activation(hi, raw, ACT.Copy).then_inc(s_hi, 1)

            for kind, i in STEPS:
                if kind == "params":
                    act.wait_ge(*used("c_norm1"))
                    copy("params", m.pcol[:, :], bank("params")[:, 0:N_PARAM_ROWS])

                elif kind == "memory":
                    act.wait_ge(s_mfull, 1)
                    act.activation(mem_hi, memT, ACT.Copy).then_inc(s_mhi, 1)

                elif kind == "proj":
                    group, j = (i.split(".") + ["0"])[:2]
                    j = int(j)
                    b = bank(f"proj {i}")
                    if group == "mk":
                        copy(f"proj {i}", mkT[:, j, :], b[:, 0:MEM])
                    else:
                        dst = {"d_q": dqT[:, j, :], "c_q": craw[:, min(j, 1), :], "ckv": craw[:, 2, :], "ak": akT,
                               "a_q": aqT[:, j, :]}[group]
                        copy(f"proj {i}", dst, b, SWA_D ** -0.5 if group == "a_q" else 1.0)

                elif kind == "mv":
                    act.wait_ge(*done(f"xt{i}.1"))
                    act.activation(m.h_hi[:, :, i * P:(i + 1) * P], hf[:, :, i * P:(i + 1) * P], ACT.Copy).then_inc(s_hhi, 1)
                    if i == 3:
                        for mt in range(2):
                            copy(f"mv{mt}", mvr[:, mt, :], bank(f"mv{mt}"))

                elif kind == "gate":
                    tanh_half(bank(f"gate {i}"), f"gate {i}", filled(f"gate {i}"))
                    if i == "a_z.3":
                        load_bias(0)
                        load_bias(1)

                elif kind == "scores":
                    n, width = segments(i)
                    group = UNITS[i][0]
                    act.wait_ge(s_neg, i + 1)
                    if i == 8:
                        act.wait_ge(*done("gate a_z.3"))
                    if group != "A" and before_in_slot(i) is not None:
                        act.wait_ge(*filled(f"turn{before_in_slot(i)}"))
                    for seg in range(n):
                        cs = slice(seg * width, (seg + 1) * width)
                        src = prob_of(i)[:, cs] if group == "A" else bank(f"scores{i}")[:, cs]
                        ins = act.activation(prob_of(i)[:, cs], src, ACT.Exp, scale=SCALE[group],
                                             bias=stats(1, i)[:, seg:seg + 1], accum_out=stats(2, i)[:, seg:seg + 1])
                    if group == "A":
                        act.activation(stats(3, i), stats(3, i), ACT.Exp).then_inc(s_expA, 1)
                    else:
                        ins.then_inc(s_act, 1)

                elif kind == "turn":
                    group, a, c, n, width = UNITS[i]
                    g = GROUP_OF[i]
                    act.wait_ge(*filled(f"turn{i}"))
                    before = g - (2 if group == "D" else 1)
                    if i == FIRST_UNIT[g] and before >= 0 and GROUPS[before][0] == group:
                        act.wait_ge(*filled(f"pv{before}"))
                    nb = width // P
                    src = bank(f"turn{i}")[:, 0:nb * n * P].rearrange("p (j c) -> p j c", j=nb)
                    if group == "D":
                        dst = ptD[:, g % 2, :, 2 * c * P:(2 * c + 2) * P]
                    elif group == "C":
                        dst = pt[:, 0, 0:nb, c * P:(c + 1) * P]
                    else:
                        s, jp = divmod(c, 2)
                        dst = pt[:, 1, 2 * s + 2 - nb:2 * s + 2, 2 * jp * P:(2 * jp + 2) * P]
                    act.activation(dst, src, ACT.Copy).then_inc(s_act, 1)

                elif kind == "pv":
                    group, a = GROUPS[i]
                    if group == "A" and a + 2 < T:
                        act.wait_ge(*done(f"scores{LAST_UNIT[i]}"))
                        load_bias(a + 2)

                elif kind == "conv":
                    if i >= 2:
                        act.wait_ge(s_taps, i - 1)
                    copy(f"conv{i}", m.pad[:, i % 2, CONV - 1:CONV - 1 + S], bank(f"conv{i}"))
                    if i:
                        tanh_half(qkvT[:, i - 1, :], f"conv{i - 1}", (s_taps, i))
                    if i == 11:
                        tanh_half(qkvT[:, 11, :], "conv11", (s_taps, 12))

                elif kind == "av":
                    copy("avT", turning["av"], bank("avT"))

                elif kind == "ab":
                    copy("abT", turning["ab"][0:8, :], bank("abT")[0:8, :])

                elif kind == "av_turn":
                    copy("av", avr.rearrange("p t c -> p (t c)"), bank("av"))

                elif kind == "ab_turn":
                    copy("ab", sm[:, 32:64], bank("ab")[:, 0:32])

                elif kind == "log_decay":
                    act.wait_ge(*done("ab"))
                    act.activation(th4(tb), abr[:, :, 4:8], ACT.Exp, scale=-1.0).then_inc(s_ab, 1)
                    act.activation(ea[:, 0:4], alog, ACT.Exp).then_inc(s_ab, 1)
                    act.wait_ge(s_nabs, 1)
                    link(act.activation(lnp, nabs, ACT.Exp))
                    act.activation(lnp, lnp, ACT.Ln, bias=1.0).then_inc(s_ln1p, 1)

                elif kind == "cum":
                    act.wait_ge(s_diff, 1)
                    act.activation(eg, gc[:, 0:16], ACT.Exp)
                    act.activation(ed, gdiff, ACT.Exp).then_inc(s_exps, 1)

                elif kind == "square":
                    if i in (("l2.", 4), ("on", 0)):
                        act.preload_act_table_set(LN_EXP)
                    square(*i)
                    if i == ("on", 1):
                        load_uq()

                elif kind == "l2":
                    inv_root(f"l2.{i}", f"l2{i}", 0.25)

                elif kind == "decay":
                    act.wait_ge(*done(f"gr{i}"))
                    act.activation(dec[:, i, :], dec[:, i, :], ACT.Exp).then_inc(s_dec, 1)

                elif kind == "solve_a":
                    lv, t = i
                    if lv == 0:
                        act.wait_ge(*done(f"qk{t}"))
                    elif lv == 1:
                        act.wait_ge(s_sol0, t + 1)
                    elif lv > 1:
                        act.wait_ge(*filled(f"yy{(lv - 1, t)}"))
                    copy(f"p{i}", dec[:, t, :], bank(f"p{i}"))

                elif kind == "w":
                    copy(f"w{i}", nwT[:, i, :], bank(f"w{i}"))

                elif kind == "qg":
                    at = TH_AT[f"qg{i}"]
                    act.wait_ge(*th_free(at))
                    act.wait_ge(*filled(f"gq{i}"))
                    act.activation(m.th[:, at % 2, :], bank(f"gq{i}"), ACT.Exp).then_inc(s_act, 1)

                elif kind == "state_v":
                    r = slice(CH * (i % 2), CH * (i % 2) + CH)
                    if i >= 2:
                        act.wait_ge(*filled(f"o{i - 2}"))
                    copy(f"vn{i}", vnew[r, i % 2, :], bank(f"vn{i}")[r, :])

                elif kind == "state_o":
                    copy(f"o{i}", oT[:, :, i * CH:(i + 1) * CH], bank(f"o{i}")[:, 0:NH * CH].rearrange("p (h c) -> p h c", h=NH))

                elif kind == "delta_out":
                    inv_root(f"on{i}", f"delta_out{i}", 1.0 / P)

                elif kind == "c_norm":
                    inv_root(f"cn{i}", f"c_norm{i}", 1.0 / (2 * P if i == 0 else P))

                elif kind in ("qn", "kn", "cv"):
                    if (kind, i) == ("kn", 0):
                        act.wait_ge(s_mixB, NH)
                    dst = {"qn": qnT, "kn": knT, "cv": cvr}[kind][:, i, :]
                    copy(f"{kind}{i}", dst, bank(f"{kind}{i}"))

                elif kind == "mix_split":
                    if i == 0:
                        act.wait_ge(*filled(f"pv{len(GROUPS) - 1}"))
                        act.dma_start(gpost, weights("norm_post").partition_broadcast(P).rearrange("p a c -> p (a c)")).then_inc(s_gpost, 16)
                    act.wait_ge(*mix_ready(i))
                    if i >= MIX_SLOTS:
                        act.wait_ge(s_part, PARTIAL.index(("out", i - MIX_SLOTS)) + 1)
                    act.activation(m.h_hi[:, 2 * (i % MIX_SLOTS), :], m.mix[:, OUT_K[i], :], ACT.Copy).then_inc(s_xhi, 1)

                elif kind == "residual":
                    if i == 0:
                        act.preload_act_table_set(LN_EXP)
                    if i < T:
                        for n in range(2):
                            act.wait_ge(*filled(f"y{i}.{n}"))
                            act.activation(junk[:, 0:FB], bank(f"y{i}.{n}"), ACT.Square,
                                           accum_out=ss2[:, 2 * i + n:2 * i + n + 1]).then_inc(s_ysum, 1)
                            act.wait_ge(s_ysum, 2 * i + n + 1)
                    t = i - 1
                    if 0 <= t < T:
                        act.wait_ge(s_yadd, t + 1)
                        link(act.activation(rs2[:, t:t + 1], lg2[:, t:t + 1], ACT.Ln, scale=1.0 / D, bias=eps))
                        act.activation(rs2[:, t:t + 1], rs2[:, t:t + 1], ACT.Exp, scale=-0.5).then_inc(s_y, 1)
                    t = i - 2
                    if 0 <= t < T:
                        act.wait_ge(s_xfin, 2 * t + 2)
                        link(act.activation(junk, m.x[:, t, :], ACT.Square, accum_out=ss[:, t:t + 1]))
                    if i == T + 1:
                        link(act.activation(lg, ss, ACT.Ln, scale=1.0 / D, bias=eps))
                        link(act.activation(rstd, lg, ACT.Exp, scale=-0.5))

                for c in chunks_behind((kind, i)):
                    round_chunk(c)

        @block.vector
        def _(dve):
            chain = [0]

            def link(ins):
                chain[0] += 1
                ins.then_inc(s_dvec, 1)
                dve.wait_ge(s_dvec, chain[0])

            def th(name):
                at = TH_AT[name]
                if name.startswith("qg"):
                    dve.wait_ge(*done(f"gq{name[2:]}"))
                else:
                    dve.wait_ge(s_th, sum(not x.startswith("qg") for x, _ in TH[:at + 1]))
                return m.th[:, at % 2, :]

            def col(i):
                return m.pcol[:, i:i + 1]

            def over_free(cols, n=P):
                return cols.unsqueeze(2).to_broadcast([P, cols.shape[1], n])

            def silu2(j):
                dve.wait_ge(s_taps, j + 1)
                t = th(f"conv{j}")
                dve.scalar_tensor_tensor(out=qkvT[:, j, :], in0=t, scalar=1.0, in1=qkvT[:, j, :],
                                         op0=ALU.add, op1=ALU.mult).then_inc(s_thused, 1)

            def l2_scale(j):
                t = th(f"l2{j}")
                dve.scalar_tensor_tensor(out=qkvT[:, j, :], in0=qkvT[:, j, :], scalar=0.5 * (float(P) ** -0.5 if j < 4 else 1.0),
                                         in1=t, op0=ALU.mult, op1=ALU.mult).then_inc(s_thused, 1)

            def delta_gate(h):
                t = th(f"delta_out{h}")
                dve.scalar_tensor_tensor(out=oT[:, h, :], in0=oT[:, h, :], scalar=col(GDNN), in1=t,
                                         op0=ALU.mult, op1=ALU.mult).then_inc(s_thused, 1)
                dve.wait_ge(*used(f"delta_out{h}"))
                dve.wait_ge(*done(f"gate b_z.{h}"))
                dve.scalar_tensor_tensor(out=m.mix[:, 4 + h, :], in0=oT[:, h, :], scalar=0.5, in1=m.mix[:, 4 + h, :],
                                         op0=ALU.mult, op1=ALU.mult).then_inc(s_mixB, 1)

            for kind, i in STEPS:
                if kind == "memory":
                    dve.wait_ge(*done("params"))
                    dve.wait_ge(s_mem, 16)
                    dve.tensor_tensor(memT, memT, over_free(m.pcol[:, MEMN:MEMN + KD], MEM), ALU.mult).then_inc(s_mfull, 1)
                    dve.wait_ge(s_mfull, 1)
                    dve.wait_ge(s_mhi, 1)
                    link(dve.tensor_tensor(mem_lo, memT, mem_hi, ALU.subtract))

                elif kind == "xt":
                    if i == 0:
                        for t in range(T):
                            dve.tensor_scalar(xs[:, t, :], m.x[:, t, :], rstd[:, t:t + 1], None, ALU.mult).then_inc(s_xs, 1)
                    for kk in range(2):
                        dve.wait_ge(*filled(f"xt{i}.{kk}"))
                        dve.tensor_tensor(hf[:, 4 * kk:4 * kk + 4, i * P:(i + 1) * P], heads(bank(f"xt{i}.{kk}")),
                                          over_free(m.pcol[:, PRE + 4 * kk:PRE + 4 * kk + 4]), ALU.mult).then_inc(s_dve, 1)

                elif kind == "h_split":
                    dve.wait_ge(*filled("mv1"))
                    for t in range(T):
                        tc = slice(t * P, (t + 1) * P)
                        dve.wait_ge(s_hhi, t + 1)
                        dve.tensor_tensor(m.h_lo[:, :, tc], hf[:, :, tc], m.h_hi[:, :, tc], ALU.subtract).then_inc(s_hlo, 1)

                elif kind == "gate":
                    t = th(f"gate {i}")
                    dve.scalar_tensor_tensor(out=m.mix[:, MIX_AT[i], :], in0=t, scalar=1.0, in1=bank(f"gate {i}"),
                                             op0=ALU.add, op1=ALU.mult).then_inc(s_dve, 1)

                elif kind == "scores":
                    group, a, c, _, _ = UNITS[i]
                    n, width = segments(i)
                    b = bank(f"scores{i}")[:, 0:n * width].rearrange("p (s k) -> p s k", s=n)
                    dve.wait_ge(*filled(f"scores{i}"))
                    if group != "A":
                        link(dve.tensor_reduce(stats(0, i), b, AX.X, ALU.max))
                        dve.tensor_scalar(stats(1, i), stats(0, i), -SCALE[group], None, ALU.mult).then_inc(s_neg, 1)
                    else:
                        s, jp = divmod(c, 2)
                        h0 = 4 * s + 2 * jp
                        p = prob_of(i)[:, 0:n * width].rearrange("p (s k) -> p s k", s=n)
                        if before_in_slot(i) is not None:
                            dve.wait_ge(*filled(f"turn{before_in_slot(i)}"))
                        dve.wait_ge(s_bias[a % 2], 16 * (a // 2 + 1))
                        dve.tensor_tensor(p, b, bias[:, a % 2, h0:h0 + 2, 2 * P - width:2 * P], ALU.add).then_inc(s_dve, 1)
                        dve.wait_ge(*done(f"scores{i}"))
                        link(dve.tensor_reduce(stats(0, i), p, AX.X, ALU.max))
                        link(dve.tensor_tensor(stats(0, i), stats(0, i), sink[:, h0:h0 + 2], ALU.max))
                        link(dve.tensor_scalar(stats(1, i), stats(0, i), -1.0, None, ALU.mult))
                        dve.tensor_tensor(stats(3, i), sink[:, h0:h0 + 2], stats(1, i), ALU.add).then_inc(s_neg, 1)

                elif kind == "norm":
                    n, width = segments(i)
                    if UNITS[i][0] == "A":
                        dve.wait_ge(s_expA, A_UNITS.index(i) + 1)
                        link(dve.tensor_tensor(stats(2, i), stats(2, i), stats(3, i), ALU.add))
                    else:
                        dve.wait_ge(*done(f"scores{i}"))
                    link(dve.reciprocal(stats(4, i), stats(2, i)))
                    for seg in range(n):
                        p = prob_of(i)[:, seg * width:(seg + 1) * width]
                        ins = dve.tensor_scalar(p, p, stats(4, i)[:, seg:seg + 1], None, ALU.mult)
                    ins.then_inc(s_norm, 1)

                elif kind == "pv":
                    group, a = GROUPS[i]
                    dve.wait_ge(*filled(f"pv{i}"))
                    if group == "A":
                        dve.wait_ge(*done("gate a_z.3"))
                        g = m.mix[:, 0:4, a * P:(a + 1) * P]
                        b = heads(bank(f"pv{i}"))
                    else:
                        z = "d_z" if group == "D" else "c_z"
                        dve.wait_ge(*done(f"gate {z}.{a}"))
                        g = m.mix[:, MIX_AT[f"{z}.{a}"], :]
                        b = bank(f"pv{i}")
                    dve.scalar_tensor_tensor(out=g, in0=b, scalar=0.5, in1=g, op0=ALU.mult, op1=ALU.mult).then_inc(s_dve, 1)

                elif kind == "conv":
                    dve.wait_ge(*done(f"conv{i}"))
                    p = m.pad[:, i % 2, :]
                    acc = qkvT[:, i, :]
                    link(dve.tensor_scalar(acc, p[:, 0:S], col(CONVW + i), None, ALU.mult))
                    for tap in range(1, CONV):
                        ins = dve.scalar_tensor_tensor(out=acc, in0=p[:, tap:tap + S], scalar=col(CONVW + 12 * tap + i),
                                                       in1=acc, op0=ALU.mult, op1=ALU.add)
                        if tap < CONV - 1:
                            link(ins)
                    ins.then_inc(s_taps, 1)
                    if i:
                        silu2(i - 1)
                    if i == 11:
                        silu2(11)

                elif kind == "log_decay":
                    dve.wait_ge(s_ab, 2)
                    dve.wait_ge(*done("ab"))
                    link(dve.tensor_scalar(tb, tb, 1.0, None, ALU.add))
                    link(dve.reciprocal(beta, tb))
                    link(dve.tensor_tensor(th4(xdt), abr[:, :, 0:4], dtb.unsqueeze(1).to_broadcast([P, T, NH]), ALU.add))
                    link(dve.tensor_scalar(mx, xdt, 0.0, None, ALU.max))
                    dve.scalar_tensor_tensor(out=nabs, in0=mx, scalar=-2.0, in1=xdt, op0=ALU.mult, op1=ALU.add).then_inc(s_nabs, 1)
                    dve.wait_ge(s_ln1p, 1)
                    link(dve.tensor_tensor(mx, mx, lnp, ALU.add))
                    dve.scalar_tensor_tensor(out=th4(g16), in0=th4(mx), scalar=-1.0,
                                             in1=ea[:, 0:4].unsqueeze(1).to_broadcast([P, T, NH]),
                                             op0=ALU.mult, op1=ALU.mult).then_inc(s_g, 1)

                elif kind == "cum":
                    dve.wait_ge(*filled("cum"))
                    dve.tensor_copy(gc, bank("cum")[:, 0:32]).then_inc(s_dve, 1)
                    dve.wait_ge(*done("cum"))
                    dve.tensor_tensor(gdiff, gc[:, 16:32], gc[:, 0:16], ALU.subtract).then_inc(s_diff, 1)
                    link(dve.tensor_scalar(vbs, beta, 0.5, None, ALU.mult))
                    dve.wait_ge(s_exps, 1)
                    link(dve.scalar_tensor_tensor(out=nbeg, in0=beta, scalar=-1.0, in1=eg, op0=ALU.mult, op1=ALU.mult))

                elif kind == "l2":
                    l2_scale(i)

                elif kind == "decay":
                    dve.wait_ge(*filled(f"gr{i}"))
                    for h in range(NH):
                        hc = slice(h * P, (h + 1) * P)
                        ins = dve.scalar_tensor_tensor(out=dec[:, i, hc], in0=bank(f"gr{i}")[:, hc],
                                                       scalar=gc[:, 4 * i + h:4 * i + h + 1], in1=m.const("decay_neg"),
                                                       op0=ALU.subtract, op1=ALU.add)
                    ins.then_inc(s_dve, 1)

                elif kind == "chunk_rows":
                    dve.wait_ge(*filled(f"krows{i}"))
                    k = heads(bank(f"krows{i}"))
                    c = slice(4 * i, 4 * i + 4)
                    dve.tensor_tensor(kbg[:, i, :, :], k, over_free(nbeg[:, c]), ALU.mult)
                    dve.tensor_tensor(kd[:, i, :, :], k, over_free(ed[:, c]), ALU.mult).then_inc(s_dve, 1)
                    dve.wait_ge(*filled(f"vrows{i}"))
                    dve.tensor_tensor(vb[:, i, :, :], heads(bank(f"vrows{i}")), over_free(vbs[:, c]), ALU.mult).then_inc(s_dve, 1)

                elif kind == "chunk_products":
                    dve.wait_ge(s_dec, i + 1)
                    dve.wait_ge(*filled(f"kk{i}"))
                    dve.tensor_tensor(LT[:, i, :], bank(f"kk{i}"), dec[:, i, :], ALU.mult).then_inc(s_dve, 1)
                    dve.wait_ge(*done(f"kk{i}"))
                    dve.wait_ge(*filled(f"br{i}"))
                    dve.tensor_tensor(LT[:, i, :], bank(f"br{i}"), LT[:, i, :], ALU.mult).then_inc(s_dve, 1)
                    dve.wait_ge(*filled(f"qk{i}"))
                    dve.tensor_tensor(Aqk[:, i, :], bank(f"qk{i}"), dec[:, i, :], ALU.mult).then_inc(s_dve, 1)

                elif kind == "solve_b":
                    lv, t = i
                    if lv == 0:
                        eye = m.const("ident").unsqueeze(1).to_broadcast([P, NH, P])
                        dve.wait_ge(s_bt, t + 1)
                        dve.wait_ge(*done(f"p{i}"))
                        dve.tensor_tensor(heads(Ym[:, t, :]), eye, heads(BT[:, t, :]), ALU.subtract)
                        dve.tensor_tensor(heads(Xm[:, t, :]), eye, heads(dec[:, t, :]), ALU.subtract).then_inc(s_sol0, 1)
                    else:
                        for name, dst in ((f"xx{i}", Xm), (f"yy{i}", Ym)):
                            if name in TASK_AT:
                                dve.wait_ge(*filled(name))
                                dve.tensor_tensor(dst[:, t, :], dst[:, t, :], bank(name), ALU.subtract).then_inc(s_dve, 1)

                elif kind == "qg":
                    t = heads(th(f"qg{i}"))
                    dve.tensor_copy(gle[:, i, :, :], t[:, :, CH - 1::CH])
                    q = qkvT[:, 0:4, i * P:(i + 1) * P]
                    dve.wait_ge(*done(f"qk{i}"))
                    dve.tensor_tensor(q, q, t, ALU.mult).then_inc(s_thused, 1)

                elif kind == "state_o":
                    if i < S // CH - 1:
                        new, old = state[:, (i + 1) % 2, :], state[:, i % 2, :]
                        if i:
                            if i >= 1:
                                dve.wait_ge(*filled(f"o{i - 1}"))
                            dve.wait_ge(*done(f"ds{i - 1}"))
                            link(dve.tensor_tensor(heads(new), heads(old),
                                                   gle[:, i // 2, :, i % 2:i % 2 + 1].to_broadcast([P, NH, P]), ALU.mult))
                            dve.wait_ge(*filled(f"ds{i}"))
                            dve.tensor_tensor(new, new, bank(f"ds{i}"), ALU.add).then_inc(s_dve, 1)
                        else:
                            dve.wait_ge(*filled("ds0"))
                            dve.tensor_copy(new, bank("ds0")).then_inc(s_dve, 1)

                elif kind == "delta_out":
                    delta_gate(i)

                elif kind == "c_norm":
                    t = th(f"c_norm{i}")
                    if i == 0:
                        dve.scalar_tensor_tensor(out=cqT[:, 0, :], in0=craw[:, 0, :], scalar=col(CQN), in1=t,
                                                 op0=ALU.mult, op1=ALU.mult).then_inc(s_cq0, 1)
                        dve.scalar_tensor_tensor(out=cqT[:, 1, :], in0=craw[:, 1, :], scalar=col(CQN + 1), in1=t,
                                                 op0=ALU.mult, op1=ALU.mult).then_inc(s_thused, 1)
                    else:
                        dve.scalar_tensor_tensor(out=ckvT, in0=craw[:, 2, :], scalar=col(CKVN), in1=t,
                                                 op0=ALU.mult, op1=ALU.mult).then_inc(s_thused, 1)

                elif kind == "rope":
                    dst = krT if i == "k" else qrT[:, i, :]
                    dve.wait_ge(*filled(f"rope{i}"))
                    dve.tensor_tensor(dst, bank(f"rope{i}"), m.cosT[:, :], ALU.mult).then_inc(s_dve, 1)
                    dve.wait_ge(*filled(f"ropes{i}"))
                    dve.tensor_tensor(prob_ca[0], bank(f"ropes{i}"), m.sinT[:, :], ALU.mult).then_inc(s_dve, 1)
                    dve.wait_ge(*done(f"ropes{i}"))
                    dve.tensor_tensor(dst, dst, prob_ca[0], ALU.add).then_inc(s_rope, 1)
                    dve.wait_ge(s_rope, ["k", 0, 1].index(i) + 1)

                elif kind == "mix_split":
                    dve.wait_ge(s_xhi, i + 1)
                    slot = 2 * (i % MIX_SLOTS)
                    dve.tensor_tensor(m.h_hi[:, slot + 1, :], m.mix[:, OUT_K[i], :], m.h_hi[:, slot, :], ALU.subtract).then_inc(s_xlo, 1)

                elif kind == "residual":
                    if i == 0:
                        dve.wait_ge(s_gpost, 16)
                    if i < T:
                        dve.wait_ge(s_ysum, 2 * i + 2)
                        dve.tensor_tensor(lg2[:, i:i + 1], ss2[:, 2 * i:2 * i + 1], ss2[:, 2 * i + 1:2 * i + 2], ALU.add).then_inc(s_yadd, 1)
                    t = i - 1
                    if 0 <= t < T:
                        dve.wait_ge(s_y, t + 1)
                        if t:
                            dve.wait_ge(s_xfin, 2 * t)
                        for n in range(2):
                            c = slice(n * FB, (n + 1) * FB)
                            dve.scalar_tensor_tensor(out=ytmp[:, n, :], in0=bank(f"y{t}.{n}"), scalar=rs2[:, t:t + 1], in1=gpost[:, c],
                                                     op0=ALU.mult, op1=ALU.mult).then_inc(s_dve, 1)
                        for n in range(2):
                            c = slice(n * FB, (n + 1) * FB)
                            dve.wait_ge(*done(f"y{t}.{n}"))
                            dve.tensor_tensor(m.x[:, t, c], m.x[:, t, c], ytmp[:, n, :], ALU.add).then_inc(s_xfin, 1)


LAYER_SEMS = ["bank_filled", "freed_by_act", "freed_by_dve", "chunk_in0", "chunk_in1", "chunk_in2", "chunk_in3", "w_rounded", "w_split",
              "part_done", "params_in", "memory_in", "uq_in", "bias_in0", "bias_in1", "gpost_in", "scalars_in", "xs_ready",
              "mem_hi_ready", "mem_gained", "h_hi_ready", "h_lo_ready", "mix_hi_ready", "mix_lo_ready",
              "act_chain", "dve_chain", "neg_max_ready", "exp_ready", "prob_ready", "taps_done", "th_ready", "th_used",
              "squares_ready", "ab_ready", "nabs_ready", "ln1p_ready", "log_decay_ready", "decay_ready", "diff_ready", "exps_ready",
              "level_ready", "solve0_ready", "mix_delta_ready", "cq0_ready", "rope_ready", "x_ready", "y_sums_ready",
              "y_sum_ready", "y_rstd_ready"]


def program(nc, ins, out):
    with ExitStack() as ctx:
        m = Memory(nc, ctx)
        bias_dram = nc.dram_tensor("swa_bias", (T, P, SWA_H, 2 * P), F32, kind="Internal").ap()
        sems = [m._sem(n) for n in LAYER_SEMS]
        w = {n: ins[n] for n in ("norm_pre", "norm_post", "w_in", "attn_sinks", "gdn_conv_w", "gdn_a_log", "gdn_dt_bias",
                                 "gdn_norm", "mla_q_norm", "mla_kv_norm", "mla_w_uq", "mla_w_ukv", "mem_norm", "mem_w_kv", "w_out")}
        grouped = sems[0:3] + [sems[3:7]] + sems[7:13] + [sems[13:15]] + sems[15:]
        mem_dram = nc.dram_tensor("mem_normed", (P, KD, MEM), F32, kind="Internal").ap()
        prologue(nc, m, w, ctx, (ins["x"], ins["mem"], ins["positions"], ins["rel_bias"], ins["consts"]), bias_dram, mem_dram)
        with nc.Fori(0, DEPTH) as l:
            layer(nc, m, l, w, bias_dram, mem_dram, grouped)
            with nc.Block() as block:
                @block.gpsimd
                def _(pool):
                    pool.sem_clear(range(sems[0].num, sems[-1].num + 1))
        s_out = m._sem("out_written")
        with nc.Block() as block:
            @block.sync
            def _(sp):
                sp.dma_start(out[0].rearrange("(t p) d -> p t d", p=P), m.x[:, :, :]).then_inc(s_out, 16)
                sp.wait_ge(s_out, 16)


_INS = ["x", "mem", "positions", "rel_bias", "norm_pre", "norm_post", "w_in", "attn_sinks", "gdn_conv_w", "gdn_a_log",
        "gdn_dt_bias", "gdn_norm", "mla_q_norm", "mla_kv_norm", "mla_w_uq", "mla_w_ukv", "mem_norm", "mem_w_kv", "w_out"]


def kernel(**inputs):
    import numpy as _np
    import concourse.bacc as _bacc
    from concourse import mybir as _mybir
    from concourse.bass_utils import run_bass_kernel_spmd as _run

    nc = _bacc.Bacc("TRN2", target_bir_lowering=False, num_devices=1)
    arrays, args = {}, {}
    for name in _INS:
        a = _np.ascontiguousarray(inputs[name])
        arrays[f"in_{name}"] = a
        args[name] = nc.dram_tensor(f"in_{name}", a.shape, _mybir.dt.from_np(a.dtype), kind="ExternalInput").ap()
    arrays["in_consts"] = CONSTS
    args["consts"] = nc.dram_tensor("in_consts", CONSTS.shape, _mybir.dt.float32, kind="ExternalInput").ap()
    out = nc.dram_tensor("out", (1, S, D), _mybir.dt.float32, kind="ExternalOutput").ap()
    program(nc, args, out)
    r = _run(nc, [arrays], core_ids=[0])
    return r.results[0]["out"]
```
